# Optimizing a Trainium2 kernel written in Bass

```python
import functools
import jax
import jax.numpy as jnp
from jax import lax
import numpy as np
import math

D_MODEL = 1024
BATCH = 1
SEQ = 256
DEPTH = 4

GRID_W = 64
CTX_LEN = 256
N_MIXERS = 3
EPS = 1e-6
NEG_INF = -1e30
ROPE_BASE = 10000.0
ADA_STD = 0.02

A_HEADS = 16
A_KV_HEADS = 4
A_HEAD_DIM = 64
A_WINDOW = 128
A_BLOCK = 128
A_WIDTH = A_HEADS * A_HEAD_DIM
A_KV_WIDTH = A_KV_HEADS * A_HEAD_DIM
A_IN = 2 * A_WIDTH + 2 * A_KV_WIDTH

B_HEADS = 8
B_NOPE = 128
B_ROPE = 64
B_VDIM = 128
B_Q_RANK = 256
B_KV_RANK = 128
B_BLOCK = 128
B_WIDTH = B_HEADS * B_VDIM
B_IN = B_Q_RANK + B_KV_RANK + B_ROPE + B_WIDTH

C_HEADS = 4
C_QK_DIM = 128
C_V_DIM = 256
C_QK_WIDTH = C_HEADS * C_QK_DIM
C_WIDTH = C_HEADS * C_V_DIM
C_CONV = 5
C_CHUNK = 128
C_IN = 2 * C_QK_WIDTH + 3 * C_WIDTH + 4 * C_HEADS
F_BIAS = 3.0


def rmsnorm(x, g):
    xf = x.astype(jnp.float32)
    y = xf * lax.rsqrt(jnp.mean(xf * xf, axis=-1, keepdims=True) + EPS)
    return (y * g.astype(jnp.float32)).astype(x.dtype)

def axial_rope(n_tok, rot_dim, dtype):
    rows = n_tok // GRID_W
    r, cidx = jnp.meshgrid(jnp.arange(rows), jnp.arange(GRID_W), indexing='ij')
    r = r.reshape(-1).astype(jnp.float32)
    cc = cidx.reshape(-1).astype(jnp.float32)
    n_freq = rot_dim // 4
    inv = ROPE_BASE ** (-jnp.arange(n_freq, dtype=jnp.float32) / n_freq)
    ang = jnp.concatenate([r[:, None] * inv, cc[:, None] * inv], axis=-1)
    return jnp.cos(ang).astype(dtype), jnp.sin(ang).astype(dtype)

def apply_rope(x, cos, sin):
    x1, x2 = x[..., 0::2], x[..., 1::2]
    cos, sin = cos[:, None, :], sin[:, None, :]
    return jnp.stack([x1 * cos - x2 * sin, x1 * sin + x2 * cos], axis=-1).reshape(x.shape)

def sink_softmax(logits, sink):
    m = jnp.maximum(jnp.max(logits, axis=-1, keepdims=True), sink)
    e = jnp.exp(logits - m)
    return e / (jnp.sum(e, axis=-1, keepdims=True) + jnp.exp(sink - m))

def centred_dwconv(x, w):
    k = w.shape[0]
    return lax.conv_general_dilated(x, w[:, None, :].astype(x.dtype), window_strides=(1,),
                                    padding=[(k // 2, k // 2)],
                                    dimension_numbers=('NWC', 'WIO', 'NWC'),
                                    feature_group_count=x.shape[-1])

def window_gqa_mixer(h_lat, h_ctx, need_ctx, w_in, sink, w_out):
    bsz, n_lat, _ = h_lat.shape
    n_ctx = h_ctx.shape[1]
    grp = A_HEADS // A_KV_HEADS
    scale = A_HEAD_DIM ** -0.5
    cuts = [A_WIDTH, A_WIDTH + A_KV_WIDTH, A_WIDTH + 2 * A_KV_WIDTH]
    sink_l = sink.astype(jnp.float32).reshape(A_KV_HEADS, grp, 1, 1)

    q_l, k_l, v_l, z_l = jnp.split(h_lat @ w_in, cuts, axis=-1)
    if need_ctx:
        q_c, k_c, v_c, z_c = jnp.split(h_ctx @ w_in, cuts, axis=-1)
    else:
        k_c, v_c = jnp.split(h_ctx @ w_in[:, A_WIDTH:A_WIDTH + 2 * A_KV_WIDTH], 2, axis=-1)
    k_c = k_c.reshape(bsz, n_ctx, A_KV_HEADS, A_HEAD_DIM)
    v_c = v_c.reshape(bsz, n_ctx, A_KV_HEADS, A_HEAD_DIM)

    cos, sin = axial_rope(n_lat, A_HEAD_DIM, h_lat.dtype)
    q_l = apply_rope(q_l.reshape(bsz, n_lat, A_HEADS, A_HEAD_DIM), cos, sin)
    q_l = q_l.reshape(bsz, n_lat, A_KV_HEADS, grp, A_HEAD_DIM)
    k_l = apply_rope(k_l.reshape(bsz, n_lat, A_KV_HEADS, A_HEAD_DIM), cos, sin)
    v_l = v_l.reshape(bsz, n_lat, A_KV_HEADS, A_HEAD_DIM)

    pad = ((0, 0), (A_BLOCK, A_BLOCK), (0, 0), (0, 0))
    k_pad, v_pad = jnp.pad(k_l, pad), jnp.pad(v_l, pad)
    band = 3 * A_BLOCK
    k_off = jnp.arange(band) - A_BLOCK
    in_window = jnp.abs(k_off[None, :] - jnp.arange(A_BLOCK)[:, None]) <= A_WINDOW
    ctx_ok = jnp.ones((A_BLOCK, n_ctx), dtype=bool)

    def block(n):
        start = n * A_BLOCK
        q_b = lax.dynamic_slice_in_dim(q_l, start, A_BLOCK, axis=1)
        k_b = jnp.concatenate([lax.dynamic_slice_in_dim(k_pad, start, band, axis=1), k_c], axis=1)
        v_b = jnp.concatenate([lax.dynamic_slice_in_dim(v_pad, start, band, axis=1), v_c], axis=1)
        kpos = start + k_off
        valid = in_window & ((kpos >= 0) & (kpos < n_lat))[None, :]
        mask = jnp.concatenate([valid, ctx_ok], axis=1)
        logits = jnp.einsum('bqkgd,bjkd->bkgqj', q_b, k_b).astype(jnp.float32) * scale
        p = sink_softmax(jnp.where(mask, logits, NEG_INF), sink_l)
        return jnp.einsum('bkgqj,bjkd->bqkgd', p.astype(v_b.dtype), v_b)

    o = lax.map(block, jnp.arange(n_lat // A_BLOCK))
    o_l = jnp.moveaxis(o, 0, 1).reshape(bsz, n_lat, A_WIDTH)
    y_l = (o_l * jax.nn.silu(z_l)) @ w_out

    y_c = None
    if need_ctx:
        q_c = q_c.reshape(bsz, n_ctx, A_KV_HEADS, grp, A_HEAD_DIM)
        logits = jnp.einsum('bqkgd,bjkd->bkgqj', q_c, k_c).astype(jnp.float32) * scale
        p = sink_softmax(logits, sink_l)
        o_c = jnp.einsum('bkgqj,bjkd->bqkgd', p.astype(v_c.dtype), v_c).reshape(bsz, n_ctx, A_WIDTH)
        y_c = (o_c * jax.nn.silu(z_c)) @ w_out
    return y_l, y_c

def mla_mixer(h_lat, h_ctx, need_ctx, w_in, g_qa, g_kva, w_uq, w_ukv, w_out):
    bsz, n_lat, _ = h_lat.shape
    n_ctx = h_ctx.shape[1]
    dqk = B_NOPE + B_ROPE
    scale = dqk ** -0.5
    cuts = [B_Q_RANK, B_Q_RANK + B_KV_RANK, B_Q_RANK + B_KV_RANK + B_ROPE]

    def queries(q_a):
        b, n, _ = q_a.shape
        return (rmsnorm(q_a, g_qa) @ w_uq).reshape(b, n, B_HEADS, dqk)

    def keys_values(kv_a, k_pe):
        b, n, _ = kv_a.shape
        kv = (rmsnorm(kv_a, g_kva) @ w_ukv).reshape(b, n, B_HEADS, B_NOPE + B_VDIM)
        k_nope, v = jnp.split(kv, [B_NOPE], axis=-1)
        k_pe = jnp.broadcast_to(k_pe[:, :, None, :], (b, n, B_HEADS, B_ROPE))
        return jnp.concatenate([k_nope, k_pe], axis=-1), v

    q_a_l, kv_a_l, kpe_l, z_l = jnp.split(h_lat @ w_in, cuts, axis=-1)
    if need_ctx:
        q_a_c, kv_a_c, kpe_c, z_c = jnp.split(h_ctx @ w_in, cuts, axis=-1)
    else:
        kv_a_c, kpe_c = jnp.split(h_ctx @ w_in[:, B_Q_RANK:cuts[2]], [B_KV_RANK], axis=-1)

    cos, sin = axial_rope(n_lat, B_ROPE, h_lat.dtype)
    q_l = queries(q_a_l)
    q_l = jnp.concatenate([q_l[..., :B_NOPE], apply_rope(q_l[..., B_NOPE:], cos, sin)], axis=-1)
    kpe_l = apply_rope(kpe_l[:, :, None, :], cos, sin)[:, :, 0]
    k_l, v_l = keys_values(kv_a_l, kpe_l)
    k_c, v_c = keys_values(kv_a_c, kpe_c)

    k_all = jnp.concatenate([k_c, k_l], axis=1)
    v_all = jnp.concatenate([v_c, v_l], axis=1)

    def block(q_b):
        logits = jnp.einsum('bqhd,bkhd->bhqk', q_b, k_all).astype(jnp.float32) * scale
        p = jax.nn.softmax(logits, axis=-1)
        return jnp.einsum('bhqk,bkhd->bqhd', p.astype(v_all.dtype), v_all)

    nb = n_lat // B_BLOCK
    q_blocks = jnp.moveaxis(q_l.reshape(bsz, nb, B_BLOCK, B_HEADS, dqk), 1, 0)
    o = lax.map(block, q_blocks)
    o_l = jnp.moveaxis(o, 0, 1).reshape(bsz, n_lat, B_WIDTH)
    y_l = (o_l * jax.nn.silu(z_l)) @ w_out

    y_c = None
    if need_ctx:
        q_c = queries(q_a_c)
        logits = jnp.einsum('bqhd,bkhd->bhqk', q_c, k_c).astype(jnp.float32) * scale
        p = jax.nn.softmax(logits, axis=-1)
        o_c = jnp.einsum('bhqk,bkhd->bqhd', p.astype(v_c.dtype), v_c).reshape(bsz, n_ctx, B_WIDTH)
        y_c = (o_c * jax.nn.silu(z_c)) @ w_out
    return y_l, y_c

def mlstm_chunkwise(q, k, v, i_pre, f_pre, state, need_out):
    b, h, t, dk = q.shape
    dv = v.shape[-1]
    nc = t // C_CHUNK
    q = q.reshape(b, h, nc, C_CHUNK, dk)
    k = k.reshape(b, h, nc, C_CHUNK, dk)
    v = v.reshape(b, h, nc, C_CHUNK, dv)
    ig = i_pre.reshape(b, h, nc, C_CHUNK)
    cum = jnp.cumsum(jax.nn.log_sigmoid(f_pre).reshape(b, h, nc, C_CHUNK), axis=-1)
    tot = cum[..., -1]

    w_end = tot[..., None] - cum + ig
    m_loc = jnp.max(w_end, axis=-1)
    e_end = jnp.exp(w_end - m_loc[..., None])
    c_loc = jnp.einsum('bhcs,bhcsv,bhcsk->bhcvk', e_end, v, k)
    n_loc = jnp.einsum('bhcs,bhcsk->bhck', e_end, k)

    def step(carry, inp):
        c_prev, n_prev, m_prev = carry
        tot_c, m_l, c_l, n_l = inp
        m_new = jnp.maximum(tot_c + m_prev, m_l)
        a = jnp.exp(tot_c + m_prev - m_new)
        bb = jnp.exp(m_l - m_new)
        new = (a[..., None, None] * c_prev + bb[..., None, None] * c_l,
               a[..., None] * n_prev + bb[..., None] * n_l, m_new)
        return new, carry

    to_front = lambda a: jnp.moveaxis(a, 2, 0)
    final, starts = lax.scan(step, state, (to_front(tot), to_front(m_loc), to_front(c_loc), to_front(n_loc)))
    if not need_out:
        return None, final
    c_st, n_st, m_st = (jnp.moveaxis(s, 0, 2) for s in starts)

    tri = jnp.tril(jnp.ones((C_CHUNK, C_CHUNK), dtype=bool))
    log_d = jnp.where(tri, cum[..., :, None] - cum[..., None, :] + ig[..., None, :], NEG_INF)
    inter = cum + m_st[..., None]
    m_t = jnp.maximum(inter, jnp.max(log_d, axis=-1))
    s_qk = jnp.einsum('bhctd,bhcsd->bhcts', q, k) * jnp.exp(log_d - m_t[..., None])
    a_t = jnp.exp(inter - m_t)
    num = (jnp.einsum('bhcts,bhcsv->bhctv', s_qk, v)
           + a_t[..., None] * jnp.einsum('bhcvk,bhctk->bhctv', c_st, q))
    den = jnp.sum(s_qk, axis=-1) + a_t * jnp.einsum('bhck,bhctk->bhct', n_st, q)
    out = num / jnp.maximum(jnp.abs(den), jnp.exp(-m_t))[..., None]
    return out.reshape(b, h, t, dv), final

def mlstm_mixer(h_lat, h_ctx, need_ctx, w_in, conv, b_gate, g_head, w_out):
    bsz = h_lat.shape[0]
    cuts = [2 * C_QK_WIDTH, 2 * C_QK_WIDTH + C_WIDTH, 2 * C_QK_WIDTH + 2 * C_WIDTH, 2 * C_QK_WIDTH + 3 * C_WIDTH]

    def prepare(h):
        b, n, _ = h.shape
        qk, v, o, z, gates = jnp.split(h @ w_in, cuts, axis=-1)
        qk = jax.nn.silu(centred_dwconv(qk, conv))
        q, k = jnp.split(qk, 2, axis=-1)
        heads = lambda a, d: jnp.moveaxis(a.reshape(b, n, C_HEADS, d), 2, 1).astype(jnp.float32)
        q = heads(q, C_QK_DIM)
        k = heads(k, C_QK_DIM) * (C_QK_DIM ** -0.5)
        v = heads(v, C_V_DIM)
        gates = jnp.moveaxis((gates + b_gate).astype(jnp.float32).reshape(b, n, 4, C_HEADS), 1, -1)
        return q, k, v, o, z, gates

    def finish(hsum, o, z):
        b, n, _ = o.shape
        hh = jnp.moveaxis(hsum, 1, 2).astype(o.dtype)
        hh = hh * jax.nn.sigmoid(o).reshape(b, n, C_HEADS, C_V_DIM)
        hh = rmsnorm(hh, g_head.reshape(C_HEADS, C_V_DIM)).reshape(b, n, C_WIDTH)
        return (hh * jax.nn.silu(z)) @ w_out

    q_c, k_c, v_c, o_c, z_c, g_c = prepare(h_ctx)
    q_l, k_l, v_l, o_l, z_l, g_l = prepare(h_lat)
    zero_state = (jnp.zeros((bsz, C_HEADS, C_V_DIM, C_QK_DIM), jnp.float32),
                  jnp.zeros((bsz, C_HEADS, C_QK_DIM), jnp.float32),
                  jnp.full((bsz, C_HEADS), NEG_INF, jnp.float32))
    flip = lambda a: jnp.flip(a, axis=2)

    hc_f, st_f = mlstm_chunkwise(q_c, k_c, v_c, g_c[:, 0], g_c[:, 1], zero_state, need_ctx)
    hl_f, _ = mlstm_chunkwise(q_l, k_l, v_l, g_l[:, 0], g_l[:, 1], st_f, True)
    hc_b, st_b = mlstm_chunkwise(flip(q_c), flip(k_c), flip(v_c), flip(g_c[:, 2]), flip(g_c[:, 3]), zero_state, need_ctx)
    hl_b, _ = mlstm_chunkwise(flip(q_l), flip(k_l), flip(v_l), flip(g_l[:, 2]), flip(g_l[:, 3]), st_b, True)

    y_l = finish(hl_f + flip(hl_b), o_l, z_l)
    y_c = finish(hc_f + flip(hc_b), o_c, z_c) if need_ctx else None
    return y_l, y_c

def _normal(key, shape, std):
    return std * jax.random.normal(key, shape, jnp.float32)

def _gain(key, n):
    return 1.0 + 0.1 * jax.random.normal(key, (n,), jnp.float32)

def _layer_params(key, kind):
    ks = jax.random.split(key, 10)
    p = {
        'w_ada': _normal(ks[0], (D_MODEL, 3 * D_MODEL), ADA_STD),
        'b_ada': _normal(ks[1], (3 * D_MODEL,), 0.02),
        'g_pre': _gain(ks[2], D_MODEL),
        'g_post': _gain(ks[3], D_MODEL),
    }
    if kind == 0:
        p['w_in'] = _normal(ks[4], (D_MODEL, A_IN), D_MODEL ** -0.5)
        p['sink'] = _normal(ks[5], (A_HEADS,), 0.5)
        p['w_out'] = _normal(ks[6], (A_WIDTH, D_MODEL), A_WIDTH ** -0.5)
    elif kind == 1:
        p['w_in'] = _normal(ks[4], (D_MODEL, B_IN), D_MODEL ** -0.5)
        p['g_qa'] = _gain(ks[5], B_Q_RANK)
        p['g_kva'] = _gain(ks[6], B_KV_RANK)
        p['w_uq'] = _normal(ks[7], (B_Q_RANK, B_HEADS * (B_NOPE + B_ROPE)), B_Q_RANK ** -0.5)
        p['w_ukv'] = _normal(ks[8], (B_KV_RANK, B_HEADS * (B_NOPE + B_VDIM)), B_KV_RANK ** -0.5)
        p['w_out'] = _normal(ks[9], (B_WIDTH, D_MODEL), B_WIDTH ** -0.5)
    else:
        offset = jnp.repeat(jnp.array([0.0, F_BIAS, 0.0, F_BIAS], jnp.float32), C_HEADS)
        p['w_in'] = _normal(ks[4], (D_MODEL, C_IN), D_MODEL ** -0.5)
        p['conv'] = _normal(ks[5], (C_CONV, 2 * C_QK_WIDTH), C_CONV ** -0.5)
        p['b_gate'] = offset + _normal(ks[6], (4 * C_HEADS,), 0.3)
        p['g_head'] = _gain(ks[7], C_WIDTH)
        p['w_out'] = _normal(ks[8], (C_WIDTH, D_MODEL), C_WIDTH ** -0.5)
    return p

def first_inputs(seed: int = 0) -> dict:
    key = jax.random.key(seed)
    k_x, k_c, k_ctx, k_cc, k_layers = jax.random.split(key, 5)
    inputs = {
        'x': jax.random.normal(k_x, (BATCH, SEQ, D_MODEL), jnp.float32),
        'c': jax.random.normal(k_c, (BATCH, D_MODEL), jnp.float32),
        'ctx': jax.random.normal(k_ctx, (BATCH, CTX_LEN, D_MODEL), jnp.float32),
        'c_ctx': jax.random.normal(k_cc, (D_MODEL,), jnp.float32),
    }
    for i, lk in enumerate(jax.random.split(k_layers, DEPTH)):
        for name, val in _layer_params(lk, i % N_MIXERS).items():
            inputs[f'l{i}_{name}'] = val
    return inputs

def modulation(cvec, w_ada, b_ada):
    return jnp.split(jax.nn.silu(cvec) @ w_ada + b_ada, 3, axis=-1)

def first_block(x, c, ctx, c_ctx,
              l0_w_ada, l0_b_ada, l0_g_pre, l0_g_post, l0_w_in, l0_sink, l0_w_out,
              l1_w_ada, l1_b_ada, l1_g_pre, l1_g_post, l1_w_in, l1_g_qa, l1_g_kva, l1_w_uq, l1_w_ukv, l1_w_out,
              l2_w_ada, l2_b_ada, l2_g_pre, l2_g_post, l2_w_in, l2_conv, l2_b_gate, l2_g_head, l2_w_out,
              l3_w_ada, l3_b_ada, l3_g_pre, l3_g_post, l3_w_in, l3_sink, l3_w_out):
    layers = [
        (l0_w_ada, l0_b_ada, l0_g_pre, l0_g_post,
         functools.partial(window_gqa_mixer, w_in=l0_w_in, sink=l0_sink, w_out=l0_w_out)),
        (l1_w_ada, l1_b_ada, l1_g_pre, l1_g_post,
         functools.partial(mla_mixer, w_in=l1_w_in, g_qa=l1_g_qa, g_kva=l1_g_kva,
                           w_uq=l1_w_uq, w_ukv=l1_w_ukv, w_out=l1_w_out)),
        (l2_w_ada, l2_b_ada, l2_g_pre, l2_g_post,
         functools.partial(mlstm_mixer, w_in=l2_w_in, conv=l2_conv, b_gate=l2_b_gate,
                           g_head=l2_g_head, w_out=l2_w_out)),
        (l3_w_ada, l3_b_ada, l3_g_pre, l3_g_post,
         functools.partial(window_gqa_mixer, w_in=l3_w_in, sink=l3_sink, w_out=l3_w_out)),
    ]
    x_lat, x_ctx = x, ctx
    for i in range(DEPTH):
        w_ada, b_ada, g_pre, g_post, mixer = layers[i]
        need_ctx = i < DEPTH - 1
        sh_l, sc_l, gt_l = modulation(c, w_ada, b_ada)
        sh_c, sc_c, gt_c = modulation(c_ctx, w_ada, b_ada)
        h_l = rmsnorm(x_lat, g_pre) * (1.0 + sc_l[:, None, :]) + sh_l[:, None, :]
        h_c = rmsnorm(x_ctx, g_pre) * (1.0 + sc_c) + sh_c
        y_l, y_c = mixer(h_l, h_c, need_ctx=need_ctx)
        x_lat = x_lat + gt_l[:, None, :] * rmsnorm(y_l, g_post)
        if need_ctx:
            x_ctx = x_ctx + gt_c * rmsnorm(y_c, g_post)
    return x_lat


DEPTH_2 = 1

HEAD_DIM = 64
NSA_HEADS = 8
NSA_KV_GROUPS = 2
SWA_HEADS = 8
SWA_KV_GROUPS = 2
FOX_HEADS = 8
MIX_WIDTH = 8 * HEAD_DIM
N_BRANCH = 3
Q_BLOCK = 128
CMP_LEN = 32
CMP_STRIDE = 16
CMP_HIDDEN = 256
SLC_LEN = 64
SLC_TOPK = 8
NSA_WINDOW = 256
SWA_WINDOW = 128
N_BUCKETS = 32
MAX_DISTANCE = 128
D_FF = 256 * ((8 * D_MODEL // 3 + 255) // 256)
CONV_WIDTH = 3
RMS_EPS = 1e-6
NEG_INF_2 = -1e30
FORCE_SCORE = 1e9
N_QK_GAINS = 6

KV_A = NSA_KV_GROUPS * HEAD_DIM
KV_B = SWA_KV_GROUPS * HEAD_DIM
IN_SPLITS = (
    ('a_q', NSA_HEADS * HEAD_DIM), ('a_kc', KV_A), ('a_vc', KV_A), ('a_ks', KV_A), ('a_vs', KV_A),
    ('a_kw', KV_A), ('a_vw', KV_A), ('a_gate', NSA_HEADS * 3),
    ('b_q', SWA_HEADS * HEAD_DIM), ('b_k', KV_B), ('b_v', KV_B),
    ('c_q', FOX_HEADS * HEAD_DIM), ('c_k', FOX_HEADS * HEAD_DIM), ('c_v', FOX_HEADS * HEAD_DIM),
    ('c_f', FOX_HEADS),
    ('merge', N_BRANCH * D_MODEL),
)
IN_WIDTH = sum(w for _, w in IN_SPLITS)


def rms_norm(x, g):
    xf = x.astype(jnp.float32)
    return (xf * lax.rsqrt(jnp.mean(xf * xf, axis=-1, keepdims=True) + RMS_EPS)).astype(x.dtype) * g

def split_columns(h):
    cols, off = {}, 0
    for name, w in IN_SPLITS:
        cols[name] = h[..., off:off + w]
        off += w
    return cols

def to_heads(z, n_heads):
    b, t, _ = z.shape
    return z.reshape(b, t, n_heads, HEAD_DIM).transpose(0, 2, 1, 3)

def from_heads(z):
    b, h, t, d = z.shape
    return z.transpose(0, 2, 1, 3).reshape(b, t, h * d)

def t5_bucket(dist):
    max_exact = N_BUCKETS // 2
    d = jnp.maximum(dist, 0)
    log_ratio = jnp.log(jnp.maximum(d, 1).astype(jnp.float32) / max_exact) / math.log(MAX_DISTANCE / max_exact)
    large = jnp.minimum(max_exact + (log_ratio * (N_BUCKETS - max_exact)).astype(jnp.int32), N_BUCKETS - 1)
    return jnp.where(d < max_exact, d, large)

def banded_kv(z, n_prev):
    b, g, t, d = z.shape
    nb = t // Q_BLOCK
    zb = jnp.pad(z.reshape(b, g, nb, Q_BLOCK, d), ((0, 0), (0, 0), (n_prev, 0), (0, 0), (0, 0)))
    return jnp.concatenate([zb[:, :, j:j + nb] for j in range(n_prev + 1)], axis=3)

def banded_attention(q, k, v, window, tab, sinks):
    b, g, r, t, d = q.shape
    nb = t // Q_BLOCK
    n_prev = -(-(window - 1) // Q_BLOCK)
    n_keys = (n_prev + 1) * Q_BLOCK
    kb, vb = banded_kv(k, n_prev), banded_kv(v, n_prev)
    qb = q.reshape(b, g, r, nb, Q_BLOCK, d)
    qi = jnp.arange(Q_BLOCK)[:, None]
    ki = jnp.arange(n_keys)[None, :]
    dist = n_prev * Q_BLOCK + qi - ki
    s_pos = (jnp.arange(nb)[:, None, None] - n_prev) * Q_BLOCK + ki[None]
    valid = (dist >= 0) & (dist < window) & (s_pos >= 0)
    bias = jnp.transpose(tab[t5_bucket(dist)], (2, 3, 0, 1))[:, :, None]
    logits = jnp.einsum('bgrnqd,bgnkd->bgrnqk', qb, kb).astype(jnp.float32) * (HEAD_DIM ** -0.5) + bias
    logits = jnp.where(valid, logits, NEG_INF_2)
    if sinks is None:
        probs = jax.nn.softmax(logits, axis=-1)
    else:
        sink_col = jnp.broadcast_to(sinks.astype(jnp.float32).reshape(g, r, 1, 1, 1), logits.shape[:-1] + (1,))
        probs = jax.nn.softmax(jnp.concatenate([logits, sink_col], axis=-1), axis=-1)[..., :-1]
    out = jnp.einsum('bgrnqk,bgnkd->bgrnqd', probs.astype(v.dtype), vb)
    return out.reshape(b, g, r, t, d)

def nsa_mixer(cols, q_g, k_g, cmp_pos, cmp_w1, cmp_w2, tab_flat):
    b, t, _ = cols['a_q'].shape
    G, R = NSA_KV_GROUPS, NSA_HEADS // NSA_KV_GROUPS
    scale = HEAD_DIM ** -0.5
    tab = tab_flat.reshape(N_BUCKETS, G, R)
    q = rms_norm(to_heads(cols['a_q'], NSA_HEADS), q_g).reshape(b, G, R, t, HEAD_DIM)
    kc, vc = to_heads(cols['a_kc'], G), to_heads(cols['a_vc'], G)
    ks, vs = rms_norm(to_heads(cols['a_ks'], G), k_g), to_heads(cols['a_vs'], G)
    kw, vw = rms_norm(to_heads(cols['a_kw'], G), k_g), to_heads(cols['a_vw'], G)
    pos_t = jnp.arange(t)

    n_cmp = (t - CMP_LEN) // CMP_STRIDE + 1
    win_idx = jnp.arange(n_cmp)[:, None] * CMP_STRIDE + jnp.arange(CMP_LEN)[None, :]

    def compress(z, which):
        blk = z[:, :, win_idx] + cmp_pos[which]
        hid = jax.nn.gelu(blk.reshape(b, G, n_cmp, CMP_LEN * HEAD_DIM) @ cmp_w1[which])
        return hid @ cmp_w2[which]

    k_cmp = rms_norm(compress(kc, 0), k_g)
    v_cmp = compress(vc, 1)
    blk_end = jnp.arange(n_cmp) * CMP_STRIDE + CMP_LEN - 1
    dist_c = pos_t[:, None] - blk_end[None, :]
    valid_c = dist_c >= 0
    bias_c = jnp.transpose(tab[t5_bucket(dist_c)], (2, 3, 0, 1))
    logits_c = jnp.einsum('bgrtd,bgnd->bgrtn', q, k_cmp).astype(jnp.float32) * scale + bias_c
    logits_c = jnp.where(valid_c, logits_c, NEG_INF_2)
    p_cmp = jax.nn.softmax(logits_c, axis=-1) * jnp.any(valid_c, axis=-1)[:, None]
    o_cmp = jnp.einsum('bgrtn,bgnd->bgrtd', p_cmp.astype(v_cmp.dtype), v_cmp)

    n_slc = t // SLC_LEN
    n_top = min(SLC_TOPK, n_slc)
    c_start = jnp.arange(n_cmp) * CMP_STRIDE
    s_start = jnp.arange(n_slc) * SLC_LEN
    overlap = ((c_start[:, None] < s_start[None, :] + SLC_LEN)
               & (c_start[:, None] + CMP_LEN > s_start[None, :])).astype(jnp.float32)
    importance = jnp.einsum('bgtn,nj->bgtj', p_cmp.sum(axis=2), overlap)
    cur = pos_t // SLC_LEN
    jblk = jnp.arange(n_slc)[None, :]
    valid_s = jblk <= cur[:, None]
    forced = (jblk == 0) | (jblk == cur[:, None]) | (jblk == cur[:, None] - 1)
    score = jnp.where(valid_s, jnp.where(forced, FORCE_SCORE, importance), NEG_INF_2)
    top_score, top_idx = lax.top_k(score, n_top)
    top_ok = top_score > NEG_INF_2 / 2

    nb = t // Q_BLOCK
    ks_blk = ks.reshape(b, G, n_slc, SLC_LEN, HEAD_DIM)
    vs_blk = vs.reshape(b, G, n_slc, SLC_LEN, HEAD_DIM)
    q_b = jnp.moveaxis(q.reshape(b, G, R, nb, Q_BLOCK, HEAD_DIM), 3, 0)
    idx_b = jnp.moveaxis(top_idx.reshape(b, G, nb, Q_BLOCK, n_top), 2, 0)
    ok_b = jnp.moveaxis(top_ok.reshape(b, G, nb, Q_BLOCK, n_top), 2, 0)
    gather = jax.vmap(jax.vmap(lambda blocks, ix: blocks[ix]))
    bias_lookup = jax.vmap(lambda tb, bk: tb[bk], in_axes=(1, 1), out_axes=1)
    n_sel = n_top * SLC_LEN

    def selected_block(args):
        i, qi, ix, ok = args
        kg = gather(ks_blk, ix).reshape(b, G, Q_BLOCK, n_sel, HEAD_DIM)
        vg = gather(vs_blk, ix).reshape(b, G, Q_BLOCK, n_sel, HEAD_DIM)
        t_pos = i * Q_BLOCK + jnp.arange(Q_BLOCK)
        s_pos = (ix[..., None] * SLC_LEN + jnp.arange(SLC_LEN)).reshape(b, G, Q_BLOCK, n_sel)
        dist = t_pos[:, None] - s_pos
        valid = (dist >= 0) & jnp.repeat(ok, SLC_LEN, axis=-1)
        bias = jnp.moveaxis(bias_lookup(tab, t5_bucket(dist)), -1, 2)
        logits = jnp.einsum('bgrqd,bgqkd->bgrqk', qi, kg).astype(jnp.float32) * scale + bias
        logits = jnp.where(valid[:, :, None], logits, NEG_INF_2)
        probs = jax.nn.softmax(logits, axis=-1)
        return jnp.einsum('bgrqk,bgqkd->bgrqd', probs.astype(vg.dtype), vg)

    o_slc = lax.map(selected_block, (jnp.arange(nb), q_b, idx_b, ok_b))
    o_slc = jnp.moveaxis(o_slc, 0, 3).reshape(b, G, R, t, HEAD_DIM)

    o_win = banded_attention(q, kw, vw, NSA_WINDOW, tab, None)

    gate = jax.nn.sigmoid(cols['a_gate']).reshape(b, t, NSA_HEADS, 3).transpose(0, 2, 1, 3)
    gate = gate.reshape(b, G, R, t, 3)
    o = gate[..., 0:1] * o_cmp + gate[..., 1:2] * o_slc + gate[..., 2:3] * o_win
    return from_heads(o.reshape(b, NSA_HEADS, t, HEAD_DIM))

def swa_mixer(cols, q_g, k_g, sinks, tab_flat):
    b, t, _ = cols['b_q'].shape
    G, R = SWA_KV_GROUPS, SWA_HEADS // SWA_KV_GROUPS
    q = rms_norm(to_heads(cols['b_q'], SWA_HEADS), q_g).reshape(b, G, R, t, HEAD_DIM)
    k = rms_norm(to_heads(cols['b_k'], G), k_g)
    v = to_heads(cols['b_v'], G)
    o = banded_attention(q, k, v, SWA_WINDOW, tab_flat.reshape(N_BUCKETS, G, R), sinks.reshape(G, R))
    return from_heads(o.reshape(b, SWA_HEADS, t, HEAD_DIM))

def fox_mixer(cols, q_g, k_g, forget_bias):
    b, t, _ = cols['c_q'].shape
    q = rms_norm(to_heads(cols['c_q'], FOX_HEADS), q_g)
    k = rms_norm(to_heads(cols['c_k'], FOX_HEADS), k_g)
    v = to_heads(cols['c_v'], FOX_HEADS)
    log_f = jax.nn.log_sigmoid((cols['c_f'] + forget_bias).astype(jnp.float32))
    c = jnp.cumsum(log_f, axis=1).transpose(0, 2, 1)
    nb = t // Q_BLOCK
    q_b = jnp.moveaxis(q.reshape(b, FOX_HEADS, nb, Q_BLOCK, HEAD_DIM), 2, 0)
    c_b = jnp.moveaxis(c.reshape(b, FOX_HEADS, nb, Q_BLOCK), 2, 0)
    key_pos = jnp.arange(t)

    def query_block(args):
        i, qi, ci = args
        t_pos = i * Q_BLOCK + jnp.arange(Q_BLOCK)
        logits = (jnp.einsum('bhqd,bhsd->bhqs', qi, k).astype(jnp.float32) * (HEAD_DIM ** -0.5)
                  + ci[..., None] - c[:, :, None, :])
        logits = jnp.where(t_pos[:, None] >= key_pos[None, :], logits, NEG_INF_2)
        probs = jax.nn.softmax(logits, axis=-1)
        return jnp.einsum('bhqs,bhsd->bhqd', probs.astype(v.dtype), v)

    o = lax.map(query_block, (jnp.arange(nb), q_b, c_b))
    o = jnp.moveaxis(o, 0, 2).reshape(b, FOX_HEADS, t, HEAD_DIM)
    return from_heads(o)

def conv_ffn(h, w_gate, w_up, conv_w, conv_b, w_down):
    a = h @ w_gate
    a = lax.conv_general_dilated(a, conv_w[:, None, :], window_strides=(1,),
                                 padding=[(CONV_WIDTH - 1, 0)],
                                 dimension_numbers=('NWC', 'WIO', 'NWC'),
                                 feature_group_count=a.shape[-1]) + conv_b
    return (jax.nn.gelu(a) * (h @ w_up)) @ w_down

def second_inputs(seed: int = 0) -> dict:
    key = jax.random.key(seed)
    ks = jax.random.split(key, 19)
    L, D, F, d = DEPTH_2, D_MODEL, D_FF, HEAD_DIM
    nrm = jax.random.normal
    return {
        'x': nrm(ks[0], (BATCH, SEQ, D), jnp.float32),
        'rel_bias': 0.5 * nrm(ks[1], (N_BUCKETS, NSA_HEADS + SWA_HEADS), jnp.float32),
        'norm_mix': 1.0 + 0.05 * nrm(ks[2], (L, D), jnp.float32),
        'norm_ffn': 1.0 + 0.05 * nrm(ks[3], (L, D), jnp.float32),
        'w_in': nrm(ks[4], (L, D, IN_WIDTH), jnp.float32) * D ** -0.5,
        'forget_bias': 4.0 + 0.5 * nrm(ks[5], (L, FOX_HEADS), jnp.float32),
        'qk_gain': 1.0 + 0.05 * nrm(ks[6], (L, N_QK_GAINS, d), jnp.float32),
        'cmp_pos': 0.1 * nrm(ks[7], (L, 2, CMP_LEN, d), jnp.float32),
        'cmp_w1': nrm(ks[8], (L, 2, CMP_LEN * d, CMP_HIDDEN), jnp.float32) * (CMP_LEN * d) ** -0.5,
        'cmp_w2': nrm(ks[9], (L, 2, CMP_HIDDEN, d), jnp.float32) * CMP_HIDDEN ** -0.5,
        'sinks': nrm(ks[10], (L, SWA_HEADS), jnp.float32),
        'w_branch': nrm(ks[11], (L, N_BRANCH, MIX_WIDTH, D), jnp.float32) * MIX_WIDTH ** -0.5,
        'w_out': nrm(ks[12], (L, D, D), jnp.float32) * D ** -0.5,
        'w_gate': nrm(ks[13], (L, D, F), jnp.float32) * D ** -0.5,
        'w_up': nrm(ks[14], (L, D, F), jnp.float32) * D ** -0.5,
        'conv_w': nrm(ks[15], (L, CONV_WIDTH, F), jnp.float32) * CONV_WIDTH ** -0.5,
        'conv_b': 0.02 * nrm(ks[16], (L, F), jnp.float32),
        'w_down': nrm(ks[17], (L, F, D), jnp.float32) * F ** -0.5,
    }

def second_block(x, rel_bias, norm_mix, norm_ffn, w_in, forget_bias, qk_gain, cmp_pos, cmp_w1, cmp_w2,
              sinks, w_branch, w_out, w_gate, w_up, conv_w, conv_b, w_down):
    b, t, _ = x.shape
    for l in range(DEPTH_2):
        h = rms_norm(x, norm_mix[l])
        cols = split_columns(h @ w_in[l])
        o_a = nsa_mixer(cols, qk_gain[l, 0], qk_gain[l, 1], cmp_pos[l], cmp_w1[l], cmp_w2[l],
                        rel_bias[:, :NSA_HEADS])
        o_b = swa_mixer(cols, qk_gain[l, 2], qk_gain[l, 3], sinks[l], rel_bias[:, NSA_HEADS:])
        o_c = fox_mixer(cols, qk_gain[l, 4], qk_gain[l, 5], forget_bias[l])
        branches = jnp.stack([o_a, o_b, o_c], axis=2)
        proj = jnp.einsum('btnm,nmd->btnd', branches, w_branch[l])
        gates = jax.nn.sigmoid(cols['merge']).reshape(b, t, N_BRANCH, D_MODEL)
        x = x + (gates * proj).sum(axis=2) @ w_out[l]
        x = x + conv_ffn(rms_norm(x, norm_ffn[l]), w_gate[l], w_up[l], conv_w[l], conv_b[l], w_down[l])
    return x


def setup_inputs(seed=0):
    out = dict(first_inputs(seed))
    for name, value in second_inputs(seed + 1).items():
        if name != "x":
            out[name + "_2"] = value
    return out


def reference(
    x, c, ctx, c_ctx, l0_w_ada, l0_b_ada, l0_g_pre, l0_g_post, l0_w_in, l0_sink, l0_w_out,
    l1_w_ada, l1_b_ada, l1_g_pre, l1_g_post, l1_w_in, l1_g_qa, l1_g_kva, l1_w_uq, l1_w_ukv,
    l1_w_out, l2_w_ada, l2_b_ada, l2_g_pre, l2_g_post, l2_w_in, l2_conv, l2_b_gate, l2_g_head,
    l2_w_out, l3_w_ada, l3_b_ada, l3_g_pre, l3_g_post, l3_w_in, l3_sink, l3_w_out, rel_bias_2,
    norm_mix_2, norm_ffn_2, w_in_2, forget_bias_2, qk_gain_2, cmp_pos_2, cmp_w1_2, cmp_w2_2,
    sinks_2, w_branch_2, w_out_2, w_gate_2, w_up_2, conv_w_2, conv_b_2, w_down_2,
):
    x = first_block(
        x, c, ctx, c_ctx, l0_w_ada, l0_b_ada, l0_g_pre, l0_g_post, l0_w_in, l0_sink, l0_w_out,
        l1_w_ada, l1_b_ada, l1_g_pre, l1_g_post, l1_w_in, l1_g_qa, l1_g_kva, l1_w_uq, l1_w_ukv,
        l1_w_out, l2_w_ada, l2_b_ada, l2_g_pre, l2_g_post, l2_w_in, l2_conv, l2_b_gate,
        l2_g_head, l2_w_out, l3_w_ada, l3_b_ada, l3_g_pre, l3_g_post, l3_w_in, l3_sink,
        l3_w_out,
    )
    return second_block(
        x, rel_bias_2, norm_mix_2, norm_ffn_2, w_in_2, forget_bias_2, qk_gain_2, cmp_pos_2,
        cmp_w1_2, cmp_w2_2, sinks_2, w_branch_2, w_out_2, w_gate_2, w_up_2, conv_w_2, conv_b_2,
        w_down_2,
    )


_drawn_inputs = setup_inputs


def setup_inputs(seed=0):
    import zlib

    import numpy as np

    out = dict(_drawn_inputs(seed))
    spreads = {}
    factors = {'l0_sink': 8.0,
     'l1_g_qa': 3.462,
     'l3_sink': 8.0,
     'norm_mix_2': 3.319,
     'qk_gain_2': 5.247,
     'cmp_pos_2': 4.487,
     'sinks_2': 22.164,
     'conv_b_2': 6.197,
     'norm_ffn_2': 4.503}
    for name, (base, spread) in spreads.items():
        noise = np.random.default_rng([zlib.crc32(name.encode()), seed]).standard_normal(out[name].shape)
        drawn = base * np.exp(spread * noise) if base else spread * noise
        out[name] = jnp.asarray(drawn.astype(out[name].dtype))
    for name, factor in factors.items():
        out[name] = (out[name] * factor).astype(out[name].dtype)
    return out
```

```python
from contextlib import ExitStack

import numpy as np

import concourse.bass as bass
from concourse import mybir

F32 = mybir.dt.float32
R32 = mybir.dt.float32r
BF16 = mybir.dt.bfloat16
ACT = mybir.ActivationFunctionType
ALU = mybir.AluOpType
AX = mybir.AxisListType

NEG = -1.0e30
FLOOR = -3.0e38
EPS = 1e-6
D = 1024


def flat(need):
    out = []
    for n in need:
        if n is None:
            continue
        if isinstance(n, list):
            out += flat(n)
        else:
            out.append(n)
    return out


def known(need):
    return all(known(n) if isinstance(n, list) else n is not None for n in need)


def width(ap):
    return int(np.prod([n for _, n in list(ap.ap)[1:]]))


class Queue:

    def __init__(self, core, name):
        self.core, self.name, self.items, self.count, self.seen, self.t = core, name, [], 0, {}, 0.0

    def wait(self, *need):
        top = {}
        for sem, val in flat(need):
            top[sem] = max(top.get(sem, 0), val)
        for sem, val in top.items():
            if self.seen.get(sem, 0) < val:
                self.items.append((None, sem, val))
                self.seen[sem] = val
                self.t = max(self.t, self.core.when.get((sem, val), 0.0))

    def do(self, fn, *need, inc=True, cost=100.0):
        self.wait(*need)
        self.t += cost
        if inc:
            self.count += 1
            self.items.append((fn, self.name, 1))
            mark = (self.name, self.count)
            self.core.when[mark] = self.t + self.core.LATENCY[self.name]
            return mark
        self.items.append((fn, None, 0))
        return None

    def play(self, e, sems):
        for fn, sem, val in self.items:
            if fn is None:
                e.wait_ge(sems[sem], val)
            elif sem is None:
                fn(e)
            else:
                fn(e).then_inc(sems[sem], val)


class Bank:

    def __init__(self, t):
        self.t, self.free = t, []


class Slots:

    def __init__(self, n):
        self.free = [(i, []) for i in range(n)]

    def take(self):
        yield lambda: bool(self.free)
        i, marks = self.free.pop(0)
        yield marks
        return i, marks

    def give(self, i, *marks):
        self.free.append((i, flat(marks)))


class Task:
    def __init__(self, gen, prio, seq):
        self.gen, self.prio, self.seq, self.want, self.at = gen, prio, seq, None, 0.0
        self.done = False


class Core:

    SLACK = -50.0
    LATENCY = {"pe": 197.0, "act": 190.0, "dve": 170.0, "pool": 155.0}

    def __init__(self):
        self.when = {}
        self.pe, self.act, self.dve, self.pool, self.sp = (Queue(self, n) for n in ("pe", "act", "dve", "pool", "sp"))
        self.dma_count = {}
        self.banks = []
        self.tasks = []
        self.seq = 0
        self.clock = 0.0
        self.hw_t = self.dma_t = 0.0

    def spawn(self, gen, prio):
        self.seq += 1
        t = Task(gen, prio, self.seq)
        self.tasks.append(t)
        self.tasks.sort(key=lambda x: (x.prio, x.seq))
        return t

    def time(self, *need):
        return max([self.when.get(m, 0.0) for m in flat(need)] or [0.0])

    def step(self, t):
        try:
            want = next(t.gen)
        except StopIteration:
            t.done = True
            self.tasks.remove(t)
            return
        t.want, t.at = None, 0.0
        if callable(want):
            t.want = want
        elif isinstance(want, float):
            t.at = want
        else:
            t.at = self.time(want)

    def go(self, main):
        while not main.done:
            now = max(self.clock, self.pe.t)
            best = None
            for t in self.tasks:
                if t.want is not None:
                    if not t.want():
                        continue
                    t.want = None
                    best = t
                    break
                if t.at <= now + self.SLACK:
                    best = t
                    break
            else:
                ready = [t for t in self.tasks if t.want is None]
                assert ready, "every part waits"
                best = min(ready, key=lambda t: t.at)
                self.clock = max(self.clock, best.at)
            self.step(best)

    def dma(self, q, slot, out, in_, *need):
        name = "dma_" + slot
        q.wait(*need)
        self.dma_count[name] = self.dma_count.get(name, 0) + 16
        q.items.append((lambda e, o=out, i=in_: e.dma_start(o, i), name, 16))
        mark = (name, self.dma_count[name])
        n = int(np.prod([c for _, c in list(out.ap)])) * 4
        if q is self.pool:
            q.t += 1030.0
            at = q.t + 650.0
        else:
            self.hw_t = max(self.hw_t, q.t) + 450.0
            q.t = self.hw_t
            at = self.hw_t + 650.0
        self.dma_t = max(self.dma_t, at) + n / 360.0
        self.when[mark] = self.dma_t + 1000.0
        return mark

    def bank(self):
        b = min(self.banks, key=lambda x: self.time(x.free))
        self.banks.remove(b)
        return b

    def get(self, k=1):
        yield lambda: len(self.banks) >= k
        b = self.bank()
        yield b.free
        return b

    def give(self, b, *marks):
        b.free = flat(marks)
        self.banks.append(b)

    def mm(self, out, lhsT, rhs, start, stop, *need, inc=False, cost=None):
        n = width(out)
        cost = cost or (n * 1.667 if rhs.dtype == F32 else max(n * 0.417, 107.0))
        return self.pe.do(lambda e: e.matmul(out, lhsT, rhs, start=start, stop=stop), *need, inc=inc, cost=cost)

    def tr(self, out, in_, ident, *need, inc=True):
        return self.pe.do(lambda e: e.transpose(out, in_, ident), *need, inc=inc, cost=107.0)

    def a(self, out, in_, func, *need, bias=0.0, scale=1.0, accum=None):
        cost = 93.0 + 0.834 * width(in_)
        if accum is None:
            return self.act.do(lambda e: e.activation(out, in_, func, bias=bias, scale=scale), *need, cost=cost)
        return self.act.do(lambda e: e.activation(out, in_, func, bias=bias, scale=scale, accum_out=accum), *need, cost=cost + 93.0)

    def v(self, fn, ap, *need, q=None):
        q = q or self.dve
        return q.do(fn, *need, cost=70.0 + width(ap) / 0.96 + (60.0 if width(ap) > 8 else 0.0) + (350.0 if q is self.pool else 0.0))

    def cp(self, out, in_, *need, q=None):
        return self.v(lambda e: e.tensor_copy(out, in_), in_, *need, q=q)

    def tt(self, out, a, b, op, *need, q=None):
        return self.v(lambda e: e.tensor_tensor(out, a, b, op), out, *need, q=q)

    def ts(self, out, a, s1, s2, op0, op1, *need, q=None):
        if op1 is None:
            return self.v(lambda e: e.tensor_scalar(out, a, s1, None, op0), out, *need, q=q)
        return self.v(lambda e: e.tensor_scalar(out, a, s1, s2, op0, op1), out, *need, q=q)

    def stt(self, out, a, s, b, op0, op1, *need):
        return self.v(lambda e: e.scalar_tensor_tensor(out, a, s, b, op0=op0, op1=op1), out, *need)

    def ttr(self, out, a, b, scale, init, op0, op1, accum, *need):
        return self.v(lambda e: e.tensor_tensor_reduce(out, a, b, scale, init, op0, op1, accum), out, *need)

    def tsa(self, out, a, s1, op0, op1, accum, *need):
        return self.v(lambda e: e.tensor_scalar(out, a, s1, None, op0, op1, accum_out=accum), out, *need)

    def red(self, out, a, op, *need):
        return self.v(lambda e: e.tensor_reduce(out, a, AX.X, op), a, *need)

    def rec(self, out, a, *need):
        return self.v(lambda e: e.reciprocal(out, a), out, *need)

    def mset(self, out, v, *need, q=None):
        return self.v(lambda e: e.memset(out, v), out, *need, q=q)


class Job:

    def __init__(self, key, parts, kt, w, split=True):
        self.key, self.parts, self.kt, self.w, self.split = key, parts, kt, w, split
        self.rdy = [None] * kt
        self.load = None
        self.raw_place = self.place = None

    def pack(self, ins):
        out = np.empty((128, self.kt, self.w), np.float32)
        for c0, name, lead, r0, s0, cols in self.parts:
            a = np.asarray(ins[name])[lead][r0:r0 + 128 * self.kt, s0:s0 + cols]
            out[:, :, c0:c0 + cols] = a.reshape(self.kt, 128, cols).transpose(1, 0, 2)
        return out.reshape(-1)


class Ring:

    def __init__(self, cols):
        self.cols, self.at, self.held = cols, 0, []

    def take(self, n):
        at = self.at if self.at + n <= self.cols else 0
        over = [h for h in self.held if h[0] < at + n and at < h[0] + h[1]]
        if any(h[2].get("free") is None for h in over):
            return None
        self.held = [h for h in self.held if h not in over]
        rec = {"free": None}
        self.held.append((at, n, rec))
        self.at = at + n
        return at, rec, [h[2]["free"] for h in over]


class Weights:

    AHEAD = 2000.0

    def __init__(self, p, plan, dram, raw, hi, lo, nsem=6):
        self.dram, self.off = dram, 0
        self.p, self.plan, self.raw, self.hi, self.lo, self.nsem = p, plan, raw, hi, lo, nsem
        self.raw_ring, self.ring = Ring(raw.shape[1]), Ring(hi.shape[1])
        self.at = self.loads = self.preps = 0

    def pump(self):
        p = self.p
        while self.loads < len(self.plan):
            j = self.plan[self.loads]
            old = self.plan[self.loads - self.nsem].raw_rec["free"] if self.loads >= self.nsem else []
            if old is None:
                break
            ring, raw = (self.raw_ring, self.raw) if j.raw_place is None else j.raw_place
            got = ring.take(j.kt * j.w)
            if got is None:
                break
            at, j.raw_rec, need = got
            j.raw = raw[:, at:at + j.kt * j.w].rearrange("p (k c) -> p k c", k=j.kt)
            sem = f"w{self.loads % self.nsem}"
            n = j.kt * j.w
            src = self.dram[self.off:self.off + 128 * n].rearrange("(p c) -> p c", p=128)
            self.off += 128 * n
            j.load = p.dma(p.sp, sem, raw[:, at:at + n], src, need, old)
            self.loads += 1

    def place(self):
        j = self.plan[self.preps]
        if j.load is None:
            return False
        if not j.split:
            return True
        if j.place is not None:
            got = j.place()
            if got is None:
                return False
            hi, lo, j.need = got
            at, j.rec = 0, {}
        else:
            got = self.ring.take(j.kt * j.w)
            if got is None:
                return False
            at, j.rec, j.need = got
            hi, lo = self.hi, self.lo
        j.hi = hi[:, at:at + j.kt * j.w].rearrange("p (k c) -> p k c", k=j.kt)
        j.lo = lo[:, at:at + j.kt * j.w].rearrange("p (k c) -> p k c", k=j.kt)
        return True

    def prepare(self):
        p = self.p
        late = None
        while self.preps < len(self.plan):
            yield self.place
            j = self.plan[self.preps]
            self.preps += 1
            if not j.split:
                continue
            step = max(1, 512 // j.w)
            for k0 in range(0, j.kt, step):
                k1 = min(k0 + step, j.kt)
                yield [j.load, j.need]
                yield max(p.act.t, p.dve.t) - self.AHEAD
                hi, lo, raw = j.hi[:, k0:k1, :], j.lo[:, k0:k1, :], j.raw[:, k0:k1, :]
                a = p.a(hi, raw, ACT.Copy, j.load, j.need)
                yield [a]
                b = p.tt(lo, raw, hi, ALU.subtract, a, j.need)
                for k in range(k0, k1):
                    j.rdy[k] = b
            j.raw_rec["free"] = b
            self.pump()

    def job(self, key):
        j = self.plan[self.at]
        assert j.key == key, (j.key, key)
        self.at += 1
        if j.split:
            yield lambda: j.rdy[0] is not None
        else:
            yield lambda: j.load is not None
            yield [j.load]
        return j

    def free(self, j, mark):
        if j.split:
            j.rec["free"] = mark
        else:
            j.raw_rec["free"] = mark
        self.pump()


SCR = 14336
CT, LAT = 0, 1


def job(key, name, c0, w, kt=8, r0=0, split=True, lead=()):
    return Job(key, [(0, name, lead, r0, c0, w)], kt, w, split)


def ada_keys(l):
    keys = [(l, 2, j) for j in range(4)]
    if l < 3:
        keys += [(l + 1, part, j) for part in range(2) for j in range(4)]
    return keys


def ada_at(l, place, places):
    keys = ada_keys(l)
    tail = 4 if len(keys) > 4 else 2
    if place == places - 1:
        return keys[-tail:]
    n = len(keys) - tail
    return keys[n * place // (places - 1):n * (place + 1) // (places - 1)]


def plan_ada(keys):
    return [job(("ada",) + k, f"l{k[0]}_w_ada", 1024 * k[1] + 256 * k[2], 256, split=False) for k in keys]


def plan_a(l):
    n = f"l{l}_w_in"
    jobs = [job(("k", l), n, 1024, 256), job(("v", l), n, 1280, 256)]
    for t in range(8):
        jobs += [job(("q", l, t), n, 128 * t, 128), job(("z", l, t), n, 1536 + 128 * t, 128)]
        jobs += plan_ada(ada_at(l, t, 9))
    return jobs + plan_ada(ada_at(l, 8, 9))


def plan_b(l):
    n, u = f"l{l}_w_in", f"l{l}_w_uq"
    jobs = [job(("qa",), n, 0, 256), job(("kva",), n, 256, 192)]
    z = lambda h: [job(("zb", h), n, 448 + 128 * h, 128)]
    for h in range(8):
        if h == 0:
            jobs += z(0) + z(1)
        if h % 2 == 0:
            c = 192 * h
            parts = [(0, u, (), 0, c + 128, 64), (64, u, (), 0, c + 320, 64), (128, u, (), 0, c, 128), (256, u, (), 0, c + 192, 128)]
            jobs += [Job(("uq", h // 2), parts, 2, 384), job(("ukv", h // 2), f"l{l}_w_ukv", 256 * h, 512, kt=1)]
        if h > 1:
            jobs += z(h)
        jobs += plan_ada(ada_at(l, h, 9))
    return jobs + plan_ada(ada_at(l, 8, 9))


def plan_c(l):
    n = f"l{l}_w_in"
    qkv = lambda j: [job(("qc", j), n, 128 * j, 128), job(("kc", j), n, 512 + 128 * j, 128), job(("vc", j), n, 1024 + 256 * j, 256)]
    oz = lambda j: [job(("oc", j), n, 2048 + 256 * j, 256), job(("zc", j), n, 3072 + 256 * j, 256)]
    ada = lambda x: plan_ada(ada_at(l, x, 8))
    jobs = qkv(0) + [job(("gates",), n, 4096, 16)] + ada(0)
    for j in range(1, 4):
        jobs += qkv(j) + ada(2 * j - 1) + oz(j - 1) + ada(2 * j)
    return jobs + oz(3) + ada(7)


def plan_2():
    j2 = lambda key, name, c0, w, **kw: job(key, name, c0, w, lead=0, **kw)
    n = "w_in_2"
    small = Job(("small",), [(0, n, 0, 0, 1280, 24), (24, n, 0, 0, 3608, 8)], 8, 32)
    jobs = [j2(("p", c), n, c, 256) for c in (768, 1024)] + [small, j2(("p", 512), n, 512, 256)]
    for wh in range(2):
        jobs += [Job(("w1", wh, h), [(0, "cmp_w1_2", (0, wh), 1024 * h, 0, 256)], 8, 256, False) for h in range(2)]
    jobs += [j2(("p", c), n, c, 256) for c in (0, 256, 1816, 1304, 1560, 2072, 2584, 3096, 2328, 2840, 3352)]
    mg = [(d, m) for d in range(4) for m in range(3)]
    merge = lambda d, m: j2(("merge", d, m), n, 3616 + 1024 * m + 256 * d, 256)
    jobs += [merge(*m) for m in mg[:4]]
    for d, m in mg:
        if (d, m) not in mg[:4]:
            jobs.append(merge(d, m))
        jobs.append(Job(("branch", d, m), [(0, "w_branch_2", (0, m), 0, 256 * d, 256)], 4, 256))
    jobs += [j2(("out2", j), "w_out_2", 256 * j, 256) for j in range(4)]
    for c in range(12):
        if c < 11:
            jobs += [j2(("gate", c), "w_gate_2", 256 * c, 256), j2(("up", c), "w_up_2", 256 * c, 256)]
        if c > 0:
            jobs.append(Job(("down", c - 1), [(0, "w_down_2", 0, 256 * (c - 1), 0, 1024)], 2, 1024))
    return jobs


def plan():
    jobs = plan_ada([(0, part, j) for part in range(2) for j in range(4)])
    for l, mix in enumerate((plan_a, plan_b, plan_c, plan_a)):
        jobs += mix(l) + [job(("out", l, j), f"l{l}_w_out", 256 * j, 256) for j in range(4)]
    return jobs + plan_2()


class Net(Core):

    def __init__(self, nc, ctx, ins, out, upto):
        super().__init__()
        self.nc, self.ins, self.out, self.upto = nc, ins, out, upto
        sb = lambda name, shape, dt=F32: ctx.enter_context(nc.sbuf_tensor("s_" + name, shape, dt))
        self.X = sb("X", [128, 4, D])
        self.Hh = sb("Hh", [128, 8, 512], R32)
        self.Hl = sb("Hl", [128, 8, 512], R32)
        self.Gh = sb("Gh", [128, 8, 512], R32)
        self.Gl = sb("Gl", [128, 8, 512], R32)
        raw = sb("raw", [128, 4096])
        hi = sb("whi", [128, 4096], R32)
        lo = sb("wlo", [128, 4096], R32)
        self.K = sb("K", [128, 896])
        self.ident = self.K[:, 0:128]
        self.selB = self.K[:, 128:384].rearrange("p (s m) -> p s m", s=2)
        self.ropeC, self.ropeS = self.K[:, 384:640], self.K[:, 640:896]
        self.band = sb("band", [128, 2, 512], BF16)
        self.CS = sb("CS", [128, 8, 32])
        self.VC = sb("VC", [128, 168])
        self.SHc = sb("SHc", [128, 2, 8, 2])
        self.Ac = sb("Ac", [128, 2, 8, 2])
        self.st = sb("st", [128, 256])
        self.sink = sb("sink", [128, 48])
        self.G = sb("G", [128, 2, D])
        self.adaS = sb("adaS", [128, 2, 256])
        self.gp = sb("gp", [128, 2, 256])
        self.mhalf = sb("mhalf", [128, 32])
        self.bg = sb("bg", [128, 2, 256])
        with nc.sbuf_tensor("SF", [128, SCR], F32) as SF:
            pass
        self.SF, self.SR = SF, sb("SR", [128, SCR], R32)
        for i in range(8):
            self.banks.append(Bank(ctx.enter_context(nc.psum_tensor(f"ps{i}", [128, 512], F32))))
        jobs = plan()
        early = (Ring(8192), self.SF[:, 0:8192])
        for k in (0, 1, 2, 3, 6, 7):
            jobs[k].raw_place = early
        for j in jobs:
            if j.key[0] == "out" and j.key[2] == 3:
                j.place = lambda j=j: (self.SR[:, 0:2048], self.SR[:, 2048:4096], self.out_at[j.key[1]]) if j.key[1] in self.out_at else None
        self.out_at = {}
        self.w = Weights(self, jobs, ins["weights"], raw, hi, lo)
        self.o0 = out.shape[0] - 2
        self.sti = 0
        self.fence = []
        self.hr = [[None] * 8, [None] * 8]
        self.xr = [None] * 4
        self.h_free = []
        self.g_free = []

    def now(self):
        return [(q.name, q.count) for q in (self.pe, self.act, self.dve, self.pool) if q.count]

    def F(self, at, *shape):
        n = int(np.prod(shape))
        ap = self.SF[:, at:at + n]
        return ap if len(shape) == 1 else self._shape(ap, shape)

    def Rr(self, at, *shape):
        n = int(np.prod(shape))
        ap = self.SR[:, at:at + n]
        return ap if len(shape) == 1 else self._shape(ap, shape)

    @staticmethod
    def _shape(ap, shape):
        if len(shape) == 2:
            return ap.rearrange("p (a b) -> p a b", a=shape[0])
        return ap.rearrange("p (a b c) -> p a b c", a=shape[0], b=shape[1])

    def cols(self, n):
        if self.sti + n > 256:
            self.sti = 0
        at = self.sti
        self.sti += n
        return self.st[:, at:at + n]

    def start(self):
        i = self.ins
        crow, rows, rows2 = self.F(8192, 128), self.F(8320, 128), self.F(8448, 128)
        th, th2 = self.F(8576, 16), self.F(8592, 16)
        band_f = self.F(8704, 2, 512)
        c_rd = self.dma(self.sp, "c", crow[0:16, :], i["cond"])
        self.k_rd = self.dma(self.act, "k", self.K[:, :], i["konst"])
        self.w.pump()
        vec = self.dma(self.pool, "vec", rows[0:104, :], i["vecs"][0:104])
        vec2 = self.dma(self.pool, "vecb", rows2[0:64, :], i["vecs"][104:168])
        self.vc = {"l1_g_qa": 32, "l1_g_kva": 34, "l2_g_head": 35, "l2_conv": 43}
        for l in range(4):
            self.vc[f"l{l}_g_pre"] = 8 * l
            self.vc[f"l{l}_b_ada"] = 104 + 16 * l
        for t in range(4):
            src = i["ctx"][0, 128 * t:128 * t + 128, :] if t < 2 else i["x"][0, 128 * t - 256:128 * t - 128, :]
            self.xr[t] = self.dma(self.pool, f"x{t}", self.X[:, t, :], src, self.w.plan[t].load)
        bd = self.dma(self.pool, "band", band_f, i["band"].rearrange("p (a b) -> p a b", a=2), self.w.plan[4].load)
        sk = self.dma(self.pool, "sink", self.sink[:, :], i["rows"].to_broadcast([128, 48]))
        z = self.mset(self.CS[:, :, :], 0.0)
        self.mhalf_rd = self.mset(self.mhalf[:, :], -0.5)
        b = self.bank()
        ct = self.tr(b.t[:, 0:16], crow[0:16, :], self.ident[0:16, 0:16], c_rd, self.k_rd)
        t = self.a(th, b.t[:, 0:16], ACT.Tanh, ct, scale=0.5)
        t = self.stt(th2, th, 1.0, b.t[:, 0:16], ALU.add, ALU.mult, t)
        self.give(b, t)
        self.cs_rd = self.ts(self.CS[:, :, 0:2], th2.rearrange("p (s k) -> p k s", s=2), 0.5, None, ALU.mult, None, t, z)
        self.ada_slots = Slots(2)
        self.ada_rd = {}
        self.ada_left = 0
        self.g_rd = None
        self.G_free = []

        def vectors():
            b = yield from self.get()
            yield [vec, vec2]
            self.tr(b.t[:, 0:104], rows[0:104, :], self.ident[0:104, 0:104], vec)
            vt = self.tr(b.t[:, 104:168], rows2[0:64, :], self.ident[0:64, 0:64], vec2)
            yield [vt]
            self.vc_rd = self.cp(self.VC[:, :], b.t[:, 0:168], vt)
            self.give(b, self.vc_rd)

        def masks():
            yield [bd]
            self.band_rd = self.cp(self.band[:, :, :], band_f, bd)
            yield [sk]
            self.sink_rd = self.ts(self.sink[:, 0:40], self.sink[:, 0:40], -1.0, None, ALU.mult, None, sk)
        self.vc_rd = self.band_rd = self.sink_rd = None
        return [self.spawn(vectors(), 0.0), self.spawn(masks(), 0.0)]

    def ada_step(self, l, part, j):
        job = yield from self.w.job(("ada", l, part, j))
        b = yield from self.get(4)
        for kt in range(8):
            c = kt % 4
            mk = self.mm(b.t[32 * c:32 * c + 32, 0:256], self.CS[:, kt, :], job.raw[:, kt, :], kt < 4, kt >= 4,
                         job.load, self.cs_rd, b.free, inc=kt == 7, cost=128.0)
        self.w.free(job, mk)
        self.ada_left += 1
        self.spawn(self.ada_tail(l, part, j, b, mk), 0.0)

    def ada_tail(self, l, part, j, b, mk):
        s, free = yield from self.ada_slots.take()
        if part == 2:
            row = lambda a: a.rearrange("(a c) -> a c", a=1).to_broadcast([128, 256])
            o = slice(256 * j, 256 * j + 256)
            gp_rd = [self.dma(self.sp, f"gp{s}", self.gp[:, s, :], row(self.ins[f"l{l}_g_post"][o]), free),
                     self.dma(self.sp, f"gp{s}", self.bg[:, s, :], row(self.ins[f"l{l}_b_ada"][2048 + 256 * j:2304 + 256 * j]), free)]
        yield [mk]
        ev = self.a(self.adaS[:, s, :], b.t[:, 0:256], ACT.Copy, mk, free)
        yield [ev]
        if part < 2:
            for h in range(2):
                mk = self.mm(b.t[:, 256 + 2 * h:258 + 2 * h], self.adaS[:, s, 128 * h:128 * h + 128], self.selB[:, :, 0],
                             True, True, ev, inc=True, cost=215.0)
            self.ada_slots.give(s, mk)
            yield lambda: self.vc_rd is not None
            yield [mk, self.vc_rd]
            col = lambda at: self.VC[:, at:at + 2].rearrange("p (k a) -> p k a", a=1).to_broadcast([128, 2, 2])
            bias = col(self.vc[f"l{l}_b_ada"] + 8 * part + 2 * j)
            pv = b.t[:, 256:260].rearrange("p (k s) -> p k s", s=2)
            dst = (self.SHc if part == 0 else self.Ac)[:, l % 2, 2 * j:2 * j + 2, :]
            d = self.tt(dst, pv, bias, ALU.add, mk, self.vc_rd)
            self.give(b, d)
            if part == 1:
                d = self.stt(dst, dst, 1.0, col(self.vc[f"l{l}_g_pre"] + 2 * j), ALU.add, ALU.mult, d)
            self.ada_rd.setdefault(l, []).append(d)
        else:
            self.give(b, ev)
            gb = yield from self.get(2)
            for q in range(2):
                mk = self.mm(gb.t[:, 256 * q:256 * q + 256], self.selB[:, q, :], self.adaS[:, s, :],
                             True, True, ev, gb.free, inc=True)
            yield [mk, gp_rd]
            bc = lambda a: a[:, s, :].rearrange("p (a b) -> p a b", a=1).to_broadcast([128, 2, 256])
            g = self.G[:, :, 256 * j:256 * j + 256]
            d = self.tt(g, gb.t[:, :].rearrange("p (a b) -> p a b", a=2), bc(self.bg), ALU.add, mk, gp_rd, self.G_free)
            self.give(gb, d)
            d = self.tt(g, g, bc(self.gp), ALU.mult, d)
            self.ada_slots.give(s, d)
            self.g_rd = d
        self.ada_left -= 1

    def ada_some(self, l, place, places):
        for k in ada_at(l, place, places):
            yield from self.ada_step(*k)

    def rstd(self, ss, n, cnt, *need):
        out = self.cols(n)
        t = self.ts(out, ss, 1.0 / cnt, EPS, ALU.mult, ALU.add, *need)
        t = self.tt(out, out, self.mhalf[:, 0:n], ALU.pow, t, self.mhalf_rd, q=self.pool)
        return out, t

    def h_cols(self, l, s):
        return (lambda kt: self.Ac[:, l % 2, kt, s:s + 1], lambda kt: self.SHc[:, l % 2, kt, s:s + 1],
                lambda: self.ada_rd[l], lambda: len(self.ada_rd.get(l, [])) == 8)

    def new_h(self):
        self.hr = [[None] * 8, [None] * 8]
        return self.hr

    def norm_tile(self, s, i, xn, nt, *need):
        x = self.X[:, 2 * s + i, :]
        ss = self.cols(1)
        yield [self.xr[2 * s + i], *need]
        t = self.a(xn[:, i, :], x, ACT.Square, self.xr[2 * s + i], *need, accum=ss)
        yield [t]
        rs, rt = self.rstd(ss, 1, D, t)
        yield [rt]
        nt[i] = self.ts(xn[:, i, :], x, rs, None, ALU.mult, None, rt, t)

    def make_h(self, hr, cols, s, xn, hf, nt, *need):
        A_, S_, ar, there = cols
        yield there
        yield lambda: known(nt)
        hs = Slots(2)

        def tail(kp, b, mk):
            x, free = yield from hs.take()
            yield [mk]
            tb = []
            for h in range(2):
                kt = 2 * kp + h
                p = b.t[:, 256 * h:256 * h + 256]
                o, need2 = hf[:, x, h, :], [mk, ar(), free, *need]
                if kp % 2 == 1 and S_ is None:
                    tb.append(self.a(o, p, ACT.Copy, need2, scale=A_(kt)))
                elif kp % 2 == 1:
                    tb.append(self.a(o, p, ACT.Identity, need2, scale=A_(kt), bias=S_(kt)))
                elif S_ is None:
                    tb.append(self.ts(o, p, A_(kt), None, ALU.mult, None, need2))
                else:
                    tb.append(self.ts(o, p, A_(kt), S_(kt), ALU.mult, ALU.add, need2))
            self.give(b, tb)
            yield tb
            o = slice(256 * s, 256 * s + 256)
            hh, hl = self.Hh[:, 2 * kp:2 * kp + 2, o], self.Hl[:, 2 * kp:2 * kp + 2, o]
            ta = self.a(hh, hf[:, x], ACT.Copy, tb, self.h_free)
            yield [ta]
            tc = self.tt(hl, hf[:, x], hh, ALU.subtract, ta, tb, self.h_free)
            hs.give(x, tc)
            hr[s][2 * kp] = hr[s][2 * kp + 1] = tc
        for kp in range(4):
            b = yield from self.get(2)
            for i in range(2):
                yield [nt[i]]
                for h in range(2):
                    kt = 2 * kp + h
                    mk = self.tr(b.t[:, 256 * h + 128 * i:256 * h + 128 * i + 128], xn[:, i, 128 * kt:128 * kt + 128],
                                 self.ident, nt[i], b.free)
            self.spawn(tail(kp, b, mk), 0.0)
        yield lambda: known(hr[s])

    def form_a(self, job, c0, m, out, n0, n, Hh, Hl, rdy, free, every=2):
        for k in range(job.kt):
            if k % every == 0:
                ks = range(k, min(k + every, job.kt))
                need = lambda: [[job.rdy[q], rdy(q)] for q in ks]
                yield lambda: known(need())
                yield need()
            wh, wl = job.hi[:, k, c0:c0 + m], job.lo[:, k, c0:c0 + m]
            hh, hl = Hh[:, k, n0:n0 + n], Hl[:, k, n0:n0 + n]
            last = k == job.kt - 1
            self.mm(out, wh, hh, k == 0, False, job.rdy[k], rdy(k), free)
            self.mm(out, wh, hl, False, False)
            mk = self.mm(out, wl, hh, False, last, inc=last)
        return mk

    def form_b(self, job, c0, w, out, t0, Hh, Hl, rdy, free, every=4):
        for k in range(job.kt):
            if k % every == 0:
                ks = range(k, min(k + every, job.kt))
                need = lambda: [[job.rdy[q], rdy(q)] for q in ks]
                yield lambda: known(need())
                yield need()
            wh, wl = job.hi[:, k, c0:c0 + w], job.lo[:, k, c0:c0 + w]
            hh, hl = Hh[:, k, t0:t0 + 128], Hl[:, k, t0:t0 + 128]
            last = k == job.kt - 1
            self.mm(out, hh, wh, k == 0, False, job.rdy[k], rdy(k), free)
            self.mm(out, hh, wl, False, False)
            mk = self.mm(out, hl, wh, False, last, inc=last)
        return mk

    def hrd(self, s0, s1):
        hr = self.hr
        return lambda k: [hr[s][k] for s in range(s0, s1)]

    def prod_b(self, job, w, s):
        b = yield from self.get(4)
        for i in range(2):
            mk = yield from self.form_b(job, 0, w, b.t[:, w * i:w * i + w], 256 * s + 128 * i, self.Hh, self.Hl,
                                        self.hrd(s, s + 1), b.free)
        return b, mk

    def rope(self, q, tmp, *need):
        n = q.shape[0]
        a = self.v(lambda e: e.stream_shuffle(tmp[0:n], q, mask=[j ^ 1 for j in range(32)]), q, *need)
        a = self.tt(tmp[0:n], tmp[0:n], self.ropeS[0:n, :], ALU.mult, a)
        b = self.tt(q, q, self.ropeC[0:n, :], ALU.mult, a)
        return self.tt(q, q, tmp[0:n], ALU.add, a, b)

    def turned(self):
        yield lambda: self.turn.done
        self.fence = self.now()
        return self.fence

    def layer_a(self, l, streams):
        f0 = self.fence
        KH, KL = self.Rr(0, 4, 512), self.Rr(2048, 4, 512)
        QS = self.Rr(4096, 2, 2, 512)
        V = self.F(6144, 4, 256)
        ZT = self.F(7168, 2, 512)
        qf = self.F(8192, 2, 512)
        tmp = self.F(9216, 256)
        gf = self.F(13312, 2, 256)
        c = dict(l=l, streams=streams, KH=KH, KL=KL, QS=QS, V=V, ZT=ZT, qf=qf, tmp=tmp, gf=gf, kr={}, vr={},
                 qf_s=Slots(2), gf_s=Slots(2), qs_s=Slots(2), zt_s=Slots(2), q={}, z={}, f0=f0)
        self.gr = [[None] * 8, [None] * 8]

        def k_tail(s, t, b, mk, f0):
            o = slice(256 * s, 256 * s + 256)
            x, free = yield from c["qf_s"].take()
            yield [mk]
            q = qf[:, x, 0:256]
            t1 = self.a(q, b.t[:, 0:256], ACT.Copy, mk, free, f0)
            self.give(b, t1)
            yield [t1]
            if s == LAT:
                t1 = self.rope(q, tmp, t1, f0)
                yield [t1]
            rd = []
            for h in range(2):
                g, r, y = 2 * t + h, slice(64 * h, 64 * h + 64), slice(64 - 64 * h, 128 - 64 * h)
                ah = self.a(KH[r, g, o], q[r], ACT.Copy, t1, f0, scale=0.125)
                ax = self.a(KH[y, g, o], q[r], ACT.Copy, t1, f0, scale=0.125)
                yield [ah]
                d1 = self.stt(KL[r, g, o], q[r], 0.125, KH[r, g, o], ALU.mult, ALU.subtract, ah, t1, f0)
                d2 = self.stt(KL[y, g, o], q[r], 0.125, KH[r, g, o], ALU.mult, ALU.subtract, ah, t1, f0)
                rd += [ax, d1, d2]
                c["kr"][s, g] = [ax, d1, d2]
            c["qf_s"].give(x, rd)

        def v_tail(s, b, mk, f0):
            yield [mk]
            c["vr"][s] = t = self.cp(V[:, 2 * s:2 * s + 2, :], b.t[:, :].rearrange("p (i c) -> p i c", i=2), mk, f0)
            self.give(b, t)
        jk = yield from self.w.job(("k", l))
        jv = None
        for s in (CT, LAT):
            if s == LAT:
                f0 = c["f0"] = yield from self.turned()
            for t in range(2):
                b, mk = yield from self.prod_k(jk, t, s)
                self.spawn(k_tail(s, t, b, mk, f0), 0.0)
            if s == LAT:
                self.w.free(jk, mk)
            if jv is None:
                jv = yield from self.w.job(("v", l))
            b, mk = yield from self.prod_b(jv, 256, s)
            self.spawn(v_tail(s, b, mk, f0), 0.0)
        self.w.free(jv, mk)
        att = self.spawn(self.attention(self.units_a(c), at=9472), 0.5)
        yield from self.proj_qz(c)
        yield lambda: att.done

    def prod_k(self, job, t, s):
        b = yield from self.get(4)
        mk = yield from self.form_a(job, 128 * t, 128, b.t[:, 0:256], 256 * s, 256, self.Hh, self.Hl, self.hrd(s, s + 1), b.free)
        return b, mk

    def proj_qz(self, c):
        l, streams = c["l"], c["streams"]
        s0 = streams[0]
        n0, n = 256 * s0, 256 * len(streams)
        qf, tmp, QS = c["qf"], c["tmp"], c["QS"]
        o = slice(n0, n0 + n)
        f0 = c["f0"]

        def q_tail(t, b, mk):
            x, free = yield from c["qf_s"].take()
            yield [mk]
            t1 = self.a(qf[:, x, o], b.t[:, o], ACT.Copy, mk, free, f0)
            self.give(b, t1)
            yield [t1]
            r0 = [self.rope(qf[:, x, 256:512], tmp, t1, f0), t1]
            y, free = yield from c["qs_s"].take()
            yield r0
            rd = []
            for h in range(2):
                r, z = slice(64 * h, 64 * h + 64), slice(64 - 64 * h, 128 - 64 * h)
                ah = self.a(QS[r, y, h, o], qf[r, x, o], ACT.Copy, r0, free)
                yield [ah]
                d = self.tt(QS[z, y, h, o], qf[r, x, o], QS[r, y, h, o], ALU.subtract, ah, r0, free)
                rd += [ah, d]
            c["q"][t] = (y, rd)
            c["qf_s"].give(x, rd)

        def z_tail(t, b, mk):
            x, free = yield from c["zt_s"].take()
            yield [mk]
            z = c["ZT"][:, x, o]
            ta = self.a(z, b.t[:, o], ACT.Tanh, mk, free, f0, scale=0.5)
            yield [ta]
            td = self.stt(z, z, 1.0, b.t[:, o], ALU.add, ALU.mult, ta)
            self.give(b, td)
            c["z"][t] = (x, td)
        for t in range(8):
            for key, tail in (("q", q_tail), ("z", z_tail)):
                job = yield from self.w.job((key, l, t))
                b = yield from self.get(4)
                mk = yield from self.form_a(job, 0, 128, b.t[:, o], n0, n, self.Hh, self.Hl, self.hrd(s0, 2), b.free)
                self.w.free(job, mk)
                self.spawn(tail(t, b, mk), 0.0)
            if t == 7:
                self.h_free = [mk]
            yield from self.ada_some(l, t, 9)
        yield from self.ada_some(l, 8, 9)

    def units_a(self, c):
        KH, KL, QS, V = c["KH"], c["KL"], c["QS"], c["V"]
        sk = 0 if c["l"] == 0 else 16
        left, zleft = {}, {}
        for t in range(8):
            left[t], zleft[t] = 4 * len(c["streams"]), len(c["streams"])
            for s in c["streams"]:
                box = {}
                for i in range(2):
                    for e in range(2):
                        g, h = t // 2, 2 * t + e
                        nk = 256 if s == CT else 512
                        nt = nk // 128

                        def ready(t=t, g=g, s=s):
                            return t in c["q"] and all((s2, g) in c["kr"] for s2 in range(s + 1))

                        def need(t=t, g=g, s=s):
                            return [c["q"][t][1], [c["kr"][s2, g] for s2 in range(s + 1)]]

                        def scores(b, s=s, g=g, e=e, i=i, nk=nk, t=t, need=need):
                            o = 256 * s + 128 * i
                            x = c["q"][t][0]
                            self.mm(b.t[:, 0:nk], QS[:, x, e, o:o + 128], KH[:, g, 0:nk], True, False, need(), b.free)
                            mk = self.mm(b.t[:, 0:nk], QS[:, x, e, o:o + 128], KL[:, g, 0:nk], False, True, inc=True)
                            left[t] -= 1
                            if left[t] == 0:
                                c["qs_s"].give(x, mk)
                            return mk

                        def values(ob, pts, marks, s=s, g=g, i=i, nt=nt):
                            for k in range(nt):
                                for e2 in range(2):
                                    mk = self.mm(ob.t[64 * e2:64 * e2 + 64, 128 * i:128 * i + 128],
                                                 V[:, k, 64 * g:64 * g + 64], pts[e2][:, k, :], k == 0, k == nt - 1,
                                                 marks[e2], c["vr"][s], c["vr"][CT], ob.free, inc=k == nt - 1)
                            return mk

                        def gate(ob, mk, s=s, t=t):
                            o = slice(256 * s, 256 * s + 256)
                            yield lambda: t in c["z"]
                            x, zr = c["z"][t]
                            y, free = yield from c["gf_s"].take()
                            yield [mk, zr]
                            gf = c["gf"][:, y, :]
                            d = self.stt(gf, ob.t[:, 0:256], 0.5, c["ZT"][:, x, o], ALU.mult, ALU.mult, mk, zr, free, c["f0"])
                            self.give(ob, d)
                            zleft[t] -= 1
                            if zleft[t] == 0:
                                c["zt_s"].give(x, d)
                            yield [d]
                            ah = self.a(self.Gh[:, t, o], gf, ACT.Copy, d, self.g_free)
                            yield [ah]
                            d2 = self.tt(self.Gl[:, t, o], gf, self.Gh[:, t, o], ALU.subtract, ah, self.g_free)
                            c["gf_s"].give(y, d2)
                            self.gr[s][t] = d2

                        yield dict(ready=ready, need=need, scores=scores, values=values, nk=nk, pair=e, box=box, first=i == 0,
                                   vready=lambda s=s: known([c["vr"].get(s), c["vr"].get(CT)]),
                                   gate=gate if i == 1 else None, mask=self.band[:, i, 0:nk], sink=self.sink[:, sk + h:sk + h + 1],
                                   mask_rd=lambda: [self.sink_rd, self.band_rd])

    def attention(self, units, at=9472, nsm=4, npt=3, wide=514, kts=4):
        A = dict(SM=self.F(at, nsm, wide), PT=self.F(at + wide * nsm, npt, kts, 128), f0=self.fence, sm=Slots(nsm), pt=Slots(npt),
                 turned=0, values=0)
        group, tasks, n = [], [], 0
        for k, u in enumerate(units):
            yield u["ready"]
            u["at"], free = yield from A["sm"].take()
            tasks.append(self.spawn(self.unit(u, A, k, free), 0.0))
            group.append(u)
            if u["pair"] != 0:
                tasks.append(self.spawn(self.values(group, A, n), 0.0))
                group, n = [], n + 1
        yield lambda: all(t.done for t in tasks)

    def unit(self, u, A, k, free):
        nk, f0 = u["nk"], A["f0"]
        st = self.cols(2)
        sm = A["SM"][:, u["at"], 0:nk + (u["sink"] is not None)]
        rows = sm[:, 0:nk]
        b = yield from self.get(1)
        yield u["need"]()
        mk = u["scores"](b)
        mr = u["mask_rd"] and u["mask_rd"]()
        yield [mk, mr]
        need = [mk, free, f0, mr]
        if u["mask"] is None:
            t = [self.tsa(rows, b.t[:, 0:nk], -1.0, ALU.mult, ALU.min, st[:, 0:1], need)]
        elif u["sink"] is None:
            t = [self.ttr(rows, b.t[:, 0:nk], u["mask"], -1.0, -FLOOR, ALU.add, ALU.min, st[:, 0:1], need)]
        else:
            pl = self.cp(sm[:, nk:nk + 1], u["sink"], free, mr, f0, q=self.pool)
            t = [self.ttr(rows, b.t[:, 0:nk], u["mask"], -1.0, u["sink"], ALU.add, ALU.min, st[:, 0:1], need), pl]
        self.give(b, t[0])
        if u.get("shift") is not None:
            t = [self.ts(st[:, 0:1], st[:, 0:1], u["shift"], u["shift"], ALU.subtract, ALU.add, t, mr)]
        yield t
        t = self.a(sm, sm, ACT.Exp, t, bias=st[:, 0:1], scale=-1.0, accum=st[:, 1:2])
        gc, gr = u.get("gate_col"), None
        if gc is not None:
            yield u["gate_known"]
            gr = u["gate_rd"]()
        yield [t, gr]
        t = self.rec(st[:, 1:2], st[:, 1:2], t)
        if gc is None:
            done = self.ts(rows, rows, st[:, 1:2], None, ALU.mult, None, t)
        else:
            done = self.ts(rows, rows, st[:, 1:2], gc, ALU.mult, ALU.mult, t, gr)
        yield lambda: A["turned"] == k
        y, free = yield from A["pt"].take()
        b = yield from self.get(1)
        yield [done]
        nt, kw = max(1, nk // 128), min(128, nk)
        for q in range(nt):
            mk = self.tr(b.t[0:kw, 128 * q:128 * q + 128], sm[:, 128 * q:128 * q + kw], self.ident, done, b.free, inc=q == nt - 1)
        A["turned"] = k + 1
        A["sm"].give(u["at"], mk)
        yield [mk]
        u["pt"] = A["PT"][0:kw, y, 0:nt, :]
        u["ptr"] = self.a(u["pt"], b.t[0:kw, 0:128 * nt].rearrange("p (k q) -> p k q", k=nt), ACT.Copy, mk, free, f0)
        u["pt_at"] = y
        self.give(b, u["ptr"])

    def values(self, us, A, n):
        u = us[-1]
        yield lambda: A["values"] == n and all("ptr" in y for y in us) and u["vready"]()
        if u["first"]:
            u["box"]["o"] = yield from self.get(2)
        ob = u["box"]["o"]
        yield [y["ptr"] for y in us]
        mk = u["values"](ob, [y["pt"] for y in us], [y["ptr"] for y in us])
        A["values"] = n + 1
        for y in us:
            A["pt"].give(y["pt_at"], mk)
        if u["gate"] is not None:
            yield from u["gate"](ob, mk)

    def split(self, hh, hl, f, *need):
        a = self.a(hh, f, ACT.Copy, *need)
        yield [a]
        return self.tt(hl, f, hh, ALU.subtract, a, *need)

    def norm_rows(self, out, p, w, *need):
        ss = self.cols(2)
        sq = [self.a(out[:, i, 0:w], p[:, i, 0:w], ACT.Square, *need, accum=ss[:, i:i + 1]) for i in range(2)]
        yield sq
        rs, t = self.rstd(ss, 2, w, sq)
        yield [t]
        return [self.ts(out[:, i, 0:w], p[:, i, 0:w], rs[:, i:i + 1], None, ALU.mult, None, t, *need) for i in range(2)]

    def layer_b(self, l):
        f0 = self.fence
        QAh, QAl = self.Rr(0, 2, 512), self.Rr(1024, 2, 512)
        KAh, KAl = self.Rr(2048, 1, 512), self.Rr(2560, 1, 512)
        KP = self.Rr(3072, 2, 512)
        QP = self.Rr(4096, 2, 2, 512)
        QN, KN = self.F(6144, 2, 512), self.F(7168, 2, 512)
        V, ZT = self.F(8192, 2, 4, 128), self.F(9216, 2, 512)
        qf, gf, tmp = self.F(10240, 512), self.F(10752, 256), self.F(11008, 256)
        nat, nat2, f1, f2, pf = self.F(6144, 2, 256), self.F(6656, 2, 192), self.F(7168, 2, 256), self.F(7680, 1, 256), self.F(7936, 256)
        vc = self.vc
        qar, kar, kpr = [None] * 2, [None] * 2, [None] * 2
        c = dict(l=l, QN=QN, KN=KN, V=V, ZT=ZT, qf=qf, gf=gf, tmp=tmp, QP=QP, KP=KP, kpr=kpr, rd={}, qp={}, z={},
                 qn_s=Slots(2), v_s=Slots(2), qp_s=Slots(2), zt_s=Slots(2), gf_s=Slots(1), qf_s=Slots(1))
        self.gr = [[None] * 8, [None] * 8]
        free = dict(nat=[], nat2=[], f1=[], f2=[])

        def qa_tail(s, b, mk, f0, prev):
            yield lambda: prev is None or prev.done
            yield [mk]
            o = slice(256 * s, 256 * s + 256)
            nt = yield from self.norm_rows(nat, b.t[:, :].rearrange("p (i c) -> p i c", i=2), 256, mk, f0, free["nat"])
            self.give(b, nt)
            b = yield from self.get(1)
            yield nt
            for kt in range(2):
                for i in range(2):
                    mk = self.tr(b.t[:, 256 * kt + 128 * i:256 * kt + 128 * i + 128], nat[:, i, 128 * kt:128 * kt + 128],
                                 self.ident, nt, b.free)
            free["nat"] = [mk]
            yield [mk]
            ev = [self.ts(f1[:, kt, :], b.t[:, 256 * kt:256 * kt + 256], self.VC[:, vc["l1_g_qa"] + kt:vc["l1_g_qa"] + kt + 1],
                          None, ALU.mult, None, mk, f0, free["f1"]) for kt in range(2)]
            self.give(b, ev)
            yield ev
            qar[s] = yield from self.split(QAh[:, :, o], QAl[:, :, o], f1[:, :, :], ev, f0)
            free["f1"] = [qar[s]]

        def kva_tail(s, b, mk, f0, prev):
            yield lambda: prev is None or prev.done
            yield [mk]
            o = slice(256 * s, 256 * s + 256)
            p2 = b.t[:, 0:384].rearrange("p (i c) -> p i c", i=2)
            nt = yield from self.norm_rows(nat2, p2, 128, mk, f0, free["nat2"])
            nt = [nt, self.cp(nat2[:, :, 128:192], p2[:, :, 128:192], nt, free["nat2"], f0)]
            self.give(b, nt)
            b = yield from self.get(1)
            yield nt
            for i in range(2):
                mk = self.tr(b.t[:, 128 * i:128 * i + 128], nat2[:, i, 0:128], self.ident, nt, b.free)
            for i in range(2):
                mk = self.tr(b.t[0:64, 256 + 128 * i:384 + 128 * i], nat2[:, i, 128:192], self.ident, nt)
            free["nat2"] = [mk]
            yield [mk]
            ev = [self.ts(f2[:, 0, :], b.t[:, 0:256], self.VC[:, vc["l1_g_kva"]:vc["l1_g_kva"] + 1], None, ALU.mult, None,
                          mk, f0, free["f2"])]
            e2 = self.cp(pf[0:64, :], b.t[0:64, 256:512], mk, f0, free["f2"])
            self.give(b, ev, e2)
            yield ev
            kar[s] = yield from self.split(KAh[:, 0, o], KAl[:, 0, o], f2[:, 0, :], ev, f0)
            if s == LAT:
                e2 = self.rope(pf[0:64, :], tmp, e2, f0)
            yield [e2]
            kp = []
            for r in (slice(0, 64), slice(64, 128)):
                kp.append(self.a(KP[r, 0, o], pf[0:64, :], ACT.Copy, e2, f0))
            yield kp
            for r in (slice(0, 64), slice(64, 128)):
                kp.append(self.tt(KP[r, 1, o], pf[0:64, :], KP[0:64, 0, o], ALU.subtract, e2, kp[0], f0))
            free["f2"] = [kp, kar[s]]
            kpr[s] = kp
        jq = yield from self.w.job(("qa",))
        jk = None
        tq = tk = None
        tails = []
        for s in (CT, LAT):
            if s == LAT:
                f0 = yield from self.turned()
            b, mk = yield from self.prod_b(jq, 256, s)
            tq = self.spawn(qa_tail(s, b, mk, f0, tq), 0.0)
            if s == LAT:
                self.w.free(jq, mk)
            if jk is None:
                jk = yield from self.w.job(("kva",))
            b, mk = yield from self.prod_b(jk, 192, s)
            tk = self.spawn(kva_tail(s, b, mk, f0, tk), 0.0)
        self.w.free(jk, mk)
        c["f0"] = f0
        yield from self.z_b(c, 0)
        yield from self.z_b(c, 1)
        yield lambda: tq.done and tk.done
        c["fz"] = self.fence = self.now()
        att = self.spawn(self.attention(self.units_b(c), at=11264, nsm=4, npt=2, wide=512), 0.5)
        yield from self.proj_b(c, QAh, QAl, KAh, KAl, qar, kar)
        yield lambda: att.done

    def z_b(self, c, h):
        def tail(b, mk):
            x, free = yield from c["zt_s"].take()
            yield [mk]
            z = c["ZT"][:, x, :]
            ta = self.a(z, b.t[:, :], ACT.Tanh, mk, free, f0, scale=0.5)
            yield [ta]
            td = self.stt(z, z, 1.0, b.t[:, :], ALU.add, ALU.mult, ta)
            self.give(b, td)
            c["z"][h] = (x, td)
        f0 = c["f0"]
        job = yield from self.w.job(("zb", h))
        b = yield from self.get(4)
        mk = yield from self.form_a(job, 0, 128, b.t[:, :], 0, 512, self.Hh, self.Hl, self.hrd(0, 2), b.free)
        self.w.free(job, mk)
        if h == 7:
            self.h_free = [mk]
        self.spawn(tail(b, mk), 0.0)

    def proj_b(self, c, QAh, QAl, KAh, KAl, qar, kar):
        l = c["l"]
        scale = float(192.0 ** -0.5)
        QN, KN, V, qf, tmp, QP = (c[k] for k in ("QN", "KN", "V", "qf", "tmp", "QP"))
        fz = c["fz"]

        def rot_tail(p, b, mk):
            _, free = yield from c["qf_s"].take()
            yield [mk]
            t1 = self.a(qf, b.t[:, :], ACT.Copy, mk, fz, free, scale=scale)
            self.give(b, t1)
            yield [t1]
            r0 = [self.rope(qf[:, 256:512], tmp, t1, fz), t1]
            y, free = yield from c["qp_s"].take()
            yield r0
            rd = []
            for e in range(2):
                r, z = slice(64 * e, 64 * e + 64), slice(64 - 64 * e, 128 - 64 * e)
                ah = self.a(QP[r, y, e, :], qf[r], ACT.Copy, r0, free)
                yield [ah]
                d = self.tt(QP[z, y, e, :], qf[r], QP[r, y, e, :], ALU.subtract, ah, r0, free)
                rd += [ah, d]
            c["qf_s"].give(0, rd)
            c["qp"][p] = (y, rd)

        def head_tail(h, bq, mq, bk, mk, bv, mv):
            x, free = yield from c["qn_s"].take()
            yield [mq]
            rq = self.a(QN[:, x, :], bq.t[:, :], ACT.Copy, mq, fz, free, scale=scale)
            self.give(bq, rq)
            yield [mk]
            rk = self.a(KN[:, x, :], bk.t[:, :], ACT.Copy, mk, fz, free)
            self.give(bk, rk)
            y, free = yield from c["v_s"].take()
            yield [mv]
            rv = self.cp(V[:, y], bv.t[:, :].rearrange("p (t c) -> p t c", t=4), mv, fz, free)
            self.give(bv, rv)
            c["rd"][h] = (x, y, [rq, rk, rv])
        for h in range(8):
            e, p = h % 2, h // 2
            if e == 0:
                uq = yield from self.w.job(("uq", p))
                ukv = yield from self.w.job(("ukv", p))
                b = yield from self.get(4)
                mk = yield from self.form_a(uq, 0, 128, b.t[:, :], 0, 512, QAh, QAl, lambda k: qar, b.free)
                self.spawn(rot_tail(p, b, mk), 0.0)
            bq = yield from self.get(4)
            mq = yield from self.form_a(uq, 128 + 128 * e, 128, bq.t[:, :], 0, 512, QAh, QAl, lambda k: qar, bq.free)
            bk = yield from self.get(4)
            mkk = yield from self.form_a(ukv, 256 * e, 128, bk.t[:, :], 0, 512, KAh, KAl, lambda k: kar, bk.free)
            bv = yield from self.get(4)
            for t in range(4):
                mv = yield from self.form_b(ukv, 256 * e + 128, 128, bv.t[:, 128 * t:128 * t + 128], 128 * t, KAh, KAl,
                                            lambda k: kar, bv.free)
            self.spawn(head_tail(h, bq, mq, bk, mkk, bv, mv), 0.0)
            if e == 1:
                self.w.free(uq, mv)
                self.w.free(ukv, mv)
            if h > 1:
                yield from self.z_b(c, h)
            yield from self.ada_some(l, h, 9)
        yield from self.ada_some(l, 8, 9)

    def units_b(self, c):
        QN, KN, V, QP, KP = (c[k] for k in ("QN", "KN", "V", "QP", "KP"))
        left, pleft, vleft = {}, {}, {}
        for h in range(8):
            left[h], vleft[h] = 4, 4
            if h % 2 == 0:
                pleft[h // 2] = 8
            for s in (CT, LAT):
                box = {}
                for i in range(2):
                    e = h % 2
                    nk = 256 if s == CT else 512
                    nt = nk // 128

                    def ready(h=h):
                        return h in c["rd"] and h // 2 in c["qp"]

                    def need(h=h, s=s):
                        return [c["rd"][h][2], c["qp"][h // 2][1], c["kpr"][:s + 1]]

                    def scores(b, s=s, e=e, i=i, nk=nk, h=h, need=need):
                        o = slice(256 * s + 128 * i, 256 * s + 128 * i + 128)
                        x, y = c["rd"][h][0], c["qp"][h // 2][0]
                        self.mm(b.t[:, 0:nk], QN[:, x, o], KN[:, x, 0:nk], True, False, need(), b.free)
                        self.mm(b.t[:, 0:nk], QP[:, y, e, o], KP[:, 0, 0:nk], False, False)
                        mk = self.mm(b.t[:, 0:nk], QP[:, y, e, o], KP[:, 1, 0:nk], False, True, inc=True)
                        left[h] -= 1
                        pleft[h // 2] -= 1
                        if left[h] == 0:
                            c["qn_s"].give(x, mk)
                        if pleft[h // 2] == 0:
                            c["qp_s"].give(y, mk)
                        return mk

                    def values(ob, pts, marks, h=h, i=i, nt=nt):
                        y = c["rd"][h][1]
                        for k in range(nt):
                            mk = self.mm(ob.t[:, 128 * i:128 * i + 128], V[:, y, k, :], pts[0][:, k, :], k == 0, k == nt - 1,
                                         marks, ob.free, inc=k == nt - 1)
                        vleft[h] -= 1
                        if vleft[h] == 0:
                            c["v_s"].give(y, mk)
                        return mk

                    def gate(ob, mk, s=s, h=h):
                        o = slice(256 * s, 256 * s + 256)
                        yield lambda: h in c["z"]
                        x, zr = c["z"][h]
                        y, free = yield from c["gf_s"].take()
                        yield [mk, zr]
                        gf = c["gf"]
                        d = self.stt(gf, ob.t[:, 0:256], 0.5, c["ZT"][:, x, o], ALU.mult, ALU.mult, mk, zr, free, c["fz"])
                        self.give(ob, d)
                        if s == LAT:
                            c["zt_s"].give(x, d)
                        yield [d]
                        d = yield from self.split(self.Gh[:, h, o], self.Gl[:, h, o], gf, d, self.g_free)
                        c["gf_s"].give(y, d)
                        self.gr[s][h] = d

                    yield dict(ready=ready, need=need, scores=scores, values=values, nk=nk, pair=None, box=box, first=i == 0,
                               vready=lambda: True, gate=gate if i == 1 else None, mask=None, sink=None, mask_rd=None)

    def finish_layer(self, l, streams, nxt):
        self.fence = f = self.now()
        self.out_at[l] = f
        buf = {CT: 8192, LAT: 11264}
        YG = {s: self.F(buf[s], 2, D) for s in streams}
        ss = {s: self.cols(8).rearrange("p (i j) -> p i j", i=2) for s in streams}
        yr, sr = {}, {}
        if len(streams) == 2:
            seq = [(CT, 0), (LAT, 0), (CT, 1), (LAT, 1), (CT, 2), (CT, 3), (LAT, 2), (LAT, 3)]
        else:
            seq = [(LAT, j) for j in range(4)]
        if l == 0:
            self.spawn(self.ext_rows(), 0.0)
        hr = self.new_h() if nxt is not None else None
        gr = self.gr
        jobs = {}

        def tile(s, i, nt):
            yield lambda: all((s, i, j) in sr for j in range(4))
            s2 = self.cols(1)
            need = [sr[s, i, j] for j in range(4)] + [yr[s, i, j] for j in range(4)]
            yield need
            t = self.red(s2, ss[s][:, i, :], ALU.add, need)
            rs, t = self.rstd(s2, 1, D, t)
            yield [t]
            x, yg = self.X[:, 2 * s + i, :], YG[s][:, i, :]
            self.xr[2 * s + i] = t = self.stt(x, yg, rs, x, ALU.mult, ALU.add, t, need, self.xr[2 * s + i])
            if nxt is not None:
                yield from self.norm_tile(s, i, YG[s], nt, t)

        def rest(s):
            nt = [None, None]
            ts = [self.spawn(tile(s, i, nt), 0.0) for i in range(2)]
            yield lambda: all(t.done for t in ts)
            if nxt is not None:
                yield from self.make_h(hr, nxt(s), s, YG[s], self.F(buf[s] + 2048, 2, 2, 256), nt, f)

        def tail(s, i, j, b, mk):
            yield [mk]
            o = slice(256 * j, 256 * j + 256)
            yr[s, i, j] = d = self.tt(YG[s][:, i, o], b.t[:, 0:256], self.G[:, s, o], ALU.mult, mk, f, self.g_rd)
            yield [d]
            sr[s, i, j] = a = self.a(b.t[:, 0:256], b.t[:, 0:256], ACT.Square, mk, d, accum=ss[s][:, i, j:j + 1])
            self.give(b, a)
        turn = {s: self.spawn(rest(s), 0.0) for s in streams}
        for s, j in seq:
            if j not in jobs:
                jobs[j] = yield from self.w.job(("out", l, j))
            job = jobs[j]
            for i in range(2):
                b = yield from self.get(2)
                mk = yield from self.form_b(job, 0, 256, b.t[:, 0:256], 256 * s + 128 * i, self.Gh, self.Gl,
                                            lambda k, s=s: [gr[s][k]], b.free)
                self.spawn(tail(s, i, j, b, mk), 0.0)
            if s == streams[-1]:
                self.w.free(job, mk)
        self.g_free = [mk]
        if CT in streams:
            yield lambda: turn[CT].done
        yield lambda: len(yr) == 8 * len(streams)
        self.G_free = list(yr.values())
        self.turn = turn[LAT]

    def layer_c(self, l):
        f0 = self.fence
        c = dict(l=l, f0=f0, cell=-1)
        F = self.F
        c.update(QT=F(0, 2, 512), KT=F(1024, 2, 512), VA=F(2048, 2, 4, 258), Y=F(4112, 512), TH=F(4624, 512), RN=F(5136, 512),
                 BC=F(5648, 4, 36), AC=F(5792, 4, 36), MC=F(5936, 4, 36), AL=F(6080, 8, 4), E=F(6112, 2, 4),
                 DT=F(6320, 2, 512), HS=F(7344, 2, 4, 256), KE=F(9392, 2, 3, 128), CS=F(10160, 2, 2, 258), IT=F(11192, 2, 258),
                 NUM=F(11708, 2, 258), TH2=F(12224, 512), ZZ=F(12736, 2, 256), GF=F(13248, 2, 256), TH3=F(13760, 512))
        idb = self.SF[:, 6128:6192].bitcast(BF16)
        mkb = self.SF[:, 6192:6320].bitcast(BF16)
        c["idb"], c["mkb"] = idb, mkb.rearrange("p (d t) -> p d t", d=2)
        A = [F(6320 + 512 * i, 512) for i in range(6)] + [F(9392 + 512 * i, 512) for i in range(5)]
        c.update(rd={}, hs_rd={}, y_s=Slots(1), th_s=Slots(2), zz_s=Slots(1), gf_s=Slots(1), q_s=Slots(2), k_s=Slots(2), v_s=Slots(2),
                 hs_s=Slots(2), gates_rd=None)

        def masks():
            ml = self.dma(self.sp, "mlmask", c["TH"][:, 0:256], self.ins["mlmask"], f0)
            r1 = self.cp(idb, self.ident, f0, self.k_rd)
            c["ones"] = self.mset(c["VA"][:, :, :, 256:257], 1.0, f0)
            yield [ml]
            r2 = self.cp(mkb, c["TH"][:, 0:256], ml, f0)
            c["mask_rd"] = [r1, r2]
        mt = self.spawn(masks(), 0.0)
        self.gr = [[None] * 8, [None] * 8]
        c["masks"] = mt
        cell = self.spawn(self.cells(c), 0.5)
        H = (self.Hh, self.Hl)
        jobs = []
        qb = []
        for s in (CT, LAT):
            if s == LAT:
                c["fz"] = yield from self.turned()
            for x in range(2):
                if s == CT:
                    jobs.append((yield from self.w.job((("qc", "kc")[x], 0))))
                    qb.append((yield from self.get(4)))
                mk = yield from self.form_a(jobs[x], 0, 128, qb[x].t[:, 256 * s:256 * s + 256], 256 * s, 256, *H, self.hrd(s, s + 1),
                                            qb[x].free if s == CT else [])
                if s == LAT:
                    self.w.free(jobs[x], mk)
                    self.spawn(self.conv_c(c, 0, x, qb[x], mk), 0.0)
            if s == CT:
                jobs.append((yield from self.w.job(("vc", 0))))
                v, free = yield from c["v_s"].take()
                c["rd"][0] = dict(v=v)
            b, mk = yield from self.prod_b(jobs[2], 256, s)
            self.spawn(self.v_tail(c, 0, v, free, s, b, mk), 0.0)
        self.w.free(jobs[2], mk)
        yield from self.gates_c(c, A)
        yield from self.ada_some(l, 0, 8)
        for j in range(1, 4):
            yield from self.qkv_c(c, j)
            yield from self.ada_some(l, 2 * j - 1, 8)
            yield from self.oz_c(c, j - 1)
            yield from self.ada_some(l, 2 * j, 8)
        yield from self.oz_c(c, 3)
        yield from self.ada_some(l, 7, 8)
        yield lambda: all(known(self.gr[s]) for s in range(2))

    def gates_c(self, c, A):
        job = yield from self.w.job(("gates",))
        b = yield from self.get(4)
        mk = yield from self.form_a(job, 0, 16, b.t[0:16, :], 0, 512, self.Hh, self.Hl, self.hrd(0, 2), b.free)
        self.w.free(job, mk)
        self.spawn(self.gates_tail(c, A, b, mk), 0.0)

    def gates_tail(self, c, A, b, mk):
        l, f0 = c["l"], c["fz"]
        bg = A[0][0:16, 0:1]
        bg_rd = self.dma(self.sp, "bg", bg, self.ins[f"l{l}_b_gate"].rearrange("(a c) -> a c", c=1), f0)
        GT, IG, FG, T1, CM, PM, BN, AN, MN, RM, RG = (A[i] for i in (1, 2, 3, 4, 5, 6, 7, 8, 9, 10, 0))
        zs = [self.mset(a[0:36, :], 0.0, f0, q=self.pool) for a in (IG, FG, AN, MN)]
        z1 = self.mset(RM[0:36, :], 1.0, f0, q=self.pool)
        z1 = self.mset(RM[0:36, 0::128], 0.0, z1, q=self.pool)
        yield [mk, bg_rd]
        t = self.a(GT[0:16, :], b.t[0:16, :], ACT.Identity, mk, bg_rd, f0, bias=bg)
        self.give(b, t)
        z2 = self.mset(RG[0:36, :], 0.0, t, q=self.pool)
        z2 = self.mset(RG[0:36, 0::128], FLOOR, z2, q=self.pool)
        d = [self.dma(self.sp, "g0", IG[0:4, :], GT[0:4, :], t, zs), self.dma(self.sp, "g0", FG[0:4, :], GT[4:8, :], t, zs),
             self.dma(self.sp, "g0", AN[32:36, :], GT[8:12, :], t, zs), self.dma(self.sp, "g0", MN[32:36, :], GT[12:16, :], t, zs)]
        yield d
        b_ = slice(32, 36)
        rev = lambda a, s: a[b_, 256 * s:256 * s + 256][:, ::-1]
        nat = lambda a, s: a[b_, 256 * s:256 * s + 256]
        t = []
        for s in range(2):
            t.append(self.cp(nat(IG, s), rev(AN, s), d, zs))
            t.append(self.cp(nat(FG, s), rev(MN, s), d, zs))
        r = slice(0, 36)
        t = t0 = self.stt(T1[r, :], FG[r, :], -1.0, FG[r, :], ALU.mult, ALU.min, t, f0)
        yield [t]
        t = self.a(T1[r, :], T1[r, :], ACT.Exp, t)
        t = self.a(T1[r, :], T1[r, :], ACT.Ln, t, bias=1.0)
        yield [t]
        t = self.stt(FG[r, :], FG[r, :], 0.0, T1[r, :], ALU.min, ALU.subtract, t)
        t = self.v(lambda e: e.tensor_tensor_scan(CM[r, :], RM[r, :], FG[r, :], 0.0, ALU.mult, ALU.add), CM[r, :], t, z1, f0)
        tb = t = self.tt(IG[r, :], IG[r, :], CM[r, :], ALU.subtract, t)
        t = self.v(lambda e: e.tensor_tensor_scan(PM[r, :], RG[r, :], IG[r, :], FLOOR, ALU.add, ALU.max), PM[r, :], t, z2, f0)
        m = self.cols(4)[r, :]
        tm = self.mset(m[:, 0:1], NEG)
        for p in range(3):
            last = slice(128 * p + 127, 128 * p + 128)
            tm = self.stt(m[:, p + 1:p + 2], PM[r, last], m[:, p:p + 1], CM[r, last], ALU.max, ALU.add, t, tm)
        yield [tm]
        rd = []
        for p in range(4):
            o = slice(128 * p, 128 * p + 128)
            t2 = self.ts(PM[r, o], PM[r, o], m[:, p:p + 1], -1.0, ALU.max, ALU.mult, tm)
            rd.append(t2)
            rd.append(self.ts(FG[r, o], PM[r, o], m[:, p:p + 1], None, ALU.add, None, t2))
        rd.append(self.tt(T1[r, :], PM[r, :], CM[r, :], ALU.subtract, rd))
        yield rd
        out = []
        for dst, src in ((c["RN"], PM), (BN, IG), (AN, FG), (MN, T1)):
            z = self.mset(dst[r, :], 0.0, rd, f0, q=self.pool)
            out.append(self.cp(dst[0:4, :], src[0:4, :], rd, z, tb))
            for s in range(2):
                out.append(self.cp(nat(dst, s), rev(src, s), rd, z, tb))
        b = yield from self.get(2)
        b2 = yield from self.get(1)
        yield out
        pv = b.t[:, 0:432].rearrange("p (a c h) -> p a c h", a=3, c=4)
        for a, src in enumerate((BN, AN, MN)):
            for q in range(4):
                mk = self.tr(pv[:, a, q, :], src[r, 128 * q:128 * q + 128], self.ident[0:36, 0:36], out, b.free)
        for d_ in range(2):
            for h in range(4):
                row = 32 * d_ + h
                rhs = AN[r, (127 if d_ == 0 else 0)::128]
                mk2 = self.mm(b2.t[:, 4 * (4 * d_ + h):4 * (4 * d_ + h) + 4], self.ident[0:36, row:row + 1].to_broadcast([36, 128]),
                              rhs, True, True, out, b2.free, inc=True, cost=213.0)
        yield [mk2]
        t1 = self.a(c["BC"][:, :, :], pv[:, 0], ACT.Copy, mk, f0)
        t2 = self.a(c["AC"][:, :, :], pv[:, 1], ACT.Exp, mk, f0)
        t3 = self.a(c["MC"][:, :, :], pv[:, 2], ACT.Exp, mk, f0)
        self.give(b, t3)
        t4 = self.a(c["AL"][:, :, :], b2.t[:, 0:32].rearrange("p (a b) -> p a b", a=8), ACT.Exp, mk2, f0)
        self.give(b2, t4)
        yield [t4]
        t5 = self.ts(c["AC"][:, :, :], c["AC"][:, :, :], 0.5, None, ALU.mult, None, t2)
        c["gates_rd"] = [out, t1, t3, t4, t5]
        c["tmp_free"] = self.now()

    def conv_c(self, c, j, x, b, mk):
        vc = self.vc["l2_conv"] + 4 * x + j
        w = lambda d: self.VC[:, vc + 8 * d:vc + 8 * d + 1]
        Y, TH = c["Y"], c["TH"]
        x3, y3 = b.t[:, :].rearrange("p (s t) -> p s t", s=2), Y.rearrange("p (s t) -> p s t", s=2)
        yield lambda: c["masks"].done
        _, yfree = yield from c["y_s"].take()
        at, free = yield from c[("q_s", "k_s")[x]].take()
        yield [mk]
        t = self.a(Y, b.t[:, :], ACT.Copy, mk, yfree, c["mask_rd"], c["f0"], scale=w(2))
        yield [t]
        for d in (0, 1, 3, 4):
            sh = d - 2
            o, i = slice(max(0, -sh), 256 - max(0, sh)), slice(max(0, sh), 256 + min(0, sh))
            t = self.stt(y3[:, :, o], x3[:, :, i], w(d), y3[:, :, o], ALU.mult, ALU.add, t)
        self.give(b, t)
        yield [t]
        ta = self.a(TH, Y, ACT.Tanh, t, yfree, scale=0.5)
        yield [ta]
        dst = (c["QT"], c["KT"])[x][:, at]
        td = self.stt(dst, TH, 1.0, Y, ALU.add, ALU.mult, ta, free, c["fz"])
        c["y_s"].give(0, td)
        r = c["rd"].setdefault(j, {})
        r["qk"[x]] = at
        r["qk"[x] + "r"] = td

    def v_tail(self, c, j, v, free, s, b, mk):
        yield lambda: c["masks"].done
        yield [mk]
        t = self.a(c["VA"][:, v, 2 * s:2 * s + 2, 0:256], b.t[:, :].rearrange("p (i v) -> p i v", i=2), ACT.Copy, mk, free, c["ones"])
        self.give(b, t)
        c["rd"][j][f"v{s}"] = t

    def qkv_c(self, c, j):
        for x, key in enumerate(("qc", "kc")):
            job = yield from self.w.job((key, j))
            b = yield from self.get(4)
            mk = yield from self.form_a(job, 0, 128, b.t[:, :], 0, 512, self.Hh, self.Hl, self.hrd(0, 2), b.free)
            self.w.free(job, mk)
            self.spawn(self.conv_c(c, j, x, b, mk), 0.0)
        job = yield from self.w.job(("vc", j))
        v, free = yield from c["v_s"].take()
        c["rd"].setdefault(j, {})["v"] = v
        for s in range(2):
            b, mk = yield from self.prod_b(job, 256, s)
            self.spawn(self.v_tail(c, j, v, free, s, b, mk), 0.0)
        self.w.free(job, mk)

    def cells(self, c):
        kap = 0.25 * 128.0 ** -0.5
        kst = 0.5 * 128.0 ** -0.5
        order = ((0, 1, 2, 3), (1, 0, 3, 2))
        free = dict(dt=[], ke=[], e=[], cs=[[[], []], [[], []]], it=[[], []], num=[[], []])

        def direction(h, hx, d, R, sq, ke, seen):
            QT, VA, HS = c["QT"][:, R["q"]], c["VA"][:, R["v"]], c["HS"][:, hx]
            DT, KE, CS = c["DT"], c["KE"], c["CS"]
            tf = c["tmp_free"]
            row = 32 * d + h
            cr = None
            for p in range(4):
                q = order[d][p]
                o = slice(128 * q, 128 * q + 128)
                va = VA[:, q, 0:257]
                ti = None
                if p > 0:
                    ib = yield from self.get(1)
                    yield [cr]
                    mn = self.mm(ib.t[:, 0:257], QT[:, o], CS[:, d, (p + 1) % 2, 0:257], True, True, cr, ib.free, inc=True)
                    free["cs"][d][(p + 1) % 2] = [mn, cr]
                if p < 3:
                    stb = yield from self.get(1)
                    yield [ke[d][p]]
                    mst = self.mm(stb.t[:, 0:257], KE[:, d, p, :], va, True, True, ke[d][p], stb.free, inc=True)
                    yield [mst]
                    new, old = CS[:, d, p % 2, 0:257], CS[:, d, (p + 1) % 2, 0:257]
                    if p == 0:
                        nr = self.cp(new, stb.t[:, 0:257], mst, free["cs"][d][p % 2], tf)
                    else:
                        nr = self.stt(new, old, c["AL"][:, 4 * d + h, q:q + 1], stb.t[:, 0:257], ALU.mult, ALU.add, mst,
                                      cr, free["cs"][d][p % 2], tf)
                        free["cs"][d][(p + 1) % 2] = [mn, nr]
                    self.give(stb, nr)
                if p > 0:
                    yield [mn]
                    ti = self.a(c["IT"][:, d, 0:257], ib.t[:, 0:257], ACT.Copy, mn, free["it"][d], tf, scale=c["AC"][:, q, row:row + 1])
                    self.give(ib, ti)
                nb = yield from self.get(1)
                mi = self.mm(nb.t[:, 0:257], DT[:, d, o], va, True, True, sq[d], nb.free, inc=True)
                if p < 3:
                    cr = nr
                yield [mi, ti]
                num = c["NUM"][:, d, 0:257]
                if p > 0:
                    t = self.tt(num, c["IT"][:, d, 0:257], nb.t[:, 0:257], ALU.add, mi, ti, free["num"][d], tf)
                    free["it"][d] = [t]
                else:
                    t = self.cp(num, nb.t[:, 0:257], mi, free["num"][d], tf)
                self.give(nb, t)
                dn = self.cols(1)
                t = self.stt(dn, num[:, 256:257], -1.0, num[:, 256:257], ALU.mult, ALU.max, t)
                t = self.tt(dn, dn, c["MC"][:, q, row:row + 1], ALU.max, t)
                t = self.rec(dn, dn, t)
                if q not in seen:
                    t = self.ts(HS[:, q, :], num[:, 0:256], dn, None, ALU.mult, None, t, free["hs"], tf)
                else:
                    t = self.stt(HS[:, q, :], num[:, 0:256], dn, HS[:, q, :], ALU.mult, ALU.add, t, seen[q])
                seen[q] = t
                free["num"][d] = [t]

        for h in range(4):
            keys = ("qr", "kr", "v0", "v1")
            yield lambda: c["gates_rd"] is not None and all(k in c["rd"].get(h, {}) for k in keys)
            R = c["rd"][h]
            QT, KT = c["QT"][:, R["q"]], c["KT"][:, R["k"]]
            DT, KE, E = c["DT"], c["KE"], c["E"]
            rd, g, tf = [[R[k] for k in keys], c["ones"]], c["gates_rd"], c["tmp_free"]
            hx, free["hs"] = yield from c["hs_s"].take()
            sb = yield from self.get(3)
            yield rd
            for q in range(4):
                o = slice(128 * q, 128 * q + 128)
                mks = self.mm(sb.t[:, o], KT[:, o], QT[:, o], True, True, rd, sb.free, inc=True)
            ex = [None, None]

            def decay(d):
                row = 32 * d + h
                b = yield from self.get(1)
                yield g
                self.mm(b.t[:, :], self.ident[0:36, row:row + 1].to_broadcast([36, 128]), c["RN"][0:36, :], True, False, g, b.free)
                mk = self.mm(b.t[:, :], c["idb"], c["mkb"][:, d:d + 1, :].to_broadcast([128, 4, 128]), False, True,
                             c["mask_rd"], inc=True, cost=213.0)
                te = []
                yield [mk, free["dt"]]
                for q in range(4):
                    o = slice(128 * q, 128 * q + 128)
                    te.append(self.a(DT[:, d, o], b.t[:, o], ACT.Exp, mk, free["dt"], tf, bias=c["BC"][:, q, row:row + 1]))
                self.give(b, te)
                yield te
                last = (127 if d == 0 else 0)
                ex[d] = [te, self.cp(E[:, d, :], DT[:, d, last::128], te, free["e"])]
                sq[d] = self.stt(DT[:, d, :], sb.t[:, :], kap, DT[:, d, :], ALU.mult, ALU.mult, mks, ex[d])
            sq = [None, None]
            tasks = [self.spawn(decay(d), 0.0) for d in range(2)]
            yield lambda: all(t.done for t in tasks)
            self.give(sb, sq)
            kb = yield from self.get(1)
            for q in range(4):
                mkk = self.tr(kb.t[:, 128 * q:128 * q + 128], KT[:, 128 * q:128 * q + 128], self.ident, kb.free)
            yield [mkk]
            ke = [[None] * 3, [None] * 3]
            for p in range(3):
                for d in range(2):
                    q = order[d][p]
                    ke[d][p] = self.ts(KE[:, d, p, :], kb.t[:, 128 * q:128 * q + 128], E[:, d, q:q + 1], kst, ALU.mult, ALU.mult,
                                       mkk, ex[d], free["ke"], tf)
            self.give(kb, ke[0][2], ke[1][2])
            free["e"] = [ke]
            seen = {}
            tasks = [self.spawn(direction(h, hx, d, R, sq, ke, seen), 0.0) for d in range(2)]
            yield lambda: all(t.done for t in tasks)
            fr = [(self.pe.name, self.pe.count)]
            free["dt"] = free["ke"] = fr
            for k in ("q", "k", "v"):
                c[k + "_s"].give(R[k], fr)
            c["hs_rd"][h] = (hx, [seen[q] for q in range(4)])
            c["cell"] = h

    def oz_c(self, c, j):
        l = c["l"]
        rs, rt = [None] * 2, [None] * 2
        ths = (c["TH2"], c["TH3"])

        def o_tail(s, b, mk):
            x, free = yield from c["th_s"].take()
            yield lambda: c["gates_rd"] is not None
            tf = c["tmp_free"]
            yield [mk]
            th = ths[x]
            ta = self.a(th, b.t[:, :], ACT.Tanh, mk, free, tf, scale=0.5)
            self.give(b, ta)
            yield lambda: c["cell"] >= j
            hx, hrd = c["hs_rd"][j]
            hs = c["HS"][:, hx, 2 * s:2 * s + 2, :]
            yield [ta, hrd]
            t = self.stt(hs, th.rearrange("p (i v) -> p i v", i=2), 1.0, hs, ALU.add, ALU.mult, ta, hrd)
            c["th_s"].give(x, t)
            ss = self.cols(2)
            _, free = yield from c["zz_s"].take()
            yield [t]
            sq = [self.a(c["ZZ"][:, i, :], hs[:, i, :], ACT.Square, t, free, tf, accum=ss[:, i:i + 1]) for i in range(2)]
            c["zz_s"].give(0, sq)
            yield sq
            rs[s], rt[s] = self.rstd(ss, 2, 1024, sq)

        def z_tail(s, b, mk):
            x, free = yield from c["th_s"].take()
            tf = c["tmp_free"]
            yield [mk]
            th = ths[x]
            ta = self.a(th, b.t[:, :], ACT.Tanh, mk, free, tf, scale=0.5)
            bz = b.t[:, :].rearrange("p (i v) -> p i v", i=2)
            yield lambda: rt[s] is not None
            _, free = yield from c["zz_s"].take()
            yield [ta]
            t = self.stt(c["ZZ"][:, :, :], th.rearrange("p (i v) -> p i v", i=2), 1.0, bz, ALU.add, ALU.mult, ta, free)
            self.give(b, t)
            c["th_s"].give(x, t)
            gt = []
            hx = c["hs_rd"][j][0]
            HS = c["HS"][:, hx]
            yield [rt[s]]
            for i in range(2):
                hs = HS[:, 2 * s + i, :]
                gt.append(self.stt(hs, hs, rs[s][:, i:i + 1], c["ZZ"][:, i, :], ALU.mult, ALU.mult, t, rt[s]))
            c["zz_s"].give(0, gt)
            b = yield from self.get(1)
            yield gt
            for f in range(2):
                for i in range(2):
                    mt = self.tr(b.t[:, 256 * f + 128 * i:256 * f + 128 * i + 128], HS[:, 2 * s + i, 128 * f:128 * f + 128],
                                 self.ident, gt, b.free)
            _, free = yield from c["gf_s"].take()
            yield [mt]
            ev = []
            for f in range(2):
                g = self.vc["l2_g_head"] + 2 * j + f
                ev.append(self.ts(c["GF"][:, f, :], b.t[:, 256 * f:256 * f + 256], self.VC[:, g:g + 1], 0.25, ALU.mult, ALU.mult,
                                  mt, free, tf))
            self.give(b, ev)
            done[s] = mt
            if known(done):
                c["hs_s"].give(hx, done)
            yield ev
            o = slice(256 * s, 256 * s + 256)
            d = yield from self.split(self.Gh[:, 2 * j:2 * j + 2, o], self.Gl[:, 2 * j:2 * j + 2, o], c["GF"][:, :, :], ev, self.g_free)
            c["gf_s"].give(0, d)
            self.gr[s][2 * j] = self.gr[s][2 * j + 1] = d
        done = [None, None]
        for key, tail in (("oc", o_tail), ("zc", z_tail)):
            job = yield from self.w.job((key, j))
            for s in range(2):
                b, mk = yield from self.prod_b(job, 256, s)
                self.spawn(tail(s, b, mk), 0.0)
            self.w.free(job, mk)
        if j == 3:
            self.h_free = [mk]

    def ext_rows(self):
        tab, t34, ev = self.F(4096, 384), self.F(4480, 16), self.F(4608, 384)
        f0 = self.fence
        r = [self.dma(self.sp, "ext", tab[0:34, :], self.ins["onehot"], f0),
             self.dma(self.sp, "ext", t34[0:32, :], self.ins["rel_bias_2"], f0),
             self.dma(self.sp, "ext", t34[32:34, :], self.ins["tabrows"], f0)]
        b = yield from self.get(2)
        yield r
        mk = self.mm(b.t[0:16, 0:384], t34[0:34, :], tab[0:34, :], True, True, r, self.fence, b.free, inc=True)
        yield [mk]
        t = self.cp(ev[0:16, :], b.t[0:16, 0:384], mk, self.fence)
        self.give(b, t)
        self.ext = self.nc.dram_tensor("ext_rows", (16, 128, 384), F32).ap()
        src = ev[0:16, :].rearrange("p (a c) -> p a c", a=1).to_broadcast([16, 128, 384])
        self.ext_rd = self.dma(self.sp, "extw", self.ext, src, t)

    def second(self):
        f0 = self.fence = self.now()
        F, X, K, i = self.F, self.X, self.K, self.ins
        Xf = X[:, 0:2, :].rearrange("p a b -> p (a b)")
        c = dict(f0=f0, at=set(), gf_s=Slots(1), nq_s=Slots(2), sq_s=Slots(1), kw_s=Slots(1))
        c["Q"] = F(0, 12, 256)
        c["KD"] = F(3072, 3, 2, 256)
        c["CK"] = F(4608, 4, 256)
        c["VN"] = F(5632, 3, 2, 128)
        c["CV"] = F(6400, 2, 2, 256)
        c["strip"] = F(7424, 16, 256)
        c["NQ"] = [Xf[:, 0:512], Xf[:, 512:1024]]
        ST = Xf[:, 1024:2048].rearrange("p (w k m) -> p w k m", w=2, k=16)
        aS = self.adaS[:, :, :].rearrange("p a b -> p (a b)")
        gP = self.gp[:, :, :].rearrange("p a b -> p (a b)")
        cS = self.CS[:, :, :].rearrange("p a b -> p (a b)")
        bD = self.band[:, :, :].rearrange("p a b -> p (a b)").bitcast(F32)
        V2, PS = aS[:, 0:110], aS[:, 110:142]
        GN = aS[:, 142:154]
        c["GS"] = aS[:, 154:202].rearrange("p (i g) -> p i g", i=2)
        c["CN"] = aS[:, 202:218].rearrange("p (i g) -> p i g", i=2)
        LF = aS[:, 218:234].rearrange("p (i g) -> p i g", i=2)
        L1 = aS[:, 234:250].rearrange("p (i g) -> p i g", i=2)
        c["NCR"] = bD[:, 0:256]
        c["KC"] = bD[:, 256:320].rearrange("p (g n) -> p g n", g=2)
        c["VM"] = cS[:, 128:256].rearrange("p (g d) -> p g d", g=2)
        HID = cS[:, 0:128].rearrange("p (c m) -> p c m", c=2)
        OS = gP[:, 0:256]
        W2 = gP[:, 256:512].rearrange("p (w c d) -> p w c d", w=2, c=2)
        KCN = bD[:, 320:448].rearrange("p (u d) -> p u d", u=2)
        tri, one, selC = K[:, 128:256], K[:, 256:384], K[:, 384:448]
        caus, rmask = K[:, 448:704], K[:, 704:705]
        k2 = self.dma(self.sp, "k2", K[:, 128:705], i["konst2"], f0)
        rows, prow = Xf[:, 0:128], Xf[:, 128:256]
        vec = self.dma(self.sp, "vec2", rows[0:110, :], i["vecs2"][0:110], f0)
        pr = self.dma(self.sp, "pos", prow[0:32, :], i["vecs2"][110:142], f0)
        self.vc.update(norm_mix=0, norm_ffn=8, conv_w=16, conv_b=82)
        at = 110
        FB, SK = self.sink[:, 40:48], self.sink[:, 32:40]
        w2 = self.dma(self.sp, "cw2", W2, i["cmp_w2_2"][0].rearrange("w (c p) d -> p w c d", p=128), f0)
        st = []
        for h in range(16):
            src = bass.AP(self.ext.tensor, self.ext.offset + 128 * 384 * h + 127, [[383, 128], [1, 256]])
            st.append(self.dma(self.sp, "strip", c["strip"][:, h, :], src, f0, self.ext_rd))
        c["strip_rd"] = st
        b = yield from self.get(2)
        yield [vec, pr]
        mk = self.tr(b.t[:, 0:at], rows[0:at, :], self.ident[0:at, 0:at], vec, b.free)
        mk = self.tr(b.t[:, 128:160], prow[0:32, :], self.ident[0:32, 0:32], pr)
        v2 = self.cp(V2, b.t[:, 0:110], mk, f0)
        ps = self.cp(PS, b.t[:, 128:160], mk, f0)
        g1 = self.ts(GN[:, 0:6], b.t[:, 104:110], 0.125, None, ALU.mult, None, mk, f0)
        g1 = [g1, self.cp(GN[:, 6:12], b.t[:, 104:110], mk, f0)]
        self.give(b, v2, ps, g1)
        c["gn_rd"] = g1
        c["SK"], c["GN"] = SK, GN
        c["sk_rd"] = self.sink_rd
        c["pos"], c["pos_rd"] = PS, ps
        c.update(ST=ST, HID=HID, OS=OS, W2=W2, w2_rd=w2, KCN=KCN, tri=tri, one=one, selC=selC, caus=caus, rmask=rmask, k2=k2, LF=LF,
                 L1=L1, FB=FB, fb=self.sink_rd)
        self.V2 = V2
        self.v2_rd = v2
        fz = self.fence = self.now()
        hr = self.new_h()
        nt, xn = [None, None], F(0, 2, D)
        ts = [self.spawn(self.norm_tile(LAT, n, xn, nt, fz), 0.0) for n in range(2)]
        cols = (lambda kt: V2[:, self.vc["norm_mix"] + kt:self.vc["norm_mix"] + kt + 1], None, lambda: [v2], lambda: True)
        yield from self.make_h(hr, cols, LAT, xn, F(2048, 2, 2, 256), nt, fz)
        c["fz"] = [hr[LAT]] + self.now()
        self.fence = c["fz"]
        MG = self.G[:, :, :].rearrange("p a (b t) -> p (a b) t", t=256)
        c["MG"] = MG
        c.update(kd_rd=[None] * 3, q_rd=[None] * 12, ck_rd=[None] * 4, cv_rd=[None] * 2, mg_rd={}, hid=[])
        c["GF"] = self.G[:, :, :].rearrange("p a b -> p (a b)")
        self.br = [[None] * 4 for _ in range(3)]
        att = self.spawn(self.attention(self.units_2(c), at=11520, nsm=4, npt=3, wide=258, kts=2), 0.5)
        yield from self.proj_2(c)
        yield lambda: att.done
        yield from self.merge_2(c)
        yield from self.ffn(c)

    def nat_2(self, c0):
        job = yield from self.w.job(("p", c0))
        b, mk = yield from self.prod_b(job, 256, LAT)
        self.w.free(job, mk)
        return b, mk

    def heads_norm(self, c, src, n, *need):
        ss = self.cols(2 * n)
        _, free = yield from c["sq_s"].take()
        sq = self.F(13576, 512)[:, 0:2 * n * 64]
        sv = sq.rearrange("p (i n d) -> p (i n) d", i=2, d=64)
        yield [*need]
        t = self.a(sq.rearrange("p (i w) -> p i w", i=2), src, ACT.Square, *need, free, c["fz"])
        yield [t]
        t = self.red(ss, sv, ALU.add, t)
        c["sq_s"].give(0, t)
        rs, t = self.rstd(ss, 2 * n, 64, t)
        yield [t]
        return rs, t

    def q_2(self, c, c0, dst, gain, key, ks):
        b, mk = yield from self.nat_2(c0)
        self.spawn(self.q_tail(c, dst, gain, key, ks, b, mk), 0.0)

    def q_tail(self, c, dst, gain, key, ks, b, mk):
        x, free = yield from c["nq_s"].take()
        NQ = c["NQ"][x]
        yield [mk]
        t = self.a(NQ, b.t[:, :], ACT.Copy, mk, free, c["fz"])
        self.give(b, t)
        rs, tr = yield from self.heads_norm(c, NQ.rearrange("p (i w) -> p i w", i=2), 4, t)
        nv = NQ.rearrange("p (g d) -> p g d", d=64)
        tn = self.tt(nv, nv, rs.rearrange("p (g a) -> p g a", a=1).to_broadcast([128, 8, 64]), ALU.mult, tr, t)
        b = yield from self.get(1)
        yield [tn]
        for p in range(2):
            for i in range(2):
                mk = self.tr(b.t[:, 256 * p + 128 * i:256 * p + 128 * i + 128], NQ[:, 256 * i + 128 * p:256 * i + 128 * p + 128],
                             self.ident, tn, b.free)
        c["nq_s"].give(x, mk)
        yield [mk]
        t = self.a(dst, b.t[:, :].rearrange("p (a t) -> p a t", a=2), ACT.Copy, mk, c["fz"], c["gn_rd"], scale=c["GN"][:, gain:gain + 1])
        self.give(b, t)
        for k in ks:
            c[key][k] = t

    def kv_2(self, c, k, c0, gain):
        b, mk = yield from self.nat_2(c0)
        self.spawn(self.kv_tail(c, k, gain, b, mk), 0.0)

    def kv_tail(self, c, k, gain, b, mk):
        kd, vn = c["KD"][:, k], c["VN"][:, k]
        x, free = yield from c["nq_s"].take()
        NQ = c["NQ"][x]
        b3 = b.t[:, :].rearrange("p (i w) -> p i w", i=2)
        kn = NQ[:, 0:256].rearrange("p (i w) -> p i w", i=2)
        yield [mk]
        t = self.a(kn, b3[:, :, 0:128], ACT.Copy, mk, free, c["fz"])
        t2 = self.a(vn, b3[:, :, 128:256], ACT.Copy, mk, c["fz"])
        self.give(b, t, t2)
        rs, tr = yield from self.heads_norm(c, kn, 2, t)
        _, free = yield from c["kw_s"].take()
        tn = []
        kw = c["GF"][:, 0:512]
        for u in range(2):
            o = kw.rearrange("p (g u d) -> p g u d", u=2, d=64)[:, :, u, :]
            tn.append(self.tt(o, NQ[:, 0:256].rearrange("p (g d) -> p g d", d=64),
                              rs.rearrange("p (g a) -> p g a", a=1).to_broadcast([128, 4, 64]), ALU.mult, tr, t, free, c["fz"]))
        c["nq_s"].give(x, tn)
        b = yield from self.get(1)
        yield tn
        for g in range(2):
            for i in range(2):
                mk = self.tr(b.t[:, 256 * g + 128 * i:256 * g + 128 * i + 128], kw[:, 256 * i + 128 * g:256 * i + 128 * g + 128],
                             self.ident, tn, b.free)
        c["kw_s"].give(0, mk)
        yield [mk]
        t = self.a(kd, b.t[:, :].rearrange("p (a t) -> p a t", a=2), ACT.Copy, mk, c["fz"], c["gn_rd"], scale=c["GN"][:, gain:gain + 1])
        self.give(b, t)
        c["kd_rd"][k] = [t, t2]

    def small_2(self, c):
        job = yield from self.w.job(("small",))
        b = yield from self.get(4)
        mk = yield from self.form_a(job, 0, 32, b.t[0:32, 0:256], 256, 256, self.Hh, self.Hl, self.hrd(1, 2), b.free)
        self.w.free(job, mk)
        self.spawn(self.small_tail(c, b, mk), 0.0)

    def small_tail(self, c, b, mk):
        R = c["GF"][0:32, 512:768]
        yield [mk]
        t = self.a(R, b.t[0:32, 0:256], ACT.Copy, mk, c["fz"])
        self.give(b, t)
        b = yield from self.get(1)
        yield [t]
        for i in range(2):
            mk = self.tr(b.t[:, 32 * i:32 * i + 32], R[:, 128 * i:128 * i + 128], self.ident[0:32, 0:32], t, b.free)
        c["r_free"] = [mk]
        yield [mk]
        bv = b.t[:, 0:64].rearrange("p (i g) -> p i g", i=2)
        GS, LF, L1, CN, NCR = c["GS"], c["LF"], c["L1"], c["CN"], c["NCR"]
        t = self.a(GS, bv[:, :, 0:24], ACT.Tanh, mk, c["fz"], scale=0.5)
        yield [t]
        t1 = self.tt(LF, bv[:, :, 24:32], c["FB"].rearrange("p (a g) -> p a g", a=1).to_broadcast([128, 2, 8]), ALU.add, mk, c["fb"], t, c["fz"])
        self.give(b, t1)
        t = self.ts(GS, GS, 1.0, 0.5, ALU.add, ALU.mult, t)
        g0 = GS[:, 0, 0::3]
        c["gs_rd"] = self.ts(g0, g0, c["rmask"], None, ALU.mult, None, t, c["k2"])
        t = self.stt(L1, LF, -1.0, LF, ALU.mult, ALU.min, t1)
        yield [t]
        t = self.a(L1, L1, ACT.Exp, t)
        t = self.a(L1, L1, ACT.Ln, t, bias=1.0)
        yield [t]
        t = self.stt(LF, LF, 0.0, L1, ALU.min, ALU.subtract, t)
        b = yield from self.get(1)
        yield [t]
        tri, one = c["tri"], c["one"]
        cn, cr = b.t[:, 0:16].rearrange("p (i g) -> p i g", i=2), b.t[0:8, 128:384]
        self.mm(cn[:, 0], tri, LF[:, 0], True, True, t, c["k2"], b.free)
        self.mm(cn[:, 1], one, LF[:, 0], True, False)
        self.mm(cn[:, 1], tri, LF[:, 1], False, True)
        self.mm(cr[:, 0:128], LF[:, 0], tri, True, True)
        self.mm(cr[:, 128:256], LF[:, 0], one, True, False)
        mk = self.mm(cr[:, 128:256], LF[:, 1], tri, False, True, inc=True)
        yield [mk]
        t = self.cp(CN, cn, mk, c["fz"])
        t2 = self.ts(NCR[0:8, :], cr, -1.0, None, ALU.mult, None, mk, c["fz"])
        self.give(b, t, t2)
        c["cn_rd"] = [t, t2]

    def cmp_2(self, c):
        b, mk = yield from self.nat_2(512)
        x, free = yield from c["nq_s"].take()
        NQ = c["NQ"][x]
        st = []
        mine = {"st": None}

        def stage(b, mk):
            yield [mk]
            t = self.a(NQ, b.t[:, :], ACT.Copy, mk, free, c["fz"])
            self.give(b, t)
            b = yield from self.get(1)
            yield [t]
            for w in range(2):
                for i in range(2):
                    mk = self.tr(b.t[:, 256 * w + 128 * i:256 * w + 128 * i + 128], NQ[:, 256 * i + 128 * w:256 * i + 128 * w + 128],
                                 self.ident, t, b.free)
            c["nq_s"].give(x, mk)
            yield [mk]
            ST = c["ST"]
            st.append(self.mset(ST[:, :, :, 31:32], 0.0, c["fz"]))
            for w in range(2):
                for g in range(2):
                    for e in range(2):
                        src = b.t[64 * g:64 * g + 64, 256 * w:256 * w + 256]
                        src = bass.AP(src.tensor, src.offset + e, [src.ap[0], [2, 16], [16, 15]])
                        st.append(self.cp(ST[64 * e:64 * e + 64, w, :, 15 * g:15 * g + 15], src, mk, c["fz"]))
                st.append(self.cp(ST[:, w, :, 30:31], c["pos"][:, 16 * w:16 * w + 16].rearrange("p (k a) -> p k a", a=1), c["pos_rd"], c["fz"]))
            self.give(b, st)
            mine["st"] = True
        self.spawn(stage(b, mk), 0.0)
        return mine, st

    def hid_2(self, c, mine, st, w):
        yield lambda: mine["st"] is not None
        b = yield from self.get(4)
        for h in range(2):
            job = yield from self.w.job(("w1", w, h))
            yield [st]
            for k in range(8):
                q = k % 4
                mk = self.mm(b.t[32 * q:32 * q + 32, 0:256], c["ST"][:, w, 8 * h + k, :], job.raw[:, k, :], h == 0 and k < 4,
                             h == 1 and k >= 4, job.load, st, b.free, inc=k == 7, cost=128.0)
            self.w.free(job, mk)
        c["hid"].append(self.spawn(self.hid_tail(c, w, b, mk, c["hid"][-1] if c["hid"] else None), 0.0))

    def hid_tail(self, c, w, b, mk, prev):
        HID, OS, KCN = c["HID"], c["OS"], c["KCN"]
        yield lambda: prev is None or prev.done
        yield [mk]
        t = self.a(OS, b.t[:, 0:256], ACT.Copy, mk, c.get("os_free"), c["fz"])
        self.give(b, t)
        b = yield from self.get(1)
        yield [t]
        for q in range(2):
            mk = self.mm(b.t[:, 64 * q:64 * q + 64], OS[:, 128 * q:128 * q + 128], c["selC"], True, True, t, c["k2"], b.free, inc=True)
        c["os_free"] = [mk]
        yield [mk]
        t = self.a(HID, b.t[:, 0:128].rearrange("p (c m) -> p c m", c=2), ACT.Gelu_apprx_tanh, mk, c.get("hid_free"), c["fz"])
        self.give(b, t)
        b = yield from self.get(1)
        yield [t]
        for g in range(2):
            for q in range(2):
                mk = self.mm(b.t[0:32, 64 * g:64 * g + 64], HID[:, q, 32 * g:32 * g + 32], c["W2"][:, w, q, :], q == 0, q == 1,
                             t, c["w2_rd"], b.free, inc=True)
        c["hid_free"] = [mk]
        yield [mk]
        bv = b.t[0:32, 0:128].rearrange("p (g d) -> p g d", g=2)
        if w == 1:
            t = self.cp(c["VM"][0:32], bv, mk, c["fz"])
            self.give(b, t)
            c["vm_rd"] = t
            return
        kn = OS[0:32, 0:128].rearrange("p (g d) -> p g d", g=2)
        t = self.cp(kn, bv, mk, c["os_free"])
        self.give(b, t)
        _, free = yield from c["sq_s"].take()
        sq = self.F(13576, 128)[0:32, :].rearrange("p (g d) -> p g d", g=2)
        yield [t]
        t1 = self.a(sq, kn, ACT.Square, t, free, c["fz"])
        yield [t1]
        ss = self.cols(2)[0:32, :]
        t1 = self.red(ss, sq, ALU.add, t1)
        c["sq_s"].give(0, t1)
        t1 = self.ts(ss, ss, 1.0 / 64, EPS, ALU.mult, ALU.add, t1)
        t1 = self.tt(ss, ss, self.mhalf[0:32, 0:2], ALU.pow, t1, self.mhalf_rd, q=self.pool)
        b = yield from self.get(1)
        mks = []
        for g in range(2):
            yield [t1, mks]
            tn = [self.ts(KCN[0:32, u, :], kn[:, g], ss[:, g:g + 1], None, ALU.mult, None, t1, t, mks, c["fz"]) for u in range(2)]
            yield tn
            mks = self.tr(b.t[:, 32 * g:32 * g + 32], KCN[0:32, :, :].rearrange("p u d -> p (u d)"), self.ident[0:32, 0:32], tn, b.free)
        c["os_free"] = [mks]
        yield [mks]
        c["kc_rd"] = self.a(c["KC"], b.t[:, 0:64].rearrange("p (g n) -> p g n", g=2), ACT.Copy, mks, c["gn_rd"], c["fz"],
                            scale=c["GN"][:, 7:8])
        self.give(b, c["kc_rd"])

    def proj_2(self, c):
        Q, CK, CV = c["Q"], c["CK"], c["CV"]
        yield from self.kv_2(c, 0, 768, 7)
        yield from self.kv_2(c, 1, 1024, 7)
        yield from self.small_2(c)
        mine, st = yield from self.cmp_2(c)
        yield from self.hid_2(c, mine, st, 0)
        yield from self.hid_2(c, mine, st, 1)
        for h in range(2):
            yield from self.q_2(c, 256 * h, Q[:, 2 * h:2 * h + 2, :], 0, "q_rd", (2 * h, 2 * h + 1))
        yield from self.kv_2(c, 2, 1816, 9)
        for h in range(2):
            yield from self.q_2(c, 1304 + 256 * h, Q[:, 4 + 2 * h:6 + 2 * h, :], 2, "q_rd", (4 + 2 * h, 5 + 2 * h))

        def cv_tail(h, b, mk):
            yield [mk]
            c["cv_rd"][h] = t = self.a(CV[:, h], b.t[:, :].rearrange("p (i w) -> p i w", i=2), ACT.Copy, mk, c["fz"])
            self.give(b, t)
        for h in range(2):
            yield from self.q_2(c, 2072 + 256 * h, Q[:, 8 + 2 * h:10 + 2 * h, :], 4, "q_rd", (8 + 2 * h, 9 + 2 * h))
            yield from self.q_2(c, 2584 + 256 * h, CK[:, 2 * h:2 * h + 2, :], 11, "ck_rd", (2 * h, 2 * h + 1))
            b, mk = yield from self.nat_2(3096 + 256 * h)
            self.spawn(cv_tail(h, b, mk), 0.0)

        def mg_tail(k, d, n, b, mk):
            yield [mk]
            yield lambda: known(c["kd_rd"]) and "r_free" in c
            t = self.a(c["MG"][:, 2 * k:2 * k + 2, :], b.t[:, :].rearrange("p (a t) -> p a t", a=2), ACT.Tanh, mk, c["fz"],
                       c["kw_s"].free[0][1], c["r_free"], scale=0.5)
            self.give(b, t)
            c["mg_rd"][d, n] = (c["MG"][:, 2 * k:2 * k + 2, :], t)
        for k, (d, n) in enumerate(((0, 0), (0, 1), (0, 2), (1, 0))):
            b, mk = yield from self.merge_gate(d, n)
            self.spawn(mg_tail(k, d, n, b, mk), 0.0)
        yield lambda: len(c["mg_rd"]) == 4

    def merge_gate(self, d, n):
        job = yield from self.w.job(("merge", d, n))
        b = yield from self.get(4)
        for f in range(2):
            mk = yield from self.form_a(job, 128 * f, 128, b.t[:, 256 * f:256 * f + 256], 256, 256, self.Hh, self.Hl,
                                        self.hrd(1, 2), b.free)
        self.w.free(job, mk)
        return b, mk

    def units_2(self, c):
        Q, KD, CK, VN, CV, strip, GS = (c[k] for k in ("Q", "KD", "CK", "VN", "CV", "strip", "GS"))
        Gh = self.Gh[:, :, :].rearrange("p a b -> p (a b)")
        Gl = self.Gl[:, :, :].rearrange("p a b -> p (a b)")
        c["Bh"] = Gh[:, 0:3072].rearrange("p (n t) -> p n t", n=12)
        c["Bl"] = Gl[:, 0:3072].rearrange("p (n t) -> p n t", n=12)
        gfs = self.F(12552 + 768, 256)
        for br, name in enumerate("abc"):
            for t in range(4):
                box = {}
                kinds = ("cmp", "slc", "win") if br == 0 else (("swa",) if br == 1 else ("fox",))
                for i in range(2):
                    for kind in kinds:
                        for e in range(2):
                            g, h = t // 2, 2 * t + e
                            if kind == "cmp":
                                nk = 7 if i == 0 else 15
                            else:
                                nk = 128 * (i + 1)
                            r = slice(64 * e, 64 * e + 64)

                            def need(kind=kind, t=t, br=br):
                                k = {"slc": 0, "win": 1, "swa": 2}
                                return [c["q_rd"][4 * br + t], c.get("kc_rd") if kind == "cmp" else [c["ck_rd"][t], c.get("cn_rd")]
                                        if kind == "fox" else c["kd_rd"][k[kind]]]

                            def ready(need=need):
                                return known(need()) and "cn_rd" in c

                            def vready(kind=kind, t=t):
                                return known([c.get("vm_rd") if kind == "cmp" else c["cv_rd"][t // 2] if kind == "fox" else 0])

                            def scores(b, kind=kind, i=i, g=g, h=h, t=t, r=r, nk=nk, br=br):
                                q = Q[r, 4 * br + t, 128 * i:128 * i + 128]
                                need = [c["q_rd"][4 * br + t], b.free]
                                if kind == "cmp":
                                    return self.mm(b.t[:, 0:nk], q, c["KC"][r, g, 0:nk], True, True, need, c["kc_rd"], inc=True)
                                if kind == "fox":
                                    self.mm(b.t[:, 0:nk], q, CK[r, t, 0:nk], True, False, need, c["ck_rd"][t])
                                    return self.mm(b.t[:, 0:nk], self.ident[0:8, h:h + 1].to_broadcast([8, 128]), c["NCR"][0:8, 0:nk],
                                                   False, True, c["cn_rd"], inc=True)
                                k = {"slc": 0, "win": 1, "swa": 2}[kind]
                                return self.mm(b.t[:, 0:nk], q, KD[r, k, g, 0:nk], True, True, need, c["kd_rd"][k], inc=True)

                            def values(ob, pts, marks, kind=kind, kinds=kinds, i=i, g=g, t=t, br=br, nk=nk):
                                first, final = kind == kinds[0], kind == kinds[-1]
                                nt = max(1, nk // 128)
                                for k in range(nt):
                                    for e2 in range(2):
                                        if kind == "cmp":
                                            v, rd = c["VM"][0:nk, g, :], c["vm_rd"]
                                        elif kind == "fox":
                                            v, rd = CV[:, t // 2, k, 128 * (t % 2) + 64 * e2:128 * (t % 2) + 64 * e2 + 64], c["cv_rd"][t // 2]
                                        else:
                                            kk = {"slc": 0, "win": 1, "swa": 2}[kind]
                                            v, rd = VN[:, kk, k, 64 * g:64 * g + 64], c["kd_rd"][kk]
                                        mk = self.mm(ob.t[64 * e2:64 * e2 + 64, 128 * i:128 * i + 128], v, pts[e2][:, k, :],
                                                     first and k == 0, final and k == nt - 1, marks[e2], rd, ob.free, inc=k == nt - 1)
                                return mk

                            def gate(ob, mk, t=t, br=br):
                                n = 4 * br + t
                                x, free = yield from c["gf_s"].take()
                                yield [mk]
                                d = self.a(gfs, ob.t[:, 0:256], ACT.Copy, mk, free, c["fz"])
                                self.give(ob, d)
                                yield [d]
                                d2 = yield from self.split(c["Bh"][:, n, :], c["Bl"][:, n, :], gfs, d, self.g_free)
                                c["gf_s"].give(x, d2)
                                self.br[br][t] = d2

                            shift, gc = None, None
                            if kind == "fox":
                                mask = c["caus"][:, 128 - 128 * i:256]
                                shift = c["CN"][:, i, h:h + 1]
                            elif kind == "cmp":
                                mask = strip[:, h, 159::16] if i == 0 else strip[:, h, 31::16]
                            else:
                                mask = strip[:, 8 * br + h, 128 - 128 * i:256]
                            if br == 0:
                                gc = GS[:, i, 3 * h + kinds.index(kind):3 * h + kinds.index(kind) + 1]
                            sink = c["SK"][:, h:h + 1] if br == 1 else None
                            yield dict(ready=ready, need=need, scores=scores, values=values, nk=nk, pair=e, mask=mask, box=box,
                                       first=i == 0 and kind == kinds[0], vready=vready,
                                       gate=gate if i == 1 and kind == kinds[-1] else None,
                                       mask_rd=lambda: [c["strip_rd"], c["sk_rd"], c["k2"], c["cn_rd"]], gate_rd=lambda: c["gs_rd"],
                                       gate_known=lambda: "gs_rd" in c, shift=shift, sink=sink, gate_col=gc)

    def merge_2(self, c):
        fz = self.now()
        MTh, MTl = self.Rr(0, 8, 256), self.Rr(2048, 8, 256)
        ACC, TMP, TH = self.F(4096, 2, 512), self.F(5120, 2, 512), self.F(6144, 2, 512)
        acc_s, tmp_s, th_s = Slots(2), Slots(2), Slots(2)
        mt = [None] * 8
        state = {}

        def th_tail(d, n, b, mk):
            x, free = yield from th_s.take()
            yield [mk]
            th = TH[:, x].rearrange("p (a t) -> p a t", a=2)
            t = self.a(th, b.t[:, :].rearrange("p (a t) -> p a t", a=2), ACT.Tanh, mk, free, fz, scale=0.5)
            self.give(b, t)
            c["mg_rd"][d, n] = (th, t, x)

        def branch_tail(d, n, b, mk, prev):
            yield lambda: (d, n) in c["mg_rd"] and (prev is None or prev.done)
            th, tr, *x = c["mg_rd"][d, n]
            if n == 0:
                state[d] = yield from acc_s.take()
            at, free = state[d]
            acc = ACC[:, at].rearrange("p (a t) -> p a t", a=2)
            bv = b.t[:, :].rearrange("p (a t) -> p a t", a=2)
            yield [tr, mk]
            if n == 0:
                t = ta = self.stt(acc, th, 1.0, bv, ALU.add, ALU.mult, tr, mk, free, fz)
                self.give(b, t)
            else:
                y, free = yield from tmp_s.take()
                tmp = TMP[:, y].rearrange("p (a t) -> p a t", a=2)
                t = self.stt(tmp, th, 1.0, bv, ALU.add, ALU.mult, tr, mk, free, fz)
                self.give(b, t)
                ta = self.tt(acc, acc, tmp, ALU.add, t, state[d, "t"])
                tmp_s.give(y, ta)
            if x:
                th_s.give(x[0], t)
            state[d, "t"] = ta
            if n == 2:
                o = slice(2 * d, 2 * d + 2)
                yield [ta]
                t = self.a(MTh[:, o, :], acc, ACT.Copy, ta, fz, scale=0.5)
                yield [t]
                t = self.stt(MTl[:, o, :], acc, 0.5, MTh[:, o, :], ALU.mult, ALU.subtract, t, ta, fz)
                acc_s.give(at, t)
                mt[2 * d] = mt[2 * d + 1] = t
        prev = None
        for d in range(4):
            for n in range(3):
                if (d, n) not in c["mg_rd"]:
                    b, mk = yield from self.merge_gate(d, n)
                    self.spawn(th_tail(d, n, b, mk), 0.0)
                job = yield from self.w.job(("branch", d, n))
                b = yield from self.get(4)
                Bh, Bl = c["Bh"][:, 4 * n:4 * n + 4, :], c["Bl"][:, 4 * n:4 * n + 4, :]
                for f in range(2):
                    mk = yield from self.form_a(job, 128 * f, 128, b.t[:, 256 * f:256 * f + 256], 0, 256, Bh, Bl,
                                                lambda k, n=n: [self.br[n][k]], b.free)
                self.w.free(job, mk)
                prev = self.spawn(branch_tail(d, n, b, mk, prev), 0.0)
        self.h_free = [mk]

        def out_tail(j, b, mk):
            yield [mk]
            xs = self.X[:, 2:4, 256 * j:256 * j + 256]
            t = self.tt(xs, xs, b.t[:, :].rearrange("p (i c) -> p i c", i=2), ALU.add, mk, self.xr[2], self.xr[3])
            self.give(b, t)
        ts = []
        for j in range(4):
            job = yield from self.w.job(("out2", j))
            b = yield from self.get(4)
            for i in range(2):
                mk = yield from self.form_b(job, 0, 256, b.t[:, 256 * i:256 * i + 256], 128 * i, MTh, MTl, lambda k: [mt[k]], b.free)
            self.w.free(job, mk)
            ts.append(self.spawn(out_tail(j, b, mk), 0.0))
        yield lambda: all(t.done for t in ts)
        self.xr[2] = self.xr[3] = (self.dve.name, self.dve.count)

    def ffn(self, c):
        f0 = self.fence = self.now()
        vc, V2 = self.vc, self.V2
        hr = self.new_h()
        nt, xn = [None, None], self.F(4096, 2, D)
        for n in range(2):
            self.spawn(self.norm_tile(LAT, n, xn, nt, f0), 0.0)
        cols = (lambda kt: V2[:, vc["norm_ffn"] + kt:vc["norm_ffn"] + kt + 1], None, lambda: [self.v2_rd], lambda: True)
        yield from self.make_h(hr, cols, LAT, xn, self.F(6144, 2, 2, 256), nt, f0)
        FTh, FTl = self.Rr(0, 3, 2, 256), self.Rr(1536, 3, 2, 256)
        fz = [hr[LAT], self.now()]
        Yv = self.F(4096, 2, 2, 256)
        y_s, ft_s, ft = Slots(2), Slots(3), {}
        acc = []
        for _ in range(4):
            acc.append((yield from self.get(1)))
        V = lambda name, k: V2[:, vc[name] + k:vc[name] + k + 1]
        st = {}

        def gate_tail(k, b, mk):
            x, free = yield from y_s.take()
            Y = Yv[:, x]
            yield [mk]
            ts = []
            for f in range(2):
                m = 2 * k + f
                p = b.t[:, 256 * f:256 * f + 256]
                ts.append(self.a(Y[:, f, :], p, ACT.Identity, mk, free, fz, scale=V("conv_w", 44 + m), bias=V("conv_b", m)))
            tl = []
            yield ts
            for f in range(2):
                m = 2 * k + f
                p = b.t[:, 256 * f:256 * f + 256]
                t1 = self.stt(Y[:, f, 1:256], p[:, 0:255], V("conv_w", 22 + m), Y[:, f, 1:256], ALU.mult, ALU.add, ts)
                tl.append(self.stt(Y[:, f, 2:256], p[:, 0:254], V("conv_w", m), Y[:, f, 2:256], ALU.mult, ALU.add, t1))
            self.give(b, tl)
            yield tl
            st[k] = (x, self.a(Y, Y, ACT.Gelu_apprx_tanh, tl))

        def up_tail(k, b, mk):
            yield lambda: k in st
            x, tg = st[k]
            Y = Yv[:, x]
            yield [tg, mk]
            t = self.tt(Y, Y, b.t[:, :].rearrange("p (f t) -> p f t", f=2), ALU.mult, tg, mk)
            self.give(b, t)
            z, free = yield from ft_s.take()
            yield [t]
            t = yield from self.split(FTh[:, z], FTl[:, z], Y, t, free, fz)
            ft[k] = (z, t)
            y_s.give(x, t)
        for k in range(12):
            if k < 11:
                for key, tail in (("gate", gate_tail), ("up", up_tail)):
                    job = yield from self.w.job((key, k))
                    b = yield from self.get(1)
                    for f in range(2):
                        mk = yield from self.form_a(job, 128 * f, 128, b.t[:, 256 * f:256 * f + 256], 256, 256, self.Hh, self.Hl,
                                                    self.hrd(1, 2), b.free)
                    self.w.free(job, mk)
                    self.spawn(tail(k, b, mk), 0.0)
            if k > 0:
                q = k - 1
                job = yield from self.w.job(("down", q))
                yield lambda: q in ft and known(job.rdy)
                z, tf = ft[q]
                for i in range(2):
                    for hf in range(2):
                        yield [tf, job.rdy]
                        a = acc[2 * i + hf]
                        for f in range(2):
                            fh, fl = FTh[:, z, f, 128 * i:128 * i + 128], FTl[:, z, f, 128 * i:128 * i + 128]
                            wh, wl = job.hi[:, f, 512 * hf:512 * hf + 512], job.lo[:, f, 512 * hf:512 * hf + 512]
                            last = q == 10 and f == 1
                            self.mm(a.t[:, :], fh, wh, q == 0 and f == 0, False, tf, job.rdy[f], a.free)
                            self.mm(a.t[:, :], fh, wl, False, False)
                            mk = self.mm(a.t[:, :], fl, wh, False, last, inc=True)
                        if q == 10:
                            xs = self.X[:, 2 + i, 512 * hf:512 * hf + 512]
                            t = self.tt(xs, xs, a.t[:, :], ALU.add, mk, self.xr[2 + i])
                            self.dma(self.sp, "out", self.out[self.o0 + i][:, 512 * hf:512 * hf + 512], xs, t)
                self.w.free(job, mk)
                ft_s.give(z, mk)

    def main(self):
        begun = self.start()
        hr = self.new_h()
        nt = {s: [None, None] for s in (CT, LAT)}
        xn = self.F(9728, 2, D)
        for i in range(2):
            self.spawn(self.norm_tile(CT, i, xn, nt[CT], []), 0.0)
        made = self.spawn(self.make_h(hr, self.h_cols(0, CT), CT, xn, self.F(11776, 2, 2, 256), nt[CT]), 0.0)
        for n in range(8):
            yield from self.ada_step(0, n // 4, n % 4)
        yield lambda: made.done and all(t.done for t in begun)
        fz = self.fence = self.now()
        self.spawn(self.w.prepare(), 1.0)

        def turn():
            xn = self.F(11264, 2, D)
            for i in range(2):
                self.spawn(self.norm_tile(LAT, i, xn, nt[LAT], fz), 0.0)
            yield from self.make_h(hr, self.h_cols(0, LAT), LAT, xn, self.F(13312, 2, 2, 256), nt[LAT], fz)
        self.turn = self.spawn(turn(), 0.0)
        for l in range(min(self.upto, 3) + 1):
            streams = [CT, LAT] if l < 3 else [LAT]
            yield from (self.layer_a, self.layer_b, self.layer_c, self.layer_a)[l](*((l, streams) if l % 3 == 0 else (l,)))
            yield lambda: self.ada_left == 0
            nxt = (lambda s, l=l: self.h_cols(l + 1, s)) if l < 3 and self.upto > l else None
            yield from self.finish_layer(l, streams, nxt)
            if nxt is None:
                yield lambda: self.turn.done
            self.fence = self.now()
            if l == 0:
                self.fence += [self.ext_rd]
        if self.upto > 3:
            yield from self.second()
        else:
            for t in range(4):
                self.dma(self.sp, "out", self.out[t], self.X[:, t, :], self.xr[t])

    def build(self):
        self.go(self.spawn(self.main(), 2.0))
        self.sp.wait(("dma_out", 64), self.ext_rd)

    def emit(self, ctx):
        nc = self.nc
        names = ["pe", "act", "dve", "pool", "sp"] + sorted(self.dma_count)
        sems = {n: ctx.enter_context(nc.semaphore("s_" + n)) for n in names}
        blk = ctx.enter_context(nc.Block())

        @blk.tensor
        def _(e):
            self.pe.play(e, sems)

        @blk.scalar
        def _(e):
            self.act.play(e, sems)

        @blk.vector
        def _(e):
            self.dve.play(e, sems)

        @blk.gpsimd
        def _(e):
            self.pool.play(e, sems)

        @blk.sync
        def _(e):
            self.sp.play(e, sems)


def packed(ins):
    a = {k: np.asarray(v) for k, v in ins.items()}
    r = lambda x: x.reshape(-1, 128)
    first = [r(a[f"l{l}_g_pre"]) for l in range(4)] + [r(a[n]) for n in ("l1_g_qa", "l1_g_kva", "l2_g_head", "l2_conv")]
    pad = [np.zeros((104 - sum(len(x) for x in first), 128), np.float32)]
    bias = [r(a[f"l{l}_b_ada"][0:2048]) for l in range(4)]
    gains = np.concatenate([a["qk_gain_2"][0]] * 2, axis=1)
    second = [r(a[n]) for n in ("norm_mix_2", "norm_ffn_2", "conv_w_2", "conv_b_2")] + [gains, r(a["cmp_pos_2"])]
    return {
        "weights": np.concatenate([j.pack(a) for j in plan()]),
        "cond": np.concatenate([r(a["c_ctx"]), r(a["c"])]),
        "vecs": np.concatenate(first + pad + bias),
        "vecs2": np.concatenate(second),
        "rows": np.concatenate([a["l0_sink"], a["l3_sink"], a["sinks_2"][0], a["forget_bias_2"][0]])[None],
        **{n: a[n] for n in ("x", "ctx", "l2_b_gate", "rel_bias_2", "cmp_w2_2")},
        **{f"l{l}_{n}": a[f"l{l}_{n}"] for l in range(4) for n in ("g_post", "b_ada")},
    }


def konst():
    f = np.float32
    K = np.zeros((128, 896), f)
    K[:, 0:128] = np.eye(128, dtype=f)
    for s in range(2):
        K[s::32, 128 + 128 * s:256 + 128 * s] = 1.0
    tok = np.arange(256)
    r, c = (tok // 64).astype(f), (tok % 64).astype(f)
    inv = (f(10000.0) ** (-np.arange(16, dtype=f) / f(16))).astype(f)
    ang = np.concatenate([r[:, None] * inv, c[:, None] * inv], axis=-1).astype(f)
    p = np.arange(128)
    a = ang[:, (p % 64) // 2].T
    K[:, 384:640] = np.cos(a)
    K[:, 640:896] = np.sin(a) * np.where(p % 2 == 0, -1.0, 1.0)[:, None]
    band = np.zeros((128, 2, 512), f)
    q = np.arange(128)
    for i in range(2):
        kk = np.arange(256)
        bad = np.abs(128 * i + q[:, None] - kk[None, :]) > 128
        band[:, i, 256:512] = np.where(bad, f(NEG), f(0))
    a = np.arange(128)
    ml = np.zeros((128, 2, 128), f)
    ml[:, 0] = np.where(a[:, None] <= a[None, :], f(0), f(NEG))
    ml[:, 1] = np.where(a[:, None] >= a[None, :], f(0), f(NEG))
    K2 = np.zeros((128, 577), f)
    K2[:, 0:128] = a[:, None] <= a[None, :]
    K2[:, 128:256] = 1.0
    for g in range(2):
        for n in range(15):
            K2[15 * g + n::32, 256 + 32 * g + n] = 1.0
            K2[30::32, 256 + 32 * g + n] = 1.0
    jj = np.arange(256)
    K2[:, 320:576] = np.where(128 + a[:, None] - jj[None, :] >= 0, f(0), f(NEG))
    K2[:, 576] = a >= 31
    m = np.arange(384)
    dist = 255 - m
    dd = np.maximum(dist, 0)
    ratio = np.log(np.maximum(dd, 1).astype(f) / f(16)) / f(np.log(8.0))
    large = np.minimum(16 + (ratio * f(16)).astype(np.int32), 31)
    bucket = np.where(dd < 16, dd, large)
    oh = np.zeros((34, 384), f)
    ok = dist >= 0
    oh[bucket[ok], m[ok]] = 1.0
    oh[32] = np.where(ok, f(0), f(NEG))
    oh[33] = np.where(dist >= 128, f(NEG), f(0))
    tr = np.zeros((2, 16), f)
    tr[0] = 1.0
    tr[1, 8:] = 1.0
    return {"konst2": K2, "onehot": oh, "tabrows": tr, "mlmask": ml.reshape(128, 256), "konst": K, "band": band.reshape(128, 1024)}


def ctx_stack_two_blocks_kernel(nc, ins, out):
    with ExitStack() as ctx:
        net = Net(nc, ctx, ins, out.rearrange("a (t p) d -> (a t) p d", p=128), 4)
        net.build()
        net.emit(ctx)


def kernel(**inputs):
    import numpy as _np
    import concourse.bacc as _bacc
    from concourse import mybir as _mybir
    from concourse.bass_utils import run_bass_kernel_spmd as _run

    nc = _bacc.Bacc("TRN2", target_bir_lowering=False, num_devices=1)
    arrays, args = {}, {}
    for name, a in {**packed(inputs), **konst()}.items():
        a = _np.ascontiguousarray(a)
        arrays[f"in_{name}_dram"] = a
        args[name] = nc.dram_tensor(f"in_{name}_dram", a.shape, _mybir.dt.from_np(a.dtype), kind="ExternalInput").ap()
    out = nc.dram_tensor("out_0_dram", (1, 256, 1024), _mybir.dt.float32, kind="ExternalOutput").ap()
    ctx_stack_two_blocks_kernel(nc, args, out)
    r = _run(nc, [arrays], core_ids=[0])
    return r.results[0]["out_0_dram"]
```

```python
from contextlib import ExitStack

import numpy as np

import concourse.bass as bass
from concourse import mybir

F32 = mybir.dt.float32
R32 = mybir.dt.float32r
BF16 = mybir.dt.bfloat16
ACT = mybir.ActivationFunctionType
ALU = mybir.AluOpType
AX = mybir.AxisListType

NEG = -1.0e30
FLOOR = -3.0e38
EPS = 1e-6
D = 1024


def flat(need):
    out = []
    for n in need:
        if n is None:
            continue
        if isinstance(n, list):
            out += flat(n)
        else:
            out.append(n)
    return out


def known(need):
    return all(known(n) if isinstance(n, list) else n is not None for n in need)


def width(ap):
    return int(np.prod([n for _, n in list(ap.ap)[1:]]))


class Queue:

    def __init__(self, core, name):
        self.core, self.name, self.items, self.count, self.seen, self.t = core, name, [], 0, {}, 0.0

    def wait(self, *need):
        top = {}
        for sem, val in flat(need):
            top[sem] = max(top.get(sem, 0), val)
        for sem, val in top.items():
            if self.seen.get(sem, 0) < val:
                self.items.append((None, sem, val))
                self.seen[sem] = val
                self.t = max(self.t, self.core.when.get((sem, val), 0.0))

    def do(self, fn, *need, inc=True, cost=100.0):
        self.wait(*need)
        self.t += cost
        if inc:
            self.count += 1
            self.items.append((fn, self.name, 1))
            mark = (self.name, self.count)
            self.core.when[mark] = self.t + self.core.LATENCY[self.name]
            return mark
        self.items.append((fn, None, 0))
        return None

    def play(self, e, sems):
        for fn, sem, val in self.items:
            if fn is None:
                e.wait_ge(sems[sem], val)
            elif sem is None:
                fn(e)
            else:
                fn(e).then_inc(sems[sem], val)


class Bank:

    def __init__(self, t):
        self.t, self.free = t, []


class Slots:

    def __init__(self, n):
        self.free = [(i, []) for i in range(n)]

    def take(self):
        yield lambda: bool(self.free)
        i, marks = self.free.pop(0)
        yield marks
        return i, marks

    def give(self, i, *marks):
        self.free.append((i, flat(marks)))


class Task:
    def __init__(self, gen, prio, seq):
        self.gen, self.prio, self.seq, self.want, self.at = gen, prio, seq, None, 0.0
        self.done = False


class Core:

    SLACK = 0.0
    COLD = 20000.0
    LATENCY = {"pe": 197.0, "act": 190.0, "dve": 170.0, "pool": 155.0}

    def __init__(self):
        self.when = {}
        self.pe, self.act, self.dve, self.pool, self.sp = (Queue(self, n) for n in ("pe", "act", "dve", "pool", "sp"))
        self.dma_count = {}
        self.banks = []
        self.tasks = []
        self.seq = 0
        self.clock = 0.0
        self.hw_t = self.dma_t = 0.0

    def spawn(self, gen, prio):
        self.seq += 1
        t = Task(gen, prio, self.seq)
        self.tasks.append(t)
        self.tasks.sort(key=lambda x: (x.prio, x.seq))
        return t

    def time(self, *need):
        return max([self.when.get(m, 0.0) for m in flat(need)] or [0.0])

    def step(self, t):
        try:
            want = next(t.gen)
        except StopIteration:
            t.done = True
            self.tasks.remove(t)
            return
        t.want, t.at = None, 0.0
        if callable(want):
            t.want = want
        elif isinstance(want, float):
            t.at = want
        else:
            t.at = self.time(want)

    def go(self, main):
        while not main.done:
            now = max(self.clock, self.pe.t)
            best = None
            for t in self.tasks:
                if t.want is not None:
                    if not t.want():
                        continue
                    t.want = None
                    best = t
                    break
                if t.at <= now + self.SLACK:
                    best = t
                    break
            else:
                ready = [t for t in self.tasks if t.want is None]
                assert ready, "every part waits"
                best = min(ready, key=lambda t: t.at)
                self.clock = max(self.clock, best.at)
            self.step(best)

    def dma(self, q, slot, out, in_, *need):
        name = "dma_" + slot
        q.wait(*need)
        self.dma_count[name] = self.dma_count.get(name, 0) + 16
        q.items.append((lambda e, o=out, i=in_: e.dma_start(o, i), name, 16))
        mark = (name, self.dma_count[name])
        n = int(np.prod([c for _, c in list(out.ap)])) * 4
        if q is self.pool:
            q.t += 1030.0
            at = q.t + 650.0
        else:
            self.hw_t = max(self.hw_t, q.t) + 450.0
            q.t = self.hw_t
            at = self.hw_t + 650.0
        self.dma_t = max(self.dma_t, at) + n / 360.0
        self.when[mark] = self.dma_t + 1000.0
        return mark

    def bank(self):
        b = min(self.banks, key=lambda x: self.time(x.free))
        self.banks.remove(b)
        return b

    def get(self, k=1):
        yield lambda: len(self.banks) >= k
        b = self.bank()
        yield b.free
        return b

    def give(self, b, *marks):
        b.free = flat(marks)
        self.banks.append(b)

    def clocks(self):
        return 2.0 if self.pe.t < self.COLD else 1.0

    def mm(self, out, lhsT, rhs, start, stop, *need, inc=False, cost=None):
        n = width(out)
        cost = (cost or (n * 1.667 if rhs.dtype == F32 else max(n * 0.417, 107.0))) * self.clocks()
        return self.pe.do(lambda e: e.matmul(out, lhsT, rhs, start=start, stop=stop), *need, inc=inc, cost=cost)

    def tr(self, out, in_, ident, *need, inc=True):
        return self.pe.do(lambda e: e.transpose(out, in_, ident), *need, inc=inc, cost=107.0 * self.clocks())

    def a(self, out, in_, func, *need, bias=0.0, scale=1.0, accum=None):
        cost = 93.0 + 0.834 * width(in_)
        if accum is None:
            return self.act.do(lambda e: e.activation(out, in_, func, bias=bias, scale=scale), *need, cost=cost)
        return self.act.do(lambda e: e.activation(out, in_, func, bias=bias, scale=scale, accum_out=accum), *need, cost=cost + 93.0)

    def v(self, fn, ap, *need, q=None, more=0.0, rate=0.96):
        q = q or self.dve
        return q.do(fn, *need, cost=68.0 + width(ap) / rate + more)

    def cp(self, out, in_, *need, q=None):
        return self.v(lambda e: e.tensor_copy(out, in_), in_, *need, q=q)

    def tt(self, out, a, b, op, *need, q=None):
        return self.v(lambda e: e.tensor_tensor(out, a, b, op), out, *need, q=q, more=400.0 if op == ALU.pow else 0.0)

    def ts(self, out, a, s1, s2, op0, op1, *need, q=None, rate=0.96):
        if op1 is None:
            return self.v(lambda e: e.tensor_scalar(out, a, s1, None, op0), out, *need, q=q, more=61.0, rate=rate)
        return self.v(lambda e: e.tensor_scalar(out, a, s1, s2, op0, op1), out, *need, q=q, more=61.0, rate=rate)

    def stt(self, out, a, s, b, op0, op1, *need):
        return self.v(lambda e: e.scalar_tensor_tensor(out, a, s, b, op0=op0, op1=op1), out, *need, more=30.0)

    def ttr(self, out, a, b, scale, init, op0, op1, accum, *need):
        return self.v(lambda e: e.tensor_tensor_reduce(out, a, b, scale, init, op0, op1, accum), out, *need, more=30.0)

    def tsa(self, out, a, s1, op0, op1, accum, *need):
        return self.v(lambda e: e.tensor_scalar(out, a, s1, None, op0, op1, accum_out=accum), out, *need)

    def red(self, out, a, op, *need):
        return self.v(lambda e: e.tensor_reduce(out, a, AX.X, op), a, *need)

    def rec(self, out, a, *need):
        return self.v(lambda e: e.reciprocal(out, a), out, *need)

    def mset(self, out, v, *need, q=None):
        return self.v(lambda e: e.memset(out, v), out, *need, q=q)


class Chunk:

    def __init__(self, k0, k1):
        self.k0, self.k1, self.loaded, self.spent, self.before, self.raw = k0, k1, None, None, None, None


class Job:

    def __init__(self, key, parts, kt, w, split=True):
        self.key, self.parts, self.kt, self.w, self.split = key, parts, kt, w, split
        self.ring, self.place, self.last = 0, None, None
        self.ready, self.his, self.los = [None] * kt, [None] * kt, [None] * kt
        step = max(1, 512 // w)
        self.pieces = [(k, min(k + step, kt)) for k in range(0, kt, step)]
        some = max(1, 1024 // (w * step)) * step
        self.chunks = [Chunk(k, min(k + some, kt)) for k in range(0, kt, some)]
        self.chunk = [self.chunks[k // some] for k in range(kt)]

    def pack(self, ins):
        out = np.empty((128, self.kt, self.w), np.float32)
        for c0, name, lead, r0, s0, cols in self.parts:
            a = np.asarray(ins[name])[lead][r0:r0 + 128 * self.kt, s0:s0 + cols]
            out[:, :, c0:c0 + cols] = a.reshape(self.kt, 128, cols).transpose(1, 0, 2)
        return np.concatenate([out[:, c.k0:c.k1].reshape(-1) for c in self.chunks])

    def raw(self, k):
        c = self.chunk[k]
        return c.raw[:, (k - c.k0) * self.w:(k - c.k0 + 1) * self.w]

    def loaded(self, k):
        return self.chunk[k].loaded

    def hi(self, k):
        return self.his[k]

    def lo(self, k):
        return self.los[k]


class Weights:

    AHEAD = 3000.0
    SEMS = 8

    def __init__(self, p, plan, dram, rings, hi, lo):
        self.p, self.plan, self.dram, self.off, self.hi, self.lo = p, plan, dram, 0, hi, lo
        self.chunks = [c for j in plan for c in j.chunks]
        self.jobs_at = self.loads = 0
        self.by_key = {j.key: j for j in plan}
        for r, ring in enumerate(rings):
            mine, n = [c for j in plan if j.ring == r for c in j.chunks], ring.shape[1] // 1024
            for x, c in enumerate(mine):
                c.raw = ring[:, 1024 * (x % n):1024 * (x % n) + 1024]
                c.before = mine[x - n] if x >= n else None
        n = hi.shape[1] // 512
        held = []
        for j in plan:
            if j.split and j.place is None:
                for x, (k0, k1) in enumerate(j.pieces):
                    j.pieces[x] = (k0, k1, len(held) % n, held[-n] if len(held) >= n else None)
                    held.append(j)

    def pump(self):
        p = self.p
        while self.loads < len(self.chunks):
            c = self.chunks[self.loads]
            same_sem = self.chunks[self.loads - self.SEMS] if self.loads >= self.SEMS else None
            if any(x is not None and x.spent is None for x in (c.before, same_sem)):
                break
            j = self.job_of(c)
            n = (c.k1 - c.k0) * j.w
            c.raw = c.raw[:, 0:n]
            src = self.dram[self.off:self.off + 128 * n].rearrange("(p c) -> p c", p=128)
            self.off += 128 * n
            c.loaded = p.dma(p.sp, f"w{self.loads % self.SEMS}", c.raw, src, c.before and c.before.spent, same_sem and same_sem.spent)
            self.loads += 1

    def job_of(self, c):
        while c not in self.plan[self.jobs_at].chunks:
            self.jobs_at += 1
        return self.plan[self.jobs_at]

    def prepare(self):
        p = self.p
        for j in self.plan:
            if not j.split:
                continue
            for x, (k0, k1, *held) in enumerate(j.pieces):
                c = j.chunk[k0]
                yield lambda: c.loaded is not None
                if j.place is not None:
                    yield lambda: j.place() is not None
                    hi, lo, last = j.place()
                    at = 512 * x
                else:
                    place, before = held
                    yield lambda: before is None or before.last is not None
                    last = before and before.last
                    hi, lo, at = self.hi, self.lo, 512 * place
                yield [last]
                yield [c.loaded]
                yield max(p.act.t, p.dve.t) - self.AHEAD
                w = (k1 - k0) * j.w
                raw = c.raw[:, (k0 - c.k0) * j.w:(k1 - c.k0) * j.w]
                rounded = p.a(hi[:, at:at + w], raw, ACT.Copy, c.loaded, last)
                yield [rounded]
                split = p.tt(lo[:, at:at + w], raw, hi[:, at:at + w], ALU.subtract, rounded)
                for k in range(k0, k1):
                    o = slice(at + (k - k0) * j.w, at + (k + 1 - k0) * j.w)
                    j.his[k], j.los[k], j.ready[k] = hi[:, o], lo[:, o], split
                if k1 == c.k1:
                    c.spent = split
                    self.pump()

    def job(self, key):
        j = self.by_key[key]
        if j.split:
            yield lambda: j.ready[0] is not None
        else:
            yield lambda: j.chunks[-1].loaded is not None
        return j

    def free(self, j, last):
        j.last = last
        if not j.split:
            for c in j.chunks:
                c.spent = last
            self.pump()


SCR = 14336
CT, LAT = 0, 1


def job(key, name, c0, w, kt=8, r0=0, split=True, lead=()):
    return Job(key, [(0, name, lead, r0, c0, w)], kt, w, split)


def ada_own(l):
    return [(l, 2, j) for j in range(4)]


def ada_at(l, place, places):
    keys = [(l + 1, part, j) for j in range(4) for part in range(2)] if l < 3 else []
    n = max(0, len(keys) - TAIL[l]) if l < 3 else 0
    if place == places - 1:
        return keys[n:]
    return keys[n * place // (places - 1):n * (place + 1) // (places - 1)]


TAIL = (2, 0, 2)


def plan_ada(keys):
    return [job(("ada",) + k, f"l{k[0]}_w_ada", 1024 * k[1] + 256 * k[2], 256, split=False) for k in keys]


def plan_a(l):
    n = f"l{l}_w_in"
    jobs = [job(("k", l), n, 1024, 256), job(("v", l), n, 1280, 256)] + plan_ada(ada_own(l))
    for t in range(8):
        jobs += [job(("q", l, t), n, 128 * t, 128), job(("z", l, t), n, 1536 + 128 * t, 128)]
        jobs += plan_ada(ada_at(l, t, 9))
    return jobs + plan_ada(ada_at(l, 8, 9))


def plan_b(l):
    n, u = f"l{l}_w_in", f"l{l}_w_uq"
    jobs = [job(("qa",), n, 0, 256), job(("kva",), n, 256, 192)] + plan_ada(ada_own(l))
    z = lambda h: [job(("zb", h), n, 448 + 128 * h, 128)]
    for h in range(8):
        if h == 0:
            jobs += z(0) + z(1)
        if h % 2 == 0:
            c = 192 * h
            parts = [(0, u, (), 0, c + 128, 64), (64, u, (), 0, c + 320, 64), (128, u, (), 0, c, 128), (256, u, (), 0, c + 192, 128)]
            jobs += [Job(("uq", h // 2), parts, 2, 384), job(("ukv", h // 2), f"l{l}_w_ukv", 256 * h, 512, kt=1)]
        if h > 1:
            jobs += z(h)
        jobs += plan_ada(ada_at(l, h, 9))
    return jobs + plan_ada(ada_at(l, 8, 9))


def plan_c(l):
    n = f"l{l}_w_in"
    qkv = lambda j: [job(("qc", j), n, 128 * j, 128), job(("kc", j), n, 512 + 128 * j, 128), job(("vc", j), n, 1024 + 256 * j, 256)]
    oz = lambda j: [job(("oc", j), n, 2048 + 256 * j, 256), job(("zc", j), n, 3072 + 256 * j, 256)]
    ada = lambda x: plan_ada(ada_at(l, x, 8))
    jobs = qkv(0) + plan_ada(ada_own(l)) + [job(("gates",), n, 4096, 16)] + ada(0)
    for j in range(1, 4):
        jobs += qkv(j) + ada(2 * j - 1) + oz(j - 1) + ada(2 * j)
    return jobs + oz(3) + ada(7)


def plan_2():
    j2 = lambda key, name, c0, w, **kw: job(key, name, c0, w, lead=0, **kw)
    n = "w_in_2"
    small = Job(("small",), [(0, n, 0, 0, 1280, 24), (24, n, 0, 0, 3608, 8)], 8, 32)
    jobs = [j2(("p", c), n, c, 256) for c in (512, 768, 1024)] + [small]
    for wh in range(2):
        jobs += [Job(("w1", wh, h), [(0, "cmp_w1_2", (0, wh), 1024 * h, 0, 256)], 8, 256, False) for h in range(2)]
    jobs += [j2(("p", c), n, c, 256) for c in (0, 256, 1816, 1304, 1560, 2072, 2584, 3096, 2328, 2840, 3352)]
    mg = [(d, m) for d in range(4) for m in range(3)]
    merge = lambda d, m: j2(("merge", d, m), n, 3616 + 1024 * m + 256 * d, 256)
    jobs += [merge(*m) for m in mg[:4]]
    for d, m in mg:
        if (d, m) not in mg[:4]:
            jobs.append(merge(d, m))
        jobs.append(Job(("branch", d, m), [(0, "w_branch_2", (0, m), 0, 256 * d, 256)], 4, 256))
    jobs += [j2(("out2", j), "w_out_2", 256 * j, 256) for j in range(4)]
    for c in range(12):
        if c < 11:
            jobs += [j2(("gate", c), "w_gate_2", 256 * c, 256), j2(("up", c), "w_up_2", 256 * c, 256)]
        if c > 0:
            jobs += [Job(("down", c - 1, h), [(0, "w_down_2", 0, 256 * (c - 1), 512 * h, 512)], 2, 512) for h in range(2)]
    return jobs


def plan():
    jobs = plan_ada([(0, part, j) for j in range(4) for part in range(2)])
    for l, mix in enumerate((plan_a, plan_b, plan_c, plan_a)):
        jobs += mix(l) + [job(("out", l, j), f"l{l}_w_out", 256 * j, 256) for j in range(4)]
    return jobs + plan_2()


class Net(Core):

    BY_TILE = [(0, 0), (0, 1), (1, 0), (2, 0), (1, 1), (3, 0), (2, 1), (3, 1)]

    def __init__(self, nc, ctx, ins, out, upto):
        super().__init__()
        self.nc, self.ins, self.out, self.upto = nc, ins, out, upto
        sb = lambda name, shape, dt=F32: ctx.enter_context(nc.sbuf_tensor("s_" + name, shape, dt))
        self.X = sb("X", [128, 4, D])
        self.Hh = sb("Hh", [128, 8, 512], R32)
        self.Hl = sb("Hl", [128, 8, 512], R32)
        with nc.sbuf_tensor("GF", [128, 8192], F32) as GF:
            pass
        self.Gh = sb("Gh", [128, 8, 512], R32)
        self.Gl = sb("Gl", [128, 8, 512], R32)
        raw = sb("raw", [128, 4096])
        hi = sb("whi", [128, 4096], R32)
        lo = sb("wlo", [128, 4096], R32)
        self.K = sb("K", [128, 896])
        self.ident = self.K[:, 0:128]
        self.selB = self.K[:, 128:384].rearrange("p (s m) -> p s m", s=2)
        self.ropeC, self.ropeS = self.K[:, 384:640], self.K[:, 640:896]
        self.band = sb("band", [128, 2, 512], BF16)
        self.CS = sb("CS", [128, 8, 32])
        self.VC = sb("VC", [128, 168])
        self.SHc = sb("SHc", [128, 2, 8, 2])
        self.Ac = sb("Ac", [128, 2, 8, 2])
        self.st = sb("st", [128, 256])
        self.sink = sb("sink", [128, 48])
        self.G = sb("G", [128, 2, D])
        self.adaS = sb("adaS", [128, 2, 256])
        self.gp = sb("gp", [128, 2, 256])
        self.mhalf = sb("mhalf", [128, 32])
        self.bg = sb("bg", [128, 2, 256])
        with nc.sbuf_tensor("SF", [128, SCR], F32) as SF:
            pass
        self.SF, self.SR = SF, sb("SR", [128, SCR], R32)
        for i in range(8):
            self.banks.append(Bank(ctx.enter_context(nc.psum_tensor(f"ps{i}", [128, 512], F32))))
        jobs = plan()
        for k in (0, 1, 2, 3, 6, 7):
            jobs[k].ring = 1
        for j in jobs[8:16]:
            if j.key[0] == "ada":
                j.ring = 2
        self.place = {}

        def placed(key, at):
            if key not in self.place:
                return None
            return self.SR[:, at:at + 2048], self.SR[:, at + 2048:at + 4096], self.place[key]
        for j in jobs:
            if j.key[0] == "out" and j.key[2] == 3:
                j.place = lambda key=j.key: placed(key, 0)
            if j.key in (("p", 512), ("out2", 3)):
                j.place = lambda key=j.key: placed(key, 7168)
        self.w = Weights(self, jobs, ins["weights"], (raw, self.SF[:, 0:8192], GF[:, :]), hi, lo)
        self.o0 = out.shape[0] - 2
        self.sti = 0
        self.fence = []
        self.hr = [[None] * 8, [None] * 8]
        self.xr = [None] * 4
        self.h_free = []
        self.g_free = []
        self.v2_rd = None

    def now(self):
        return [(q.name, q.count) for q in (self.pe, self.act, self.dve, self.pool) if q.count]

    def F(self, at, *shape):
        n = int(np.prod(shape))
        ap = self.SF[:, at:at + n]
        return ap if len(shape) == 1 else self._shape(ap, shape)

    def Rr(self, at, *shape):
        n = int(np.prod(shape))
        ap = self.SR[:, at:at + n]
        return ap if len(shape) == 1 else self._shape(ap, shape)

    @staticmethod
    def _shape(ap, shape):
        if len(shape) == 2:
            return ap.rearrange("p (a b) -> p a b", a=shape[0])
        return ap.rearrange("p (a b c) -> p a b c", a=shape[0], b=shape[1])

    def cols(self, n):
        if self.sti + n > 256:
            self.sti = 0
        at = self.sti
        self.sti += n
        return self.st[:, at:at + n]

    def start(self):
        i = self.ins
        crow, rows, rows2 = self.F(8192, 128), self.F(8320, 128), self.F(8448, 128)
        th, th2 = self.F(8576, 16), self.F(8592, 16)
        band_f = self.G[:, 0, :].rearrange("p (a b) -> p a b", a=2)
        c_rd = self.dma(self.sp, "c", crow[0:16, :], i["cond"])
        self.k_rd = self.dma(self.act, "k", self.K[:, 0:384], i["konst"][:, 0:384])
        self.w.pump()
        vec = self.dma(self.pool, "vec", rows[0:104, :], i["vecs"][0:104])
        vec2 = self.dma(self.pool, "vecb", rows2[0:64, :], i["vecs"][104:168])
        self.vc = {"l1_g_qa": 32, "l1_g_kva": 34, "l2_g_head": 35, "l2_conv": 43}
        for l in range(4):
            self.vc[f"l{l}_g_pre"] = 8 * l
            self.vc[f"l{l}_b_ada"] = 104 + 16 * l
        for t in range(2):
            self.xr[t] = self.dma(self.sp, f"x{t}", self.X[:, t, :], i["ctx"][0, 128 * t:128 * t + 128, :])
        z = self.mset(self.CS[:, :, :], 0.0)
        self.mhalf_rd = self.mset(self.mhalf[:, :], -0.5)
        b = self.bank()
        ct = self.tr(b.t[:, 0:16], crow[0:16, :], self.ident[0:16, 0:16], c_rd, self.k_rd)
        t = self.a(th, b.t[:, 0:16], ACT.Tanh, ct, scale=0.5)
        t = self.stt(th2, th, 1.0, b.t[:, 0:16], ALU.add, ALU.mult, t)
        self.give(b, t)
        self.cs_rd = self.ts(self.CS[:, :, 0:2], th2.rearrange("p (s k) -> p k s", s=2), 0.5, None, ALU.mult, None, t, z)
        self.ada_slots = Slots(2)
        self.ada_rd = {}
        self.ada_left = 0
        self.g_rd = None
        self.G_free = []

        def vectors():
            b = yield from self.get()
            yield [vec, vec2]
            self.tr(b.t[:, 0:104], rows[0:104, :], self.ident[0:104, 0:104], vec)
            vt = self.tr(b.t[:, 104:168], rows2[0:64, :], self.ident[0:64, 0:64], vec2)
            yield [vt]
            self.vc_rd = self.cp(self.VC[:, :], b.t[:, 0:168], vt)
            self.give(b, self.vc_rd)

        def later():
            for t, after in ((2, 3), (3, 6)):
                ld = self.w.plan[after].loaded
                yield lambda: ld(7) is not None
                yield [ld(7)]
                self.xr[t] = self.dma(self.pool, f"x{t}", self.X[:, t, :], i["x"][0, 128 * t - 256:128 * t - 128, :], ld(7))
            self.rope_rd = self.dma(self.pool, "kr", self.K[:, 384:896], i["konst"][:, 384:896])
            ld = self.w.plan[8].loaded
            yield lambda: ld(7) is not None
            yield [ld(7)]
            bd = self.dma(self.pool, "band", band_f, i["band"].rearrange("p (a b) -> p a b", a=2), ld(7))
            sk = self.dma(self.pool, "sink", self.sink[:, :], i["rows"].to_broadcast([128, 48]))
            yield [bd]
            self.band_rd = self.cp(self.band[:, :, :], band_f, bd)
            self.G_free = [self.band_rd]
            yield [sk]
            self.sink_rd = self.ts(self.sink[:, 0:40], self.sink[:, 0:40], -1.0, None, ALU.mult, None, sk)
        self.vc_rd = self.band_rd = self.sink_rd = self.rope_rd = None
        return [self.spawn(vectors(), 0.0), self.spawn(later(), 0.0)]

    def ada_step(self, l, part, j):
        job = yield from self.w.job(("ada", l, part, j))
        b = yield from self.get(4)
        for kt in range(8):
            c = kt % 4
            yield [job.loaded(kt)]
            mk = self.mm(b.t[32 * c:32 * c + 32, 0:256], self.CS[:, kt, :], job.raw(kt), kt < 4, kt >= 4,
                         job.loaded(kt), self.cs_rd, b.free, inc=kt == 7, cost=128.0)
        self.w.free(job, mk)
        self.ada_left += 1
        self.spawn(self.ada_tail(l, part, j, b, mk), 0.0)

    def ada_tail(self, l, part, j, b, mk):
        s, free = yield from self.ada_slots.take()
        if part == 2:
            row = lambda a: a.rearrange("(a c) -> a c", a=1).to_broadcast([128, 256])
            o = slice(256 * j, 256 * j + 256)
            gp_rd = [self.dma(self.sp, f"gp{s}", self.gp[:, s, :], row(self.ins[f"l{l}_g_post"][o]), free),
                     self.dma(self.sp, f"gp{s}", self.bg[:, s, :], row(self.ins[f"l{l}_b_ada"][2048 + 256 * j:2304 + 256 * j]), free)]
        yield [mk]
        ev = self.a(self.adaS[:, s, :], b.t[:, 0:256], ACT.Copy, mk, free)
        yield [ev]
        if part < 2:
            for h in range(2):
                mk = self.mm(b.t[:, 256 + 2 * h:258 + 2 * h], self.adaS[:, s, 128 * h:128 * h + 128], self.selB[:, :, 0],
                             True, True, ev, inc=True, cost=215.0)
            self.ada_slots.give(s, mk)
            yield lambda: self.vc_rd is not None
            yield [mk, self.vc_rd]
            col = lambda at: self.VC[:, at:at + 2].rearrange("p (k a) -> p k a", a=1).to_broadcast([128, 2, 2])
            bias = col(self.vc[f"l{l}_b_ada"] + 8 * part + 2 * j)
            pv = b.t[:, 256:260].rearrange("p (k s) -> p k s", s=2)
            dst = (self.SHc if part == 0 else self.Ac)[:, l % 2, 2 * j:2 * j + 2, :]
            d = self.tt(dst, pv, bias, ALU.add, mk, self.vc_rd)
            self.give(b, d)
            if part == 1:
                d = self.stt(dst, dst, 1.0, col(self.vc[f"l{l}_g_pre"] + 2 * j), ALU.add, ALU.mult, d)
            self.ada_rd[l, part, j] = d
        else:
            self.give(b, ev)
            gb = yield from self.get(2)
            for q in range(2):
                mk = self.mm(gb.t[:, 256 * q:256 * q + 256], self.selB[:, q, :], self.adaS[:, s, :],
                             True, True, ev, gb.free, inc=True)
            yield lambda: self.band_rd is not None
            yield [mk, gp_rd]
            bc = lambda a: a[:, s, :].rearrange("p (a b) -> p a b", a=1).to_broadcast([128, 2, 256])
            g = self.G[:, :, 256 * j:256 * j + 256]
            d = self.tt(g, gb.t[:, :].rearrange("p (a b) -> p a b", a=2), bc(self.bg), ALU.add, mk, gp_rd, self.G_free)
            self.give(gb, d)
            d = self.tt(g, g, bc(self.gp), ALU.mult, d)
            self.ada_slots.give(s, d)
            self.g_rd = d
        self.ada_left -= 1

    def ada_some(self, l, place=None, places=None):
        for k in ada_own(l) if place is None else ada_at(l, place, places):
            yield from self.ada_step(*k)

    def rstd(self, ss, n, cnt, *need):
        out = self.cols(n)
        t = self.ts(out, ss, 1.0 / cnt, EPS, ALU.mult, ALU.add, *need)
        t = self.tt(out, out, self.mhalf[:, 0:n], ALU.pow, t, self.mhalf_rd, q=self.pool)
        return out, t

    def h_cols(self, l, s):
        return (lambda kt: self.Ac[:, l % 2, kt, s:s + 1], lambda kt: self.SHc[:, l % 2, kt, s:s + 1],
                lambda kp: [self.ada_rd.get((l, part, kp)) for part in range(2)])

    def new_h(self):
        self.hr = [[None] * 8, [None] * 8]
        return self.hr

    def new_tiles(self):
        self.hr = [[None] * 8, [[None, None] for _ in range(8)]]
        return self.hr

    def tiles_h(self, A_, ar, xn, nt):
        hr = self.hr

        def tail(i, k0, b, mk):
            yield lambda: known(ar())
            yield [mk, ar()]
            o = slice(256 + 128 * i, 384 + 128 * i)
            p = lambda kt: b.t[:, 128 * (kt - k0):128 * (kt - k0) + 128]
            for kt in range(k0, k0 + 4):
                ta = self.a(self.Hh[:, kt, o], p(kt), ACT.Copy, mk, ar(), self.h_free, scale=A_(kt))
            yield [ta]
            for kt in range(k0, k0 + 4):
                t = self.stt(self.Hl[:, kt, o], p(kt), A_(kt), self.Hh[:, kt, o], ALU.mult, ALU.subtract, ta, mk, ar(), self.h_free)
                hr[LAT][kt][i] = t
            self.give(b, t)
        for i in range(2):
            yield lambda: nt[i] is not None
            for k0 in (0, 4):
                b = yield from self.get(2)
                yield [nt[i]]
                for kt in range(k0, k0 + 4):
                    mk = self.tr(b.t[:, 128 * (kt - k0):128 * (kt - k0) + 128], xn[:, i, 128 * kt:128 * kt + 128], self.ident, nt[i], b.free)
                self.spawn(tail(i, k0, b, mk), 0.0)
        yield lambda: known(hr[LAT])

    def norm_tile(self, s, i, xn, nt, *need):
        x = self.X[:, 2 * s + i, :]
        ss = self.cols(1)
        yield lambda: self.xr[2 * s + i] is not None
        yield [self.xr[2 * s + i], *need]
        t = self.a(xn[:, i, :], x, ACT.Square, self.xr[2 * s + i], *need, accum=ss)
        yield [t]
        rs, rt = self.rstd(ss, 1, D, t)
        yield [rt]
        nt[i] = self.ts(xn[:, i, :], x, rs, None, ALU.mult, None, rt, t, rate=1.92)

    def make_h(self, hr, cols, s, xn, hf, nt, *need):
        A_, S_, ar = cols
        yield lambda: known(nt)
        hs = Slots(2)

        def tail(kp, b, mk):
            x, free = yield from hs.take()
            yield lambda: known(ar(kp))
            yield [mk, ar(kp)]
            tb = []
            for h in range(2):
                kt = 2 * kp + h
                p = b.t[:, 256 * h:256 * h + 256]
                o, need2 = hf[:, x, h, :], [mk, ar(kp), free, *need]
                if kp % 2 == 1 and S_ is None:
                    tb.append(self.a(o, p, ACT.Copy, need2, scale=A_(kt)))
                elif kp % 2 == 1:
                    tb.append(self.a(o, p, ACT.Identity, need2, scale=A_(kt), bias=S_(kt)))
                elif S_ is None:
                    tb.append(self.ts(o, p, A_(kt), None, ALU.mult, None, need2))
                else:
                    tb.append(self.ts(o, p, A_(kt), S_(kt), ALU.mult, ALU.add, need2))
            self.give(b, tb)
            yield tb
            o = slice(256 * s, 256 * s + 256)
            hh, hl = self.Hh[:, 2 * kp:2 * kp + 2, o], self.Hl[:, 2 * kp:2 * kp + 2, o]
            ta = self.a(hh, hf[:, x], ACT.Copy, tb, self.h_free)
            yield [ta]
            tc = self.tt(hl, hf[:, x], hh, ALU.subtract, ta, tb, self.h_free)
            hs.give(x, tc)
            hr[s][2 * kp] = hr[s][2 * kp + 1] = tc
        for kp in range(4):
            b = yield from self.get(2)
            for i in range(2):
                yield [nt[i]]
                for h in range(2):
                    kt = 2 * kp + h
                    mk = self.tr(b.t[:, 256 * h + 128 * i:256 * h + 128 * i + 128], xn[:, i, 128 * kt:128 * kt + 128],
                                 self.ident, nt[i], b.free)
            self.spawn(tail(kp, b, mk), 0.0)
        yield lambda: known(hr[s])

    def form_a(self, job, c0, m, out, n0, n, Hh, Hl, rdy, free, every=2):
        for k in range(job.kt):
            if k % every == 0:
                ks = range(k, min(k + every, job.kt))
                need = lambda: [[job.ready[q], rdy(q)] for q in ks]
                yield lambda: known(need())
                yield need()
            wh, wl = job.hi(k)[:, c0:c0 + m], job.lo(k)[:, c0:c0 + m]
            hh, hl = Hh[:, k, n0:n0 + n], Hl[:, k, n0:n0 + n]
            last = k == job.kt - 1
            self.mm(out, wh, hh, k == 0, False, job.ready[k], rdy(k), free)
            self.mm(out, wh, hl, False, False)
            mk = self.mm(out, wl, hh, False, last, inc=last)
        return mk

    def form_b(self, job, c0, w, out, t0, Hh, Hl, rdy, free, every=4):
        for k in range(job.kt):
            if k % every == 0:
                ks = range(k, min(k + every, job.kt))
                need = lambda: [[job.ready[q], rdy(q)] for q in ks]
                yield lambda: known(need())
                yield need()
            wh, wl = job.hi(k)[:, c0:c0 + w], job.lo(k)[:, c0:c0 + w]
            hh, hl = Hh[:, k, t0:t0 + 128], Hl[:, k, t0:t0 + 128]
            last = k == job.kt - 1
            self.mm(out, hh, wh, k == 0, False, job.ready[k], rdy(k), free)
            self.mm(out, hh, wl, False, False)
            mk = self.mm(out, hl, wh, False, last, inc=last)
        return mk

    def hrd(self, s0, s1):
        hr = self.hr
        return lambda k: [hr[s][k] for s in range(s0, s1)]

    def prod_b(self, job, w, s):
        b = yield from self.get(4)
        for i in range(2):
            mk = yield from self.form_b(job, 0, w, b.t[:, w * i:w * i + w], 256 * s + 128 * i, self.Hh, self.Hl,
                                        self.hrd(s, s + 1), b.free)
        return b, mk

    def rope(self, q, tmp, *need):
        n = q.shape[0]
        a = self.v(lambda e: e.stream_shuffle(tmp[0:n], q, mask=[j ^ 1 for j in range(32)]), q, *need, self.rope_rd)
        a = self.tt(tmp[0:n], tmp[0:n], self.ropeS[0:n, :], ALU.mult, a)
        b = self.tt(q, q, self.ropeC[0:n, :], ALU.mult, a)
        return self.tt(q, q, tmp[0:n], ALU.add, a, b)

    def turned(self):
        yield lambda: self.turn.done
        self.fence = self.now()
        return self.fence

    def layer_a(self, l, streams):
        f0 = self.fence
        KH, KL = self.Rr(0, 4, 512), self.Rr(2048, 4, 512)
        QS = self.Rr(4096, 2, 2, 512)
        V = self.F(6144, 4, 256)
        ZT = self.F(7168, 2, 512)
        qf = self.F(8192, 2, 512)
        tmp = self.F(9216, 256)
        gf = self.F(13312, 2, 256)
        c = dict(l=l, streams=streams, KH=KH, KL=KL, QS=QS, V=V, ZT=ZT, qf=qf, tmp=tmp, gf=gf, kr={}, vr={},
                 qf_s=Slots(2), gf_s=Slots(2), qs_s=Slots(2), zt_s=Slots(2), q={}, z={}, f0=f0)
        self.gr = [[None] * 8, [None] * 8]

        def k_tail(s, t, b, mk, f0):
            o = slice(256 * s, 256 * s + 256)
            x, free = yield from c["qf_s"].take()
            yield [mk]
            q = qf[:, x, 0:256]
            t1 = self.a(q, b.t[:, 0:256], ACT.Copy, mk, free, f0)
            self.give(b, t1)
            yield [t1]
            if s == LAT:
                yield lambda: self.rope_rd is not None
                t1 = self.rope(q, tmp, t1, f0)
                yield [t1]
            rd = []
            for h in range(2):
                g, r, y = 2 * t + h, slice(64 * h, 64 * h + 64), slice(64 - 64 * h, 128 - 64 * h)
                ah = self.a(KH[r, g, o], q[r], ACT.Copy, t1, f0, scale=0.125)
                ax = self.a(KH[y, g, o], q[r], ACT.Copy, t1, f0, scale=0.125)
                yield [ah]
                d1 = self.stt(KL[r, g, o], q[r], 0.125, KH[r, g, o], ALU.mult, ALU.subtract, ah, t1, f0)
                d2 = self.stt(KL[y, g, o], q[r], 0.125, KH[r, g, o], ALU.mult, ALU.subtract, ah, t1, f0)
                rd += [ax, d1, d2]
                c["kr"][s, g] = [ax, d1, d2]
            c["qf_s"].give(x, rd)

        def v_tail(s, b, mk, f0):
            yield [mk]
            c["vr"][s] = t = self.cp(V[:, 2 * s:2 * s + 2, :], b.t[:, :].rearrange("p (i c) -> p i c", i=2), mk, f0)
            self.give(b, t)
        jk = yield from self.w.job(("k", l))
        jv = None
        for s in (CT, LAT):
            if s == LAT:
                if l == 0:
                    yield lambda: self.own.done
                else:
                    yield from self.ada_some(l)
                f0 = c["f0"] = yield from self.turned()
            for t in range(2):
                b, mk = yield from self.prod_k(jk, t, s)
                self.spawn(k_tail(s, t, b, mk, f0), 0.0)
            if s == LAT:
                self.w.free(jk, mk)
            if jv is None:
                jv = yield from self.w.job(("v", l))
            b, mk = yield from self.prod_b(jv, 256, s)
            self.spawn(v_tail(s, b, mk, f0), 0.0)
        self.w.free(jv, mk)
        att = self.spawn(self.attention(self.units_a(c), at=9472), 0.5)
        yield from self.proj_qz(c)
        yield lambda: att.done

    def prod_k(self, job, t, s):
        b = yield from self.get(4)
        mk = yield from self.form_a(job, 128 * t, 128, b.t[:, 0:256], 256 * s, 256, self.Hh, self.Hl, self.hrd(s, s + 1), b.free)
        return b, mk

    def proj_qz(self, c):
        l, streams = c["l"], c["streams"]
        s0 = streams[0]
        n0, n = 256 * s0, 256 * len(streams)
        qf, tmp, QS = c["qf"], c["tmp"], c["QS"]
        o = slice(n0, n0 + n)
        f0 = c["f0"]

        def q_tail(t, b, mk):
            x, free = yield from c["qf_s"].take()
            yield [mk]
            t1 = self.a(qf[:, x, o], b.t[:, o], ACT.Copy, mk, free, f0)
            self.give(b, t1)
            yield [t1]
            r0 = [self.rope(qf[:, x, 256:512], tmp, t1, f0), t1]
            y, free = yield from c["qs_s"].take()
            yield r0
            rd = []
            for h in range(2):
                r, z = slice(64 * h, 64 * h + 64), slice(64 - 64 * h, 128 - 64 * h)
                ah = self.a(QS[r, y, h, o], qf[r, x, o], ACT.Copy, r0, free)
                yield [ah]
                d = self.tt(QS[z, y, h, o], qf[r, x, o], QS[r, y, h, o], ALU.subtract, ah, r0, free)
                rd += [ah, d]
            c["q"][t] = (y, rd)
            c["qf_s"].give(x, rd)

        def z_tail(t, b, mk):
            x, free = yield from c["zt_s"].take()
            yield [mk]
            z = c["ZT"][:, x, o]
            ta = self.a(z, b.t[:, o], ACT.Tanh, mk, free, f0, scale=0.5)
            yield [ta]
            td = self.stt(z, z, 1.0, b.t[:, o], ALU.add, ALU.mult, ta)
            self.give(b, td)
            c["z"][t] = (x, td)
        for t in range(8):
            for key, tail in (("q", q_tail), ("z", z_tail)):
                job = yield from self.w.job((key, l, t))
                b = yield from self.get(4)
                mk = yield from self.form_a(job, 0, 128, b.t[:, o], n0, n, self.Hh, self.Hl, self.hrd(s0, 2), b.free)
                self.w.free(job, mk)
                self.spawn(tail(t, b, mk), 0.0)
            if t == 7:
                self.h_free = [mk]
            yield from self.ada_some(l, t, 9)
        yield from self.ada_some(l, 8, 9)

    def units_a(self, c):
        KH, KL, QS, V = c["KH"], c["KL"], c["QS"], c["V"]
        sk = 0 if c["l"] == 0 else 16
        left, zleft = {}, {}
        for t in range(8):
            left[t], zleft[t] = 4 * len(c["streams"]), len(c["streams"])
            for s in c["streams"]:
                box = {}
                for i in range(2):
                    for e in range(2):
                        g, h = t // 2, 2 * t + e
                        nk = 256 if s == CT else 512
                        nt = nk // 128

                        def ready(t=t, g=g, s=s):
                            return t in c["q"] and all((s2, g) in c["kr"] for s2 in range(s + 1))

                        def need(t=t, g=g, s=s):
                            return [c["q"][t][1], [c["kr"][s2, g] for s2 in range(s + 1)]]

                        def scores(b, s=s, g=g, e=e, i=i, nk=nk, t=t, need=need):
                            o = 256 * s + 128 * i
                            x = c["q"][t][0]
                            self.mm(b.t[:, 0:nk], QS[:, x, e, o:o + 128], KH[:, g, 0:nk], True, False, need(), b.free)
                            mk = self.mm(b.t[:, 0:nk], QS[:, x, e, o:o + 128], KL[:, g, 0:nk], False, True, inc=True)
                            left[t] -= 1
                            if left[t] == 0:
                                c["qs_s"].give(x, mk)
                            return mk

                        def values(ob, pts, marks, s=s, g=g, i=i, nt=nt):
                            for k in range(nt):
                                for e2 in range(2):
                                    mk = self.mm(ob.t[64 * e2:64 * e2 + 64, 128 * i:128 * i + 128],
                                                 V[:, k, 64 * g:64 * g + 64], pts[e2][:, k, :], k == 0, k == nt - 1,
                                                 marks[e2], c["vr"][s], c["vr"][CT], ob.free, inc=k == nt - 1)
                            return mk

                        def gate(ob, mk, s=s, t=t):
                            o = slice(256 * s, 256 * s + 256)
                            yield lambda: t in c["z"]
                            x, zr = c["z"][t]
                            y, free = yield from c["gf_s"].take()
                            yield [mk, zr]
                            gf = c["gf"][:, y, :]
                            d = self.stt(gf, ob.t[:, 0:256], 0.5, c["ZT"][:, x, o], ALU.mult, ALU.mult, mk, zr, free, c["f0"])
                            self.give(ob, d)
                            zleft[t] -= 1
                            if zleft[t] == 0:
                                c["zt_s"].give(x, d)
                            yield [d]
                            ah = self.a(self.Gh[:, t, o], gf, ACT.Copy, d, self.g_free)
                            yield [ah]
                            d2 = self.tt(self.Gl[:, t, o], gf, self.Gh[:, t, o], ALU.subtract, ah, self.g_free)
                            c["gf_s"].give(y, d2)
                            self.gr[s][t] = d2

                        yield dict(ready=ready, need=need, scores=scores, values=values, nk=nk, pair=e, box=box, first=i == 0,
                                   vready=lambda s=s: known([c["vr"].get(s), c["vr"].get(CT)]),
                                   gate=gate if i == 1 else None, mask=self.band[:, i, 0:nk], sink=self.sink[:, sk + h:sk + h + 1],
                                   mask_rd=lambda: [self.sink_rd, self.band_rd])

    def attention(self, units, at=9472, nsm=4, npt=3, wide=514, kts=4):
        A = dict(SM=self.F(at, nsm, wide), PT=self.F(at + wide * nsm, npt, kts, 128), f0=self.fence, sm=Slots(nsm), pt=Slots(npt),
                 turned=0, values=0)
        group, tasks, n = [], [], 0
        for k, u in enumerate(units):
            yield u["ready"]
            u["at"], free = yield from A["sm"].take()
            tasks.append(self.spawn(self.unit(u, A, k, free), 0.0))
            group.append(u)
            if u["pair"] != 0:
                tasks.append(self.spawn(self.values(group, A, n), 0.0))
                group, n = [], n + 1
        yield lambda: all(t.done for t in tasks)

    def unit(self, u, A, k, free):
        nk, f0 = u["nk"], A["f0"]
        st = self.cols(2)
        sm = A["SM"][:, u["at"], 0:nk + (u["sink"] is not None)]
        rows = sm[:, 0:nk]
        b = yield from self.get(1)
        yield u["need"]()
        mk = u["scores"](b)
        mr = u["mask_rd"] and u["mask_rd"]()
        yield [mk, mr]
        need = [mk, free, f0, mr]
        if u["mask"] is None:
            t = [self.tsa(rows, b.t[:, 0:nk], -1.0, ALU.mult, ALU.min, st[:, 0:1], need)]
        elif u["sink"] is None:
            t = [self.ttr(rows, b.t[:, 0:nk], u["mask"], -1.0, -FLOOR, ALU.add, ALU.min, st[:, 0:1], need)]
        else:
            pl = self.cp(sm[:, nk:nk + 1], u["sink"], free, mr, f0, q=self.pool)
            t = [self.ttr(rows, b.t[:, 0:nk], u["mask"], -1.0, u["sink"], ALU.add, ALU.min, st[:, 0:1], need), pl]
        self.give(b, t[0])
        if u.get("shift") is not None:
            t = [self.ts(st[:, 0:1], st[:, 0:1], u["shift"], u["shift"], ALU.subtract, ALU.add, t, mr)]
        yield t
        t = self.a(sm, sm, ACT.Exp, t, bias=st[:, 0:1], scale=-1.0, accum=st[:, 1:2])
        gc, gr = u.get("gate_col"), None
        if gc is not None:
            yield u["gate_known"]
            gr = u["gate_rd"]()
        yield [t, gr]
        t = self.rec(st[:, 1:2], st[:, 1:2], t)
        if gc is None:
            done = self.ts(rows, rows, st[:, 1:2], None, ALU.mult, None, t, rate=1.92)
        else:
            done = self.ts(rows, rows, st[:, 1:2], gc, ALU.mult, ALU.mult, t, gr, rate=1.92)
        yield lambda: A["turned"] == k
        y, free = yield from A["pt"].take()
        b = yield from self.get(1)
        yield [done]
        nt, kw = max(1, nk // 128), min(128, nk)
        for q in range(nt):
            mk = self.tr(b.t[0:kw, 128 * q:128 * q + 128], sm[:, 128 * q:128 * q + kw], self.ident, done, b.free, inc=q == nt - 1)
        A["turned"] = k + 1
        A["sm"].give(u["at"], mk)
        yield [mk]
        u["pt"] = A["PT"][0:kw, y, 0:nt, :]
        u["ptr"] = self.a(u["pt"], b.t[0:kw, 0:128 * nt].rearrange("p (k q) -> p k q", k=nt), ACT.Copy, mk, free, f0)
        u["pt_at"] = y
        self.give(b, u["ptr"])

    def values(self, us, A, n):
        u = us[-1]
        yield lambda: A["values"] == n and all("ptr" in y for y in us) and u["vready"]()
        if u["first"]:
            u["box"]["o"] = yield from self.get(2)
        ob = u["box"]["o"]
        yield [y["ptr"] for y in us]
        mk = u["values"](ob, [y["pt"] for y in us], [y["ptr"] for y in us])
        A["values"] = n + 1
        for y in us:
            A["pt"].give(y["pt_at"], mk)
        if u["gate"] is not None:
            yield from u["gate"](ob, mk)

    def split(self, hh, hl, f, *need):
        a = self.a(hh, f, ACT.Copy, *need)
        yield [a]
        return self.tt(hl, f, hh, ALU.subtract, a, *need)

    def norm_rows(self, out, p, w, *need):
        ss = self.cols(2)
        sq = [self.a(out[:, i, 0:w], p[:, i, 0:w], ACT.Square, *need, accum=ss[:, i:i + 1]) for i in range(2)]
        yield sq
        rs, t = self.rstd(ss, 2, w, sq)
        yield [t]
        return [self.ts(out[:, i, 0:w], p[:, i, 0:w], rs[:, i:i + 1], None, ALU.mult, None, t, *need) for i in range(2)]

    def layer_b(self, l):
        f0 = self.fence
        QAh, QAl = self.Rr(0, 2, 512), self.Rr(1024, 2, 512)
        KAh, KAl = self.Rr(2048, 1, 512), self.Rr(2560, 1, 512)
        KP = self.Rr(3072, 2, 512)
        QP = self.Rr(4096, 2, 2, 512)
        QN, KN = self.F(6144, 2, 512), self.F(7168, 2, 512)
        V, ZT = self.F(8192, 2, 4, 128), self.F(9216, 2, 512)
        qf, gf, tmp = self.F(10240, 512), self.F(10752, 256), self.F(11008, 256)
        nat, nat2, f1, f2, pf = self.F(6144, 2, 256), self.F(6656, 2, 192), self.F(7168, 2, 256), self.F(7680, 1, 256), self.F(7936, 256)
        vc = self.vc
        qar, kar, kpr = [None] * 2, [None] * 2, [None] * 2
        c = dict(l=l, QN=QN, KN=KN, V=V, ZT=ZT, qf=qf, gf=gf, tmp=tmp, QP=QP, KP=KP, kpr=kpr, rd={}, qp={}, z={},
                 qn_s=Slots(2), v_s=Slots(2), qp_s=Slots(2), zt_s=Slots(2), gf_s=Slots(1), qf_s=Slots(1))
        self.gr = [[None] * 8, [None] * 8]
        free = dict(nat=[], nat2=[], f1=[], f2=[])

        def qa_tail(s, b, mk, f0, prev):
            yield lambda: prev is None or prev.done
            yield [mk]
            o = slice(256 * s, 256 * s + 256)
            nt = yield from self.norm_rows(nat, b.t[:, :].rearrange("p (i c) -> p i c", i=2), 256, mk, f0, free["nat"])
            self.give(b, nt)
            b = yield from self.get(1)
            yield nt
            for kt in range(2):
                for i in range(2):
                    mk = self.tr(b.t[:, 256 * kt + 128 * i:256 * kt + 128 * i + 128], nat[:, i, 128 * kt:128 * kt + 128],
                                 self.ident, nt, b.free)
            free["nat"] = [mk]
            yield [mk]
            ev = [self.ts(f1[:, kt, :], b.t[:, 256 * kt:256 * kt + 256], self.VC[:, vc["l1_g_qa"] + kt:vc["l1_g_qa"] + kt + 1],
                          None, ALU.mult, None, mk, f0, free["f1"]) for kt in range(2)]
            self.give(b, ev)
            yield ev
            qar[s] = yield from self.split(QAh[:, :, o], QAl[:, :, o], f1[:, :, :], ev, f0)
            free["f1"] = [qar[s]]

        def kva_tail(s, b, mk, f0, prev):
            yield lambda: prev is None or prev.done
            yield [mk]
            o = slice(256 * s, 256 * s + 256)
            p2 = b.t[:, 0:384].rearrange("p (i c) -> p i c", i=2)
            nt = yield from self.norm_rows(nat2, p2, 128, mk, f0, free["nat2"])
            nt = [nt, self.cp(nat2[:, :, 128:192], p2[:, :, 128:192], nt, free["nat2"], f0)]
            self.give(b, nt)
            b = yield from self.get(1)
            yield nt
            for i in range(2):
                mk = self.tr(b.t[:, 128 * i:128 * i + 128], nat2[:, i, 0:128], self.ident, nt, b.free)
            for i in range(2):
                mk = self.tr(b.t[0:64, 256 + 128 * i:384 + 128 * i], nat2[:, i, 128:192], self.ident, nt)
            free["nat2"] = [mk]
            yield [mk]
            ev = [self.ts(f2[:, 0, :], b.t[:, 0:256], self.VC[:, vc["l1_g_kva"]:vc["l1_g_kva"] + 1], None, ALU.mult, None,
                          mk, f0, free["f2"])]
            e2 = self.cp(pf[0:64, :], b.t[0:64, 256:512], mk, f0, free["f2"])
            self.give(b, ev, e2)
            yield ev
            kar[s] = yield from self.split(KAh[:, 0, o], KAl[:, 0, o], f2[:, 0, :], ev, f0)
            if s == LAT:
                e2 = self.rope(pf[0:64, :], tmp, e2, f0)
            yield [e2]
            kp = []
            for r in (slice(0, 64), slice(64, 128)):
                kp.append(self.a(KP[r, 0, o], pf[0:64, :], ACT.Copy, e2, f0))
            yield kp
            for r in (slice(0, 64), slice(64, 128)):
                kp.append(self.tt(KP[r, 1, o], pf[0:64, :], KP[0:64, 0, o], ALU.subtract, e2, kp[0], f0))
            free["f2"] = [kp, kar[s]]
            kpr[s] = kp
        jq = yield from self.w.job(("qa",))
        jk = None
        tq = tk = None
        tails = []
        for s in (CT, LAT):
            if s == LAT:
                yield from self.ada_some(l)
                f0 = yield from self.turned()
            b, mk = yield from self.prod_b(jq, 256, s)
            tq = self.spawn(qa_tail(s, b, mk, f0, tq), 0.0)
            if s == LAT:
                self.w.free(jq, mk)
            if jk is None:
                jk = yield from self.w.job(("kva",))
            b, mk = yield from self.prod_b(jk, 192, s)
            tk = self.spawn(kva_tail(s, b, mk, f0, tk), 0.0)
        self.w.free(jk, mk)
        c["f0"] = f0
        yield from self.z_b(c, 0)
        yield from self.z_b(c, 1)
        yield lambda: tq.done and tk.done
        c["fz"] = self.fence = self.now()
        att = self.spawn(self.attention(self.units_b(c), at=11264, nsm=4, npt=2, wide=512), 0.5)
        yield from self.proj_b(c, QAh, QAl, KAh, KAl, qar, kar)
        yield lambda: att.done

    def z_b(self, c, h):
        def tail(b, mk):
            x, free = yield from c["zt_s"].take()
            yield [mk]
            z = c["ZT"][:, x, :]
            ta = self.a(z, b.t[:, :], ACT.Tanh, mk, free, f0, scale=0.5)
            yield [ta]
            td = self.stt(z, z, 1.0, b.t[:, :], ALU.add, ALU.mult, ta)
            self.give(b, td)
            c["z"][h] = (x, td)
        f0 = c["f0"]
        job = yield from self.w.job(("zb", h))
        b = yield from self.get(4)
        mk = yield from self.form_a(job, 0, 128, b.t[:, :], 0, 512, self.Hh, self.Hl, self.hrd(0, 2), b.free)
        self.w.free(job, mk)
        if h == 7:
            self.h_free = [mk]
        self.spawn(tail(b, mk), 0.0)

    def proj_b(self, c, QAh, QAl, KAh, KAl, qar, kar):
        l = c["l"]
        scale = float(192.0 ** -0.5)
        QN, KN, V, qf, tmp, QP = (c[k] for k in ("QN", "KN", "V", "qf", "tmp", "QP"))
        fz = c["fz"]

        def rot_tail(p, b, mk):
            _, free = yield from c["qf_s"].take()
            yield [mk]
            t1 = self.a(qf, b.t[:, :], ACT.Copy, mk, fz, free, scale=scale)
            self.give(b, t1)
            yield [t1]
            r0 = [self.rope(qf[:, 256:512], tmp, t1, fz), t1]
            y, free = yield from c["qp_s"].take()
            yield r0
            rd = []
            for e in range(2):
                r, z = slice(64 * e, 64 * e + 64), slice(64 - 64 * e, 128 - 64 * e)
                ah = self.a(QP[r, y, e, :], qf[r], ACT.Copy, r0, free)
                yield [ah]
                d = self.tt(QP[z, y, e, :], qf[r], QP[r, y, e, :], ALU.subtract, ah, r0, free)
                rd += [ah, d]
            c["qf_s"].give(0, rd)
            c["qp"][p] = (y, rd)

        def head_tail(h, bq, mq, bk, mk, bv, mv):
            x, free = yield from c["qn_s"].take()
            yield [mq]
            rq = self.a(QN[:, x, :], bq.t[:, :], ACT.Copy, mq, fz, free, scale=scale)
            self.give(bq, rq)
            yield [mk]
            rk = self.a(KN[:, x, :], bk.t[:, :], ACT.Copy, mk, fz, free)
            self.give(bk, rk)
            y, free = yield from c["v_s"].take()
            yield [mv]
            rv = self.cp(V[:, y], bv.t[:, :].rearrange("p (t c) -> p t c", t=4), mv, fz, free)
            self.give(bv, rv)
            c["rd"][h] = (x, y, [rq, rk, rv])
        for h in range(8):
            e, p = h % 2, h // 2
            if e == 0:
                uq = yield from self.w.job(("uq", p))
                ukv = yield from self.w.job(("ukv", p))
                b = yield from self.get(4)
                mk = yield from self.form_a(uq, 0, 128, b.t[:, :], 0, 512, QAh, QAl, lambda k: qar, b.free)
                self.spawn(rot_tail(p, b, mk), 0.0)
            bq = yield from self.get(4)
            mq = yield from self.form_a(uq, 128 + 128 * e, 128, bq.t[:, :], 0, 512, QAh, QAl, lambda k: qar, bq.free)
            bk = yield from self.get(4)
            mkk = yield from self.form_a(ukv, 256 * e, 128, bk.t[:, :], 0, 512, KAh, KAl, lambda k: kar, bk.free)
            bv = yield from self.get(4)
            for t in range(4):
                mv = yield from self.form_b(ukv, 256 * e + 128, 128, bv.t[:, 128 * t:128 * t + 128], 128 * t, KAh, KAl,
                                            lambda k: kar, bv.free)
            self.spawn(head_tail(h, bq, mq, bk, mkk, bv, mv), 0.0)
            if e == 1:
                self.w.free(uq, mv)
                self.w.free(ukv, mv)
            if h > 1:
                yield from self.z_b(c, h)
            yield from self.ada_some(l, h, 9)
        yield from self.ada_some(l, 8, 9)

    def units_b(self, c):
        QN, KN, V, QP, KP = (c[k] for k in ("QN", "KN", "V", "QP", "KP"))
        left, pleft, vleft = {}, {}, {}
        for h in range(8):
            left[h], vleft[h] = 4, 4
            if h % 2 == 0:
                pleft[h // 2] = 8
            for s in (CT, LAT):
                box = {}
                for i in range(2):
                    e = h % 2
                    nk = 256 if s == CT else 512
                    nt = nk // 128

                    def ready(h=h):
                        return h in c["rd"] and h // 2 in c["qp"]

                    def need(h=h, s=s):
                        return [c["rd"][h][2], c["qp"][h // 2][1], c["kpr"][:s + 1]]

                    def scores(b, s=s, e=e, i=i, nk=nk, h=h, need=need):
                        o = slice(256 * s + 128 * i, 256 * s + 128 * i + 128)
                        x, y = c["rd"][h][0], c["qp"][h // 2][0]
                        self.mm(b.t[:, 0:nk], QN[:, x, o], KN[:, x, 0:nk], True, False, need(), b.free)
                        self.mm(b.t[:, 0:nk], QP[:, y, e, o], KP[:, 0, 0:nk], False, False)
                        mk = self.mm(b.t[:, 0:nk], QP[:, y, e, o], KP[:, 1, 0:nk], False, True, inc=True)
                        left[h] -= 1
                        pleft[h // 2] -= 1
                        if left[h] == 0:
                            c["qn_s"].give(x, mk)
                        if pleft[h // 2] == 0:
                            c["qp_s"].give(y, mk)
                        return mk

                    def values(ob, pts, marks, h=h, i=i, nt=nt):
                        y = c["rd"][h][1]
                        for k in range(nt):
                            mk = self.mm(ob.t[:, 128 * i:128 * i + 128], V[:, y, k, :], pts[0][:, k, :], k == 0, k == nt - 1,
                                         marks, ob.free, inc=k == nt - 1)
                        vleft[h] -= 1
                        if vleft[h] == 0:
                            c["v_s"].give(y, mk)
                        return mk

                    def gate(ob, mk, s=s, h=h):
                        o = slice(256 * s, 256 * s + 256)
                        yield lambda: h in c["z"]
                        x, zr = c["z"][h]
                        y, free = yield from c["gf_s"].take()
                        yield [mk, zr]
                        gf = c["gf"]
                        d = self.stt(gf, ob.t[:, 0:256], 0.5, c["ZT"][:, x, o], ALU.mult, ALU.mult, mk, zr, free, c["fz"])
                        self.give(ob, d)
                        if s == LAT:
                            c["zt_s"].give(x, d)
                        yield [d]
                        d = yield from self.split(self.Gh[:, h, o], self.Gl[:, h, o], gf, d, self.g_free)
                        c["gf_s"].give(y, d)
                        self.gr[s][h] = d

                    yield dict(ready=ready, need=need, scores=scores, values=values, nk=nk, pair=None, box=box, first=i == 0,
                               vready=lambda: True, gate=gate if i == 1 else None, mask=None, sink=None, mask_rd=None)

    def finish_layer(self, l, streams, nxt):
        self.fence = f = self.now()
        self.place["out", l, 3] = f
        if l == 3:
            self.place["p", 512] = f
        buf = {CT: 8192, LAT: 11264}
        YG = {s: self.F(buf[s], 2, D) for s in streams}
        ss = {s: self.cols(8).rearrange("p (i j) -> p i j", i=2) for s in streams}
        yr, sr = {}, {}
        if len(streams) == 2:
            order = [(CT, 0), (LAT, 0), (CT, 1), (CT, 2), (CT, 3), (LAT, 1), (LAT, 2), (LAT, 3)]
            seq = [(s, j, i) for s, j in order for i in range(2)]
        else:
            seq = [(LAT, j, i) for j, i in self.BY_TILE]
        if l == 0:
            self.spawn(self.ext_rows(), 0.0)
        hr = None
        if nxt is not None:
            hr = self.new_tiles() if l == 3 else self.new_h()
        gr = self.gr
        jobs = {}

        def tile(s, i, nt):
            yield lambda: all((s, i, j) in sr for j in range(4))
            s2 = self.cols(1)
            need = [sr[s, i, j] for j in range(4)] + [yr[s, i, j] for j in range(4)]
            yield need
            t = self.red(s2, ss[s][:, i, :], ALU.add, need)
            rs, t = self.rstd(s2, 1, D, t)
            yield [t]
            x, yg = self.X[:, 2 * s + i, :], YG[s][:, i, :]
            self.xr[2 * s + i] = t = self.stt(x, yg, rs, x, ALU.mult, ALU.add, t, need, self.xr[2 * s + i])
            if nxt is not None:
                yield from self.norm_tile(s, i, YG[s], nt, t)

        def rest(s):
            nt = [None, None]
            ts = [self.spawn(tile(s, i, nt), 0.0) for i in range(2)]
            if nxt is not None and l == 3:
                yield from self.tiles_h(*nxt(s), YG[s], nt)
            yield lambda: all(t.done for t in ts)
            if nxt is not None and l < 3:
                yield from self.make_h(hr, nxt(s), s, YG[s], self.F(buf[s] + 2048, 2, 2, 256), nt, f)

        def tail(s, i, j, b, mk):
            yield [mk]
            o = slice(256 * j, 256 * j + 256)
            yr[s, i, j] = d = self.tt(YG[s][:, i, o], b.t[:, 0:256], self.G[:, s, o], ALU.mult, mk, f, self.g_rd)
            yield [d]
            sr[s, i, j] = a = self.a(b.t[:, 0:256], b.t[:, 0:256], ACT.Square, mk, d, accum=ss[s][:, i, j:j + 1])
            self.give(b, a)
        turn = {s: self.spawn(rest(s), 0.0) for s in streams}
        if l == 3:
            self.w.AHEAD = 600.0
        for s, j, i in seq:
            if j not in jobs:
                jobs[j] = yield from self.w.job(("out", l, j))
            b = yield from self.get(2)
            mk = yield from self.form_b(jobs[j], 0, 256, b.t[:, 0:256], 256 * s + 128 * i, self.Gh, self.Gl,
                                        lambda k, s=s: [gr[s][k]], b.free)
            self.spawn(tail(s, i, j, b, mk), 0.0)
            if s == LAT and i == 1:
                self.w.free(jobs[j], mk)
        self.g_free = [mk]
        if CT in streams:
            yield lambda: turn[CT].done
        yield lambda: len(yr) == 8 * len(streams)
        self.G_free = list(yr.values())
        self.turn = turn[LAT]

    def layer_c(self, l):
        f0 = self.fence
        c = dict(l=l, f0=f0, cell=-1)
        F = self.F
        c.update(QT=F(0, 2, 512), KT=F(1024, 2, 512), VA=F(2048, 2, 4, 258), Y=F(4112, 512), TH=F(4624, 512), RN=F(5136, 512),
                 BC=F(5648, 4, 36), AC=F(5792, 4, 36), MC=F(5936, 4, 36), AL=F(6080, 8, 4), E=F(6112, 2, 4),
                 DT=F(6320, 2, 512), HS=F(7344, 2, 4, 256), KE=F(9392, 2, 3, 128), CS=F(10160, 2, 2, 258), IT=F(11192, 2, 258),
                 NUM=F(11708, 2, 258), TH2=F(12224, 512), ZZ=F(12736, 2, 256), GF=F(13248, 2, 256), TH3=F(13760, 512))
        idb = self.SF[:, 6128:6192].bitcast(BF16)
        mkb = self.SF[:, 6192:6320].bitcast(BF16)
        c["idb"], c["mkb"] = idb, mkb.rearrange("p (d t) -> p d t", d=2)
        A = [F(6320 + 512 * i, 512) for i in range(6)] + [F(9392 + 512 * i, 512) for i in range(5)]
        c.update(rd={}, hs_rd={}, y_s=Slots(1), th_s=Slots(2), zz_s=Slots(1), gf_s=Slots(1), q_s=Slots(2), k_s=Slots(2), v_s=Slots(2),
                 hs_s=Slots(2), gates_rd=None)

        def masks():
            ml = self.dma(self.sp, "mlmask", c["TH"][:, 0:256], self.ins["mlmask"], f0)
            r1 = self.cp(idb, self.ident, f0, self.k_rd)
            c["ones"] = self.mset(c["VA"][:, :, :, 256:257], 1.0, f0)
            yield [ml]
            r2 = self.cp(mkb, c["TH"][:, 0:256], ml, f0)
            c["mask_rd"] = [r1, r2]
        mt = self.spawn(masks(), 0.0)
        self.gr = [[None] * 8, [None] * 8]
        c["masks"] = mt
        cell = self.spawn(self.cells(c), 0.5)
        H = (self.Hh, self.Hl)
        jobs = []
        qb = []
        for s in (CT, LAT):
            if s == LAT:
                yield from self.ada_some(l)
                c["fz"] = yield from self.turned()
            for x in range(2):
                if s == CT:
                    jobs.append((yield from self.w.job((("qc", "kc")[x], 0))))
                    qb.append((yield from self.get(4)))
                mk = yield from self.form_a(jobs[x], 0, 128, qb[x].t[:, 256 * s:256 * s + 256], 256 * s, 256, *H, self.hrd(s, s + 1),
                                            qb[x].free if s == CT else [])
                if s == LAT:
                    self.w.free(jobs[x], mk)
                    self.spawn(self.conv_c(c, 0, x, qb[x], mk), 0.0)
            if s == CT:
                jobs.append((yield from self.w.job(("vc", 0))))
                v, free = yield from c["v_s"].take()
                c["rd"][0] = dict(v=v)
            b, mk = yield from self.prod_b(jobs[2], 256, s)
            self.spawn(self.v_tail(c, 0, v, free, s, b, mk), 0.0)
        self.w.free(jobs[2], mk)
        yield from self.gates_c(c, A)
        yield from self.ada_some(l, 0, 8)
        for j in range(1, 4):
            yield from self.qkv_c(c, j)
            yield from self.ada_some(l, 2 * j - 1, 8)
            yield from self.oz_c(c, j - 1)
            yield from self.ada_some(l, 2 * j, 8)
        yield from self.oz_c(c, 3)
        yield from self.ada_some(l, 7, 8)
        yield lambda: all(known(self.gr[s]) for s in range(2))

    def gates_c(self, c, A):
        job = yield from self.w.job(("gates",))
        b = yield from self.get(4)
        mk = yield from self.form_a(job, 0, 16, b.t[0:16, :], 0, 512, self.Hh, self.Hl, self.hrd(0, 2), b.free)
        self.w.free(job, mk)
        self.spawn(self.gates_tail(c, A, b, mk), 0.0)

    def gates_tail(self, c, A, b, mk):
        l, f0 = c["l"], c["fz"]
        bg = A[0][0:16, 0:1]
        bg_rd = self.dma(self.sp, "bg", bg, self.ins[f"l{l}_b_gate"].rearrange("(a c) -> a c", c=1), f0)
        GT, IG, FG, T1, CM, PM, BN, AN, MN, RM, RG = (A[i] for i in (1, 2, 3, 4, 5, 6, 7, 8, 9, 10, 0))
        zs = [self.mset(a[0:36, :], 0.0, f0, q=self.pool) for a in (IG, FG, AN, MN)]
        z1 = self.mset(RM[0:36, :], 1.0, f0, q=self.pool)
        z1 = self.mset(RM[0:36, 0::128], 0.0, z1, q=self.pool)
        yield [mk, bg_rd]
        t = self.a(GT[0:16, :], b.t[0:16, :], ACT.Identity, mk, bg_rd, f0, bias=bg)
        self.give(b, t)
        z2 = self.mset(RG[0:36, :], 0.0, t, q=self.pool)
        z2 = self.mset(RG[0:36, 0::128], FLOOR, z2, q=self.pool)
        d = [self.dma(self.sp, "g0", IG[0:4, :], GT[0:4, :], t, zs), self.dma(self.sp, "g0", FG[0:4, :], GT[4:8, :], t, zs),
             self.dma(self.sp, "g0", AN[32:36, :], GT[8:12, :], t, zs), self.dma(self.sp, "g0", MN[32:36, :], GT[12:16, :], t, zs)]
        yield d
        b_ = slice(32, 36)
        rev = lambda a, s: a[b_, 256 * s:256 * s + 256][:, ::-1]
        nat = lambda a, s: a[b_, 256 * s:256 * s + 256]
        t = []
        for s in range(2):
            t.append(self.cp(nat(IG, s), rev(AN, s), d, zs))
            t.append(self.cp(nat(FG, s), rev(MN, s), d, zs))
        r = slice(0, 36)
        t = t0 = self.stt(T1[r, :], FG[r, :], -1.0, FG[r, :], ALU.mult, ALU.min, t, f0)
        yield [t]
        t = self.a(T1[r, :], T1[r, :], ACT.Exp, t)
        t = self.a(T1[r, :], T1[r, :], ACT.Ln, t, bias=1.0)
        yield [t]
        t = self.stt(FG[r, :], FG[r, :], 0.0, T1[r, :], ALU.min, ALU.subtract, t)
        t = self.v(lambda e: e.tensor_tensor_scan(CM[r, :], RM[r, :], FG[r, :], 0.0, ALU.mult, ALU.add), CM[r, :], t, z1, f0)
        tb = t = self.tt(IG[r, :], IG[r, :], CM[r, :], ALU.subtract, t)
        t = self.v(lambda e: e.tensor_tensor_scan(PM[r, :], RG[r, :], IG[r, :], FLOOR, ALU.add, ALU.max), PM[r, :], t, z2, f0)
        m = self.cols(4)[r, :]
        tm = self.mset(m[:, 0:1], NEG)
        for p in range(3):
            last = slice(128 * p + 127, 128 * p + 128)
            tm = self.stt(m[:, p + 1:p + 2], PM[r, last], m[:, p:p + 1], CM[r, last], ALU.max, ALU.add, t, tm)
        yield [tm]
        rd = []
        for p in range(4):
            o = slice(128 * p, 128 * p + 128)
            t2 = self.ts(PM[r, o], PM[r, o], m[:, p:p + 1], -1.0, ALU.max, ALU.mult, tm)
            rd.append(t2)
            rd.append(self.ts(FG[r, o], PM[r, o], m[:, p:p + 1], None, ALU.add, None, t2))
        rd.append(self.tt(T1[r, :], PM[r, :], CM[r, :], ALU.subtract, rd))
        yield rd
        out = []
        for dst, src in ((c["RN"], PM), (BN, IG), (AN, FG), (MN, T1)):
            z = self.mset(dst[r, :], 0.0, rd, f0, q=self.pool)
            out.append(self.cp(dst[0:4, :], src[0:4, :], rd, z, tb))
            for s in range(2):
                out.append(self.cp(nat(dst, s), rev(src, s), rd, z, tb))
        b = yield from self.get(2)
        b2 = yield from self.get(1)
        yield out
        pv = b.t[:, 0:432].rearrange("p (a c h) -> p a c h", a=3, c=4)
        for a, src in enumerate((BN, AN, MN)):
            for q in range(4):
                mk = self.tr(pv[:, a, q, :], src[r, 128 * q:128 * q + 128], self.ident[0:36, 0:36], out, b.free)
        for d_ in range(2):
            for h in range(4):
                row = 32 * d_ + h
                rhs = AN[r, (127 if d_ == 0 else 0)::128]
                mk2 = self.mm(b2.t[:, 4 * (4 * d_ + h):4 * (4 * d_ + h) + 4], self.ident[0:36, row:row + 1].to_broadcast([36, 128]),
                              rhs, True, True, out, b2.free, inc=True, cost=213.0)
        yield [mk2]
        t1 = self.a(c["BC"][:, :, :], pv[:, 0], ACT.Copy, mk, f0)
        t2 = self.a(c["AC"][:, :, :], pv[:, 1], ACT.Exp, mk, f0)
        t3 = self.a(c["MC"][:, :, :], pv[:, 2], ACT.Exp, mk, f0)
        self.give(b, t3)
        t4 = self.a(c["AL"][:, :, :], b2.t[:, 0:32].rearrange("p (a b) -> p a b", a=8), ACT.Exp, mk2, f0)
        self.give(b2, t4)
        yield [t4]
        t5 = self.ts(c["AC"][:, :, :], c["AC"][:, :, :], 0.5, None, ALU.mult, None, t2)
        c["gates_rd"] = [out, t1, t3, t4, t5]
        c["tmp_free"] = self.now()

    def conv_c(self, c, j, x, b, mk):
        vc = self.vc["l2_conv"] + 4 * x + j
        w = lambda d: self.VC[:, vc + 8 * d:vc + 8 * d + 1]
        Y, TH = c["Y"], c["TH"]
        x3, y3 = b.t[:, :].rearrange("p (s t) -> p s t", s=2), Y.rearrange("p (s t) -> p s t", s=2)
        yield lambda: c["masks"].done
        _, yfree = yield from c["y_s"].take()
        at, free = yield from c[("q_s", "k_s")[x]].take()
        yield [mk]
        t = self.a(Y, b.t[:, :], ACT.Copy, mk, yfree, c["mask_rd"], c["f0"], scale=w(2))
        yield [t]
        for d in (0, 1, 3, 4):
            sh = d - 2
            o, i = slice(max(0, -sh), 256 - max(0, sh)), slice(max(0, sh), 256 + min(0, sh))
            t = self.stt(y3[:, :, o], x3[:, :, i], w(d), y3[:, :, o], ALU.mult, ALU.add, t)
        self.give(b, t)
        yield [t]
        ta = self.a(TH, Y, ACT.Tanh, t, yfree, scale=0.5)
        yield [ta]
        dst = (c["QT"], c["KT"])[x][:, at]
        td = self.stt(dst, TH, 1.0, Y, ALU.add, ALU.mult, ta, free, c["fz"])
        c["y_s"].give(0, td)
        r = c["rd"].setdefault(j, {})
        r["qk"[x]] = at
        r["qk"[x] + "r"] = td

    def v_tail(self, c, j, v, free, s, b, mk):
        yield lambda: c["masks"].done
        yield [mk]
        t = self.a(c["VA"][:, v, 2 * s:2 * s + 2, 0:256], b.t[:, :].rearrange("p (i v) -> p i v", i=2), ACT.Copy, mk, free, c["ones"])
        self.give(b, t)
        c["rd"][j][f"v{s}"] = t

    def qkv_c(self, c, j):
        for x, key in enumerate(("qc", "kc")):
            job = yield from self.w.job((key, j))
            b = yield from self.get(4)
            mk = yield from self.form_a(job, 0, 128, b.t[:, :], 0, 512, self.Hh, self.Hl, self.hrd(0, 2), b.free)
            self.w.free(job, mk)
            self.spawn(self.conv_c(c, j, x, b, mk), 0.0)
        job = yield from self.w.job(("vc", j))
        v, free = yield from c["v_s"].take()
        c["rd"].setdefault(j, {})["v"] = v
        for s in range(2):
            b, mk = yield from self.prod_b(job, 256, s)
            self.spawn(self.v_tail(c, j, v, free, s, b, mk), 0.0)
        self.w.free(job, mk)

    def cells(self, c):
        kap = 0.25 * 128.0 ** -0.5
        kst = 0.5 * 128.0 ** -0.5
        order = ((0, 1, 2, 3), (1, 0, 3, 2))
        free = dict(dt=[], ke=[], e=[], cs=[[[], []], [[], []]], it=[[], []], num=[[], []])

        def direction(h, hx, d, R, sq, ke, seen):
            QT, VA, HS = c["QT"][:, R["q"]], c["VA"][:, R["v"]], c["HS"][:, hx]
            DT, KE, CS = c["DT"], c["KE"], c["CS"]
            tf = c["tmp_free"]
            row = 32 * d + h
            cr = None
            for p in range(4):
                q = order[d][p]
                o = slice(128 * q, 128 * q + 128)
                va = VA[:, q, 0:257]
                ti = None
                if p > 0:
                    ib = yield from self.get(1)
                    yield [cr]
                    mn = self.mm(ib.t[:, 0:257], QT[:, o], CS[:, d, (p + 1) % 2, 0:257], True, True, cr, ib.free, inc=True)
                    free["cs"][d][(p + 1) % 2] = [mn, cr]
                if p < 3:
                    stb = yield from self.get(1)
                    yield [ke[d][p]]
                    mst = self.mm(stb.t[:, 0:257], KE[:, d, p, :], va, True, True, ke[d][p], stb.free, inc=True)
                    yield [mst]
                    new, old = CS[:, d, p % 2, 0:257], CS[:, d, (p + 1) % 2, 0:257]
                    if p == 0:
                        nr = self.cp(new, stb.t[:, 0:257], mst, free["cs"][d][p % 2], tf)
                    else:
                        nr = self.stt(new, old, c["AL"][:, 4 * d + h, q:q + 1], stb.t[:, 0:257], ALU.mult, ALU.add, mst,
                                      cr, free["cs"][d][p % 2], tf)
                        free["cs"][d][(p + 1) % 2] = [mn, nr]
                    self.give(stb, nr)
                if p > 0:
                    yield [mn]
                    ti = self.a(c["IT"][:, d, 0:257], ib.t[:, 0:257], ACT.Copy, mn, free["it"][d], tf, scale=c["AC"][:, q, row:row + 1])
                    self.give(ib, ti)
                nb = yield from self.get(1)
                mi = self.mm(nb.t[:, 0:257], DT[:, d, o], va, True, True, sq[d], nb.free, inc=True)
                if p < 3:
                    cr = nr
                yield [mi, ti]
                num = c["NUM"][:, d, 0:257]
                if p > 0:
                    t = self.tt(num, c["IT"][:, d, 0:257], nb.t[:, 0:257], ALU.add, mi, ti, free["num"][d], tf)
                    free["it"][d] = [t]
                else:
                    t = self.cp(num, nb.t[:, 0:257], mi, free["num"][d], tf)
                self.give(nb, t)
                dn = self.cols(1)
                t = self.stt(dn, num[:, 256:257], -1.0, num[:, 256:257], ALU.mult, ALU.max, t)
                t = self.tt(dn, dn, c["MC"][:, q, row:row + 1], ALU.max, t)
                t = self.rec(dn, dn, t)
                if q not in seen:
                    t = self.ts(HS[:, q, :], num[:, 0:256], dn, None, ALU.mult, None, t, free["hs"], tf)
                else:
                    t = self.stt(HS[:, q, :], num[:, 0:256], dn, HS[:, q, :], ALU.mult, ALU.add, t, seen[q])
                seen[q] = t
                free["num"][d] = [t]

        for h in range(4):
            keys = ("qr", "kr", "v0", "v1")
            yield lambda: c["gates_rd"] is not None and all(k in c["rd"].get(h, {}) for k in keys)
            R = c["rd"][h]
            QT, KT = c["QT"][:, R["q"]], c["KT"][:, R["k"]]
            DT, KE, E = c["DT"], c["KE"], c["E"]
            rd, g, tf = [[R[k] for k in keys], c["ones"]], c["gates_rd"], c["tmp_free"]
            hx, free["hs"] = yield from c["hs_s"].take()
            sb = yield from self.get(3)
            yield rd
            for q in range(4):
                o = slice(128 * q, 128 * q + 128)
                mks = self.mm(sb.t[:, o], KT[:, o], QT[:, o], True, True, rd, sb.free, inc=True)
            ex = [None, None]

            def decay(d):
                row = 32 * d + h
                b = yield from self.get(1)
                yield g
                self.mm(b.t[:, :], self.ident[0:36, row:row + 1].to_broadcast([36, 128]), c["RN"][0:36, :], True, False, g, b.free)
                mk = self.mm(b.t[:, :], c["idb"], c["mkb"][:, d:d + 1, :].to_broadcast([128, 4, 128]), False, True,
                             c["mask_rd"], inc=True, cost=213.0)
                te = []
                yield [mk, free["dt"]]
                for q in range(4):
                    o = slice(128 * q, 128 * q + 128)
                    te.append(self.a(DT[:, d, o], b.t[:, o], ACT.Exp, mk, free["dt"], tf, bias=c["BC"][:, q, row:row + 1]))
                self.give(b, te)
                yield te
                last = (127 if d == 0 else 0)
                ex[d] = [te, self.cp(E[:, d, :], DT[:, d, last::128], te, free["e"])]
                sq[d] = self.stt(DT[:, d, :], sb.t[:, :], kap, DT[:, d, :], ALU.mult, ALU.mult, mks, ex[d])
            sq = [None, None]
            tasks = [self.spawn(decay(d), 0.0) for d in range(2)]
            yield lambda: all(t.done for t in tasks)
            self.give(sb, sq)
            kb = yield from self.get(1)
            for q in range(4):
                mkk = self.tr(kb.t[:, 128 * q:128 * q + 128], KT[:, 128 * q:128 * q + 128], self.ident, kb.free)
            yield [mkk]
            ke = [[None] * 3, [None] * 3]
            for p in range(3):
                for d in range(2):
                    q = order[d][p]
                    ke[d][p] = self.ts(KE[:, d, p, :], kb.t[:, 128 * q:128 * q + 128], E[:, d, q:q + 1], kst, ALU.mult, ALU.mult,
                                       mkk, ex[d], free["ke"], tf)
            self.give(kb, ke[0][2], ke[1][2])
            free["e"] = [ke]
            seen = {}
            tasks = [self.spawn(direction(h, hx, d, R, sq, ke, seen), 0.0) for d in range(2)]
            yield lambda: all(t.done for t in tasks)
            fr = [(self.pe.name, self.pe.count)]
            free["dt"] = free["ke"] = fr
            for k in ("q", "k", "v"):
                c[k + "_s"].give(R[k], fr)
            c["hs_rd"][h] = (hx, [seen[q] for q in range(4)])
            c["cell"] = h

    def oz_c(self, c, j):
        l = c["l"]
        rs, rt = [None] * 2, [None] * 2
        ths = (c["TH2"], c["TH3"])

        def o_tail(s, b, mk):
            x, free = yield from c["th_s"].take()
            yield lambda: c["gates_rd"] is not None
            tf = c["tmp_free"]
            yield [mk]
            th = ths[x]
            ta = self.a(th, b.t[:, :], ACT.Tanh, mk, free, tf, scale=0.5)
            self.give(b, ta)
            yield lambda: c["cell"] >= j
            hx, hrd = c["hs_rd"][j]
            hs = c["HS"][:, hx, 2 * s:2 * s + 2, :]
            yield [ta, hrd]
            t = self.stt(hs, th.rearrange("p (i v) -> p i v", i=2), 1.0, hs, ALU.add, ALU.mult, ta, hrd)
            c["th_s"].give(x, t)
            ss = self.cols(2)
            _, free = yield from c["zz_s"].take()
            yield [t]
            sq = [self.a(c["ZZ"][:, i, :], hs[:, i, :], ACT.Square, t, free, tf, accum=ss[:, i:i + 1]) for i in range(2)]
            c["zz_s"].give(0, sq)
            yield sq
            rs[s], rt[s] = self.rstd(ss, 2, 1024, sq)

        def z_tail(s, b, mk):
            x, free = yield from c["th_s"].take()
            tf = c["tmp_free"]
            yield [mk]
            th = ths[x]
            ta = self.a(th, b.t[:, :], ACT.Tanh, mk, free, tf, scale=0.5)
            bz = b.t[:, :].rearrange("p (i v) -> p i v", i=2)
            yield lambda: rt[s] is not None
            _, free = yield from c["zz_s"].take()
            yield [ta]
            t = self.stt(c["ZZ"][:, :, :], th.rearrange("p (i v) -> p i v", i=2), 1.0, bz, ALU.add, ALU.mult, ta, free)
            self.give(b, t)
            c["th_s"].give(x, t)
            gt = []
            hx = c["hs_rd"][j][0]
            HS = c["HS"][:, hx]
            yield [rt[s]]
            for i in range(2):
                hs = HS[:, 2 * s + i, :]
                gt.append(self.stt(hs, hs, rs[s][:, i:i + 1], c["ZZ"][:, i, :], ALU.mult, ALU.mult, t, rt[s]))
            c["zz_s"].give(0, gt)
            b = yield from self.get(1)
            yield gt
            for f in range(2):
                for i in range(2):
                    mt = self.tr(b.t[:, 256 * f + 128 * i:256 * f + 128 * i + 128], HS[:, 2 * s + i, 128 * f:128 * f + 128],
                                 self.ident, gt, b.free)
            _, free = yield from c["gf_s"].take()
            yield [mt]
            ev = []
            for f in range(2):
                g = self.vc["l2_g_head"] + 2 * j + f
                ev.append(self.ts(c["GF"][:, f, :], b.t[:, 256 * f:256 * f + 256], self.VC[:, g:g + 1], 0.25, ALU.mult, ALU.mult,
                                  mt, free, tf))
            self.give(b, ev)
            done[s] = mt
            if known(done):
                c["hs_s"].give(hx, done)
            yield ev
            o = slice(256 * s, 256 * s + 256)
            d = yield from self.split(self.Gh[:, 2 * j:2 * j + 2, o], self.Gl[:, 2 * j:2 * j + 2, o], c["GF"][:, :, :], ev, self.g_free)
            c["gf_s"].give(0, d)
            self.gr[s][2 * j] = self.gr[s][2 * j + 1] = d
        done = [None, None]
        for key, tail in (("oc", o_tail), ("zc", z_tail)):
            job = yield from self.w.job((key, j))
            for s in range(2):
                b, mk = yield from self.prod_b(job, 256, s)
                self.spawn(tail(s, b, mk), 0.0)
            self.w.free(job, mk)
        if j == 3:
            self.h_free = [mk]

    def ext_rows(self):
        tab, t34, ev = self.F(4096, 384), self.F(4480, 16), self.F(4608, 384)
        f0 = self.fence
        r = [self.dma(self.sp, "ext", tab[0:34, :], self.ins["onehot"], f0),
             self.dma(self.sp, "ext", t34[0:32, :], self.ins["rel_bias_2"], f0),
             self.dma(self.sp, "ext", t34[32:34, :], self.ins["tabrows"], f0)]
        b = yield from self.get(2)
        yield r
        mk = self.mm(b.t[0:16, 0:384], t34[0:34, :], tab[0:34, :], True, True, r, self.fence, b.free, inc=True)
        yield [mk]
        t = self.cp(ev[0:16, :], b.t[0:16, 0:384], mk, self.fence)
        self.give(b, t)
        self.ext = self.nc.dram_tensor("ext_rows", (16, 128, 384), F32).ap()
        src = ev[0:16, :].rearrange("p (a c) -> p a c", a=1).to_broadcast([16, 128, 384])
        self.ext_rd = self.dma(self.sp, "extw", self.ext, src, t)

    def second(self):
        f0 = self.fence = self.now()
        F, X, K, i = self.F, self.X, self.K, self.ins
        Xf = X[:, 0:2, :].rearrange("p a b -> p (a b)")
        c = dict(f0=f0, at=set(), gf_s=Slots(1), nq_s=Slots(2), sq_s=Slots(1), kw_s=Slots(1))
        c["Q"] = F(0, 12, 256)
        c["KD"] = F(3072, 3, 2, 256)
        c["CK"] = F(4608, 4, 256)
        c["VN"] = F(5632, 3, 2, 128)
        c["CV"] = F(6400, 2, 2, 256)
        c["strip"] = F(7424, 16, 256)
        c["NQ"] = [Xf[:, 0:512], Xf[:, 512:1024]]
        ST = Xf[:, 1024:2048].rearrange("p (w k m) -> p w k m", w=2, k=16)
        aS = self.adaS[:, :, :].rearrange("p a b -> p (a b)")
        gP = self.gp[:, :, :].rearrange("p a b -> p (a b)")
        cS = self.CS[:, :, :].rearrange("p a b -> p (a b)")
        bD = self.band[:, :, :].rearrange("p a b -> p (a b)").bitcast(F32)
        GN = self.VC[:, 142:154]
        c["GS"] = aS[:, 154:202].rearrange("p (i g) -> p i g", i=2)
        c["CN"] = aS[:, 202:218].rearrange("p (i g) -> p i g", i=2)
        LF = aS[:, 218:234].rearrange("p (i g) -> p i g", i=2)
        L1 = aS[:, 234:250].rearrange("p (i g) -> p i g", i=2)
        c["NCR"] = bD[:, 0:256]
        c["KC"] = bD[:, 256:320].rearrange("p (g n) -> p g n", g=2)
        c["VM"] = cS[:, 128:256].rearrange("p (g d) -> p g d", g=2)
        HID = cS[:, 0:128].rearrange("p (c m) -> p c m", c=2)
        OS = gP[:, 0:256]
        W2 = gP[:, 256:512].rearrange("p (w c d) -> p w c d", w=2, c=2)
        KCN = bD[:, 320:448].rearrange("p (u d) -> p u d", u=2)
        tri, one, selC = K[:, 128:256], K[:, 256:384], K[:, 384:448]
        caus, rmask = K[:, 448:704], K[:, 704:705]
        k2 = self.dma(self.sp, "k2", K[:, 128:705], i["konst2"], f0)
        FB, SK = self.sink[:, 40:48], self.sink[:, 32:40]
        w2 = self.dma(self.sp, "cw2", W2, i["cmp_w2_2"][0].rearrange("w (c p) d -> p w c d", p=128), f0)
        c["SK"], c["GN"], c["gn_rd"] = SK, GN, self.v2_rd
        c["sk_rd"] = self.sink_rd
        c["pos"], c["pos_rd"] = self.VC[:, 110:142], self.v2_rd
        c.update(ST=ST, HID=HID, OS=OS, W2=W2, w2_rd=w2, KCN=KCN, tri=tri, one=one, selC=selC, caus=caus, rmask=rmask, k2=k2, LF=LF,
                 L1=L1, FB=FB, fb=self.sink_rd)
        c["fz"] = f0
        MG = self.G[:, :, :].rearrange("p a (b t) -> p (a b) t", t=256)
        c["MG"] = MG
        c.update(kd_rd=[None] * 3, q_rd=[None] * 12, ck_rd=[None] * 4, cv_rd=[None] * 2, mg_rd={}, hid=[])
        c["GF"] = self.G[:, :, :].rearrange("p a b -> p (a b)")
        self.br = [[None] * 4 for _ in range(3)]
        mk = yield from self.first_2(c)
        self.fence = [f0, self.hr[LAT], mk]
        c["strip_rd"] = []
        self.spawn(self.strips(c, self.fence), 0.0)
        att = self.spawn(self.attention(self.units_2(c), at=11520, nsm=4, npt=3, wide=258, kts=2), 0.5)
        yield from self.proj_2(c)
        yield lambda: att.done
        yield from self.merge_2(c)
        yield from self.ffn(c)

    def columns_2(self):
        f0, i = self.fence, self.ins
        rows, prow = self.X[:, 0, 0:128], self.X[:, 0, 128:256]
        vec = self.dma(self.sp, "vec2", rows[0:110, :], i["vecs2"][0:110], f0)
        pr = self.dma(self.sp, "pos", prow[0:32, :], i["vecs2"][110:142], f0)
        b = yield from self.get(2)
        yield [vec, pr]
        self.tr(b.t[:, 0:110], rows[0:110, :], self.ident[0:110, 0:110], vec, b.free)
        mk = self.tr(b.t[:, 128:160], prow[0:32, :], self.ident[0:32, 0:32], pr)
        yield [mk]
        VC = self.VC
        v2 = self.cp(VC[:, 0:110], b.t[:, 0:110], mk, f0)
        ps = self.cp(VC[:, 110:142], b.t[:, 128:160], mk, f0)
        g1 = self.ts(VC[:, 142:148], b.t[:, 104:110], 0.125, None, ALU.mult, None, mk, f0)
        g2 = self.cp(VC[:, 148:154], b.t[:, 104:110], mk, f0)
        self.give(b, g2)
        self.v2_rd = [v2, ps, g1, g2]

    def strips(self, c, need):
        yield need
        for h in range(16):
            src = bass.AP(self.ext.tensor, self.ext.offset + 128 * 384 * h + 127, [[383, 128], [1, 256]])
            c["strip_rd"].append(self.dma(self.sp, "strip", c["strip"][:, h, :], src, need, self.ext_rd))

    def first_2(self, c):
        jobs, banks = {}, {}
        for i in range(2):
            for c0 in (512, 768, 1024):
                if i == 0:
                    jobs[c0] = yield from self.w.job(("p", c0))
                    banks[c0] = yield from self.get(4)
                job, b = jobs[c0], banks[c0]
                mk = yield from self.form_b(job, 0, 256, b.t[:, 256 * i:256 * i + 256], 256 + 128 * i, self.Hh, self.Hl,
                                            lambda k, i=i: [self.hr[LAT][k][i]], b.free)
                if i == 1:
                    self.w.free(job, mk)
                    if c0 == 512:
                        last = mk
                        self.spawn(self.stage(c, b, mk), 0.0)
                    else:
                        self.spawn(self.kv_tail(c, (c0 - 768) // 256, 7, b, mk), 0.0)
        self.w.AHEAD = Weights.AHEAD
        return last

    def nat_2(self, c0):
        job = yield from self.w.job(("p", c0))
        b, mk = yield from self.prod_b(job, 256, LAT)
        self.w.free(job, mk)
        return b, mk

    def heads_norm(self, c, src, n, *need):
        ss = self.cols(2 * n)
        _, free = yield from c["sq_s"].take()
        sq = self.F(13576, 512)[:, 0:2 * n * 64]
        sv = sq.rearrange("p (i n d) -> p (i n) d", i=2, d=64)
        yield [*need]
        t = self.a(sq.rearrange("p (i w) -> p i w", i=2), src, ACT.Square, *need, free, c["fz"])
        yield [t]
        t = self.red(ss, sv, ALU.add, t)
        c["sq_s"].give(0, t)
        rs, t = self.rstd(ss, 2 * n, 64, t)
        yield [t]
        return rs, t

    def q_2(self, c, c0, dst, gain, key, ks):
        b, mk = yield from self.nat_2(c0)
        self.spawn(self.q_tail(c, dst, gain, key, ks, b, mk), 0.0)

    def q_tail(self, c, dst, gain, key, ks, b, mk):
        x, free = yield from c["nq_s"].take()
        NQ = c["NQ"][x]
        yield [mk]
        t = self.a(NQ, b.t[:, :], ACT.Copy, mk, free, c["fz"])
        self.give(b, t)
        rs, tr = yield from self.heads_norm(c, NQ.rearrange("p (i w) -> p i w", i=2), 4, t)
        nv = NQ.rearrange("p (g d) -> p g d", d=64)
        tn = self.tt(nv, nv, rs.rearrange("p (g a) -> p g a", a=1).to_broadcast([128, 8, 64]), ALU.mult, tr, t)
        b = yield from self.get(1)
        yield [tn]
        for p in range(2):
            for i in range(2):
                mk = self.tr(b.t[:, 256 * p + 128 * i:256 * p + 128 * i + 128], NQ[:, 256 * i + 128 * p:256 * i + 128 * p + 128],
                             self.ident, tn, b.free)
        c["nq_s"].give(x, mk)
        yield [mk]
        t = self.a(dst, b.t[:, :].rearrange("p (a t) -> p a t", a=2), ACT.Copy, mk, c["fz"], c["gn_rd"], scale=c["GN"][:, gain:gain + 1])
        self.give(b, t)
        for k in ks:
            c[key][k] = t

    def kv_2(self, c, k, c0, gain):
        b, mk = yield from self.nat_2(c0)
        self.spawn(self.kv_tail(c, k, gain, b, mk), 0.0)

    def kv_tail(self, c, k, gain, b, mk):
        kd, vn = c["KD"][:, k], c["VN"][:, k]
        x, free = yield from c["nq_s"].take()
        NQ = c["NQ"][x]
        b3 = b.t[:, :].rearrange("p (i w) -> p i w", i=2)
        kn = NQ[:, 0:256].rearrange("p (i w) -> p i w", i=2)
        yield [mk]
        t = self.a(kn, b3[:, :, 0:128], ACT.Copy, mk, free, c["fz"])
        t2 = self.a(vn, b3[:, :, 128:256], ACT.Copy, mk, c["fz"])
        self.give(b, t, t2)
        rs, tr = yield from self.heads_norm(c, kn, 2, t)
        _, free = yield from c["kw_s"].take()
        tn = []
        kw = c["GF"][:, 0:512]
        for u in range(2):
            o = kw.rearrange("p (g u d) -> p g u d", u=2, d=64)[:, :, u, :]
            tn.append(self.tt(o, NQ[:, 0:256].rearrange("p (g d) -> p g d", d=64),
                              rs.rearrange("p (g a) -> p g a", a=1).to_broadcast([128, 4, 64]), ALU.mult, tr, t, free, c["fz"]))
        c["nq_s"].give(x, tn)
        b = yield from self.get(1)
        yield tn
        for g in range(2):
            for i in range(2):
                mk = self.tr(b.t[:, 256 * g + 128 * i:256 * g + 128 * i + 128], kw[:, 256 * i + 128 * g:256 * i + 128 * g + 128],
                             self.ident, tn, b.free)
        c["kw_s"].give(0, mk)
        yield [mk]
        t = self.a(kd, b.t[:, :].rearrange("p (a t) -> p a t", a=2), ACT.Copy, mk, c["fz"], c["gn_rd"], scale=c["GN"][:, gain:gain + 1])
        self.give(b, t)
        c["kd_rd"][k] = [t, t2]

    def small_2(self, c):
        job = yield from self.w.job(("small",))
        b = yield from self.get(4)
        mk = yield from self.form_a(job, 0, 32, b.t[0:32, 0:256], 256, 256, self.Hh, self.Hl, self.hrd(1, 2), b.free)
        self.w.free(job, mk)
        self.spawn(self.small_tail(c, b, mk), 0.0)

    def small_tail(self, c, b, mk):
        R = c["GF"][0:32, 512:768]
        yield [mk]
        t = self.a(R, b.t[0:32, 0:256], ACT.Copy, mk, c["fz"])
        self.give(b, t)
        b = yield from self.get(1)
        yield [t]
        for i in range(2):
            mk = self.tr(b.t[:, 32 * i:32 * i + 32], R[:, 128 * i:128 * i + 128], self.ident[0:32, 0:32], t, b.free)
        c["r_free"] = [mk]
        yield [mk]
        bv = b.t[:, 0:64].rearrange("p (i g) -> p i g", i=2)
        GS, LF, L1, CN, NCR = c["GS"], c["LF"], c["L1"], c["CN"], c["NCR"]
        t = self.a(GS, bv[:, :, 0:24], ACT.Tanh, mk, c["fz"], scale=0.5)
        yield [t]
        t1 = self.tt(LF, bv[:, :, 24:32], c["FB"].rearrange("p (a g) -> p a g", a=1).to_broadcast([128, 2, 8]), ALU.add, mk, c["fb"], t, c["fz"])
        self.give(b, t1)
        t = self.ts(GS, GS, 1.0, 0.5, ALU.add, ALU.mult, t)
        g0 = GS[:, 0, 0::3]
        c["gs_rd"] = self.ts(g0, g0, c["rmask"], None, ALU.mult, None, t, c["k2"])
        t = self.stt(L1, LF, -1.0, LF, ALU.mult, ALU.min, t1)
        yield [t]
        t = self.a(L1, L1, ACT.Exp, t)
        t = self.a(L1, L1, ACT.Ln, t, bias=1.0)
        yield [t]
        t = self.stt(LF, LF, 0.0, L1, ALU.min, ALU.subtract, t)
        b = yield from self.get(1)
        yield [t]
        tri, one = c["tri"], c["one"]
        cn, cr = b.t[:, 0:16].rearrange("p (i g) -> p i g", i=2), b.t[0:8, 128:384]
        self.mm(cn[:, 0], tri, LF[:, 0], True, True, t, c["k2"], b.free)
        self.mm(cn[:, 1], one, LF[:, 0], True, False)
        self.mm(cn[:, 1], tri, LF[:, 1], False, True)
        self.mm(cr[:, 0:128], LF[:, 0], tri, True, True)
        self.mm(cr[:, 128:256], LF[:, 0], one, True, False)
        mk = self.mm(cr[:, 128:256], LF[:, 1], tri, False, True, inc=True)
        yield [mk]
        t = self.cp(CN, cn, mk, c["fz"])
        t2 = self.ts(NCR[0:8, :], cr, -1.0, None, ALU.mult, None, mk, c["fz"])
        self.give(b, t, t2)
        c["cn_rd"] = [t, t2]

    def stage(self, c, b, mk):
        x, free = yield from c["nq_s"].take()
        NQ = c["NQ"][x]
        yield [mk]
        t = self.a(NQ, b.t[:, :], ACT.Copy, mk, free, c["fz"])
        self.give(b, t)
        b = yield from self.get(1)
        yield [t]
        for w in range(2):
            for i in range(2):
                mk = self.tr(b.t[:, 256 * w + 128 * i:256 * w + 128 * i + 128], NQ[:, 256 * i + 128 * w:256 * i + 128 * w + 128],
                             self.ident, t, b.free)
        c["nq_s"].give(x, mk)
        yield [mk]
        ST = c["ST"]
        st = [self.mset(ST[:, :, :, 31:32], 0.0, c["fz"])]
        for w in range(2):
            for g in range(2):
                for e in range(2):
                    src = b.t[64 * g:64 * g + 64, 256 * w:256 * w + 256]
                    src = bass.AP(src.tensor, src.offset + e, [src.ap[0], [2, 16], [16, 15]])
                    st.append(self.cp(ST[64 * e:64 * e + 64, w, :, 15 * g:15 * g + 15], src, mk, c["fz"]))
            st.append(self.cp(ST[:, w, :, 30:31], c["pos"][:, 16 * w:16 * w + 16].rearrange("p (k a) -> p k a", a=1), c["pos_rd"], c["fz"]))
        self.give(b, st)
        c["st_rd"] = st

    def hid_2(self, c, w):
        yield lambda: "st_rd" in c
        st = c["st_rd"]
        b = yield from self.get(4)
        for h in range(2):
            job = yield from self.w.job(("w1", w, h))
            yield [st]
            for k in range(8):
                q = k % 4
                yield [job.loaded(k)]
                mk = self.mm(b.t[32 * q:32 * q + 32, 0:256], c["ST"][:, w, 8 * h + k, :], job.raw(k), h == 0 and k < 4,
                             h == 1 and k >= 4, job.loaded(k), st, b.free, inc=k == 7, cost=128.0)
            self.w.free(job, mk)
        c["hid"].append(self.spawn(self.hid_tail(c, w, b, mk, c["hid"][-1] if c["hid"] else None), 0.0))

    def hid_tail(self, c, w, b, mk, prev):
        HID, OS, KCN = c["HID"], c["OS"], c["KCN"]
        yield lambda: prev is None or prev.done
        yield [mk]
        t = self.a(OS, b.t[:, 0:256], ACT.Copy, mk, c.get("os_free"), c["fz"])
        self.give(b, t)
        b = yield from self.get(1)
        yield [t]
        for q in range(2):
            mk = self.mm(b.t[:, 64 * q:64 * q + 64], OS[:, 128 * q:128 * q + 128], c["selC"], True, True, t, c["k2"], b.free, inc=True)
        c["os_free"] = [mk]
        yield [mk]
        t = self.a(HID, b.t[:, 0:128].rearrange("p (c m) -> p c m", c=2), ACT.Gelu_apprx_tanh, mk, c.get("hid_free"), c["fz"])
        self.give(b, t)
        b = yield from self.get(1)
        yield [t]
        for g in range(2):
            for q in range(2):
                mk = self.mm(b.t[0:32, 64 * g:64 * g + 64], HID[:, q, 32 * g:32 * g + 32], c["W2"][:, w, q, :], q == 0, q == 1,
                             t, c["w2_rd"], b.free, inc=True)
        c["hid_free"] = [mk]
        yield [mk]
        bv = b.t[0:32, 0:128].rearrange("p (g d) -> p g d", g=2)
        if w == 1:
            t = self.cp(c["VM"][0:32], bv, mk, c["fz"])
            self.give(b, t)
            c["vm_rd"] = t
            return
        kn = OS[0:32, 0:128].rearrange("p (g d) -> p g d", g=2)
        t = self.cp(kn, bv, mk, c["os_free"])
        self.give(b, t)
        _, free = yield from c["sq_s"].take()
        sq = self.F(13576, 128)[0:32, :].rearrange("p (g d) -> p g d", g=2)
        yield [t]
        t1 = self.a(sq, kn, ACT.Square, t, free, c["fz"])
        yield [t1]
        ss = self.cols(2)[0:32, :]
        t1 = self.red(ss, sq, ALU.add, t1)
        c["sq_s"].give(0, t1)
        t1 = self.ts(ss, ss, 1.0 / 64, EPS, ALU.mult, ALU.add, t1)
        t1 = self.tt(ss, ss, self.mhalf[0:32, 0:2], ALU.pow, t1, self.mhalf_rd, q=self.pool)
        b = yield from self.get(1)
        mks = []
        for g in range(2):
            yield [t1, mks]
            tn = [self.ts(KCN[0:32, u, :], kn[:, g], ss[:, g:g + 1], None, ALU.mult, None, t1, t, mks, c["fz"]) for u in range(2)]
            yield tn
            mks = self.tr(b.t[:, 32 * g:32 * g + 32], KCN[0:32, :, :].rearrange("p u d -> p (u d)"), self.ident[0:32, 0:32], tn, b.free)
        c["os_free"] = [mks]
        yield [mks]
        c["kc_rd"] = self.a(c["KC"], b.t[:, 0:64].rearrange("p (g n) -> p g n", g=2), ACT.Copy, mks, c["gn_rd"], c["fz"],
                            scale=c["GN"][:, 7:8])
        self.give(b, c["kc_rd"])

    def proj_2(self, c):
        Q, CK, CV = c["Q"], c["CK"], c["CV"]
        yield from self.small_2(c)
        yield from self.hid_2(c, 0)
        yield from self.hid_2(c, 1)
        for h in range(2):
            yield from self.q_2(c, 256 * h, Q[:, 2 * h:2 * h + 2, :], 0, "q_rd", (2 * h, 2 * h + 1))
        yield from self.kv_2(c, 2, 1816, 9)
        for h in range(2):
            yield from self.q_2(c, 1304 + 256 * h, Q[:, 4 + 2 * h:6 + 2 * h, :], 2, "q_rd", (4 + 2 * h, 5 + 2 * h))

        def cv_tail(h, b, mk):
            yield [mk]
            c["cv_rd"][h] = t = self.a(CV[:, h], b.t[:, :].rearrange("p (i w) -> p i w", i=2), ACT.Copy, mk, c["fz"])
            self.give(b, t)
        for h in range(2):
            yield from self.q_2(c, 2072 + 256 * h, Q[:, 8 + 2 * h:10 + 2 * h, :], 4, "q_rd", (8 + 2 * h, 9 + 2 * h))
            yield from self.q_2(c, 2584 + 256 * h, CK[:, 2 * h:2 * h + 2, :], 11, "ck_rd", (2 * h, 2 * h + 1))
            b, mk = yield from self.nat_2(3096 + 256 * h)
            self.spawn(cv_tail(h, b, mk), 0.0)

        def mg_tail(k, d, n, b, mk):
            yield [mk]
            yield lambda: known(c["kd_rd"]) and "r_free" in c
            t = self.a(c["MG"][:, 2 * k:2 * k + 2, :], b.t[:, :].rearrange("p (a t) -> p a t", a=2), ACT.Tanh, mk, c["fz"],
                       c["kw_s"].free[0][1], c["r_free"], scale=0.5)
            self.give(b, t)
            c["mg_rd"][d, n] = (c["MG"][:, 2 * k:2 * k + 2, :], t)
        for k, (d, n) in enumerate(((0, 0), (0, 1), (0, 2), (1, 0))):
            b, mk = yield from self.merge_gate(d, n)
            self.spawn(mg_tail(k, d, n, b, mk), 0.0)
        yield lambda: len(c["mg_rd"]) == 4

    def merge_gate(self, d, n):
        job = yield from self.w.job(("merge", d, n))
        b = yield from self.get(4)
        for f in range(2):
            mk = yield from self.form_a(job, 128 * f, 128, b.t[:, 256 * f:256 * f + 256], 256, 256, self.Hh, self.Hl,
                                        self.hrd(1, 2), b.free)
        self.w.free(job, mk)
        return b, mk

    def units_2(self, c):
        Q, KD, CK, VN, CV, strip, GS = (c[k] for k in ("Q", "KD", "CK", "VN", "CV", "strip", "GS"))
        Gh = self.Gh[:, :, :].rearrange("p a b -> p (a b)")
        Gl = self.Gl[:, :, :].rearrange("p a b -> p (a b)")
        c["Bh"] = Gh[:, 0:3072].rearrange("p (n t) -> p n t", n=12)
        c["Bl"] = Gl[:, 0:3072].rearrange("p (n t) -> p n t", n=12)
        gfs = self.F(12552 + 768, 256)
        for br, name in enumerate("abc"):
            for t in range(4):
                box = {}
                kinds = ("cmp", "slc", "win") if br == 0 else (("swa",) if br == 1 else ("fox",))
                for i in range(2):
                    for kind in kinds:
                        for e in range(2):
                            g, h = t // 2, 2 * t + e
                            if kind == "cmp":
                                nk = 7 if i == 0 else 15
                            else:
                                nk = 128 * (i + 1)
                            r = slice(64 * e, 64 * e + 64)

                            def need(kind=kind, t=t, br=br):
                                k = {"slc": 0, "win": 1, "swa": 2}
                                return [c["q_rd"][4 * br + t], c.get("kc_rd") if kind == "cmp" else [c["ck_rd"][t], c.get("cn_rd")]
                                        if kind == "fox" else c["kd_rd"][k[kind]]]

                            def ready(need=need):
                                return known(need()) and "cn_rd" in c and len(c["strip_rd"]) == 16

                            def vready(kind=kind, t=t):
                                return known([c.get("vm_rd") if kind == "cmp" else c["cv_rd"][t // 2] if kind == "fox" else 0])

                            def scores(b, kind=kind, i=i, g=g, h=h, t=t, r=r, nk=nk, br=br):
                                q = Q[r, 4 * br + t, 128 * i:128 * i + 128]
                                need = [c["q_rd"][4 * br + t], b.free]
                                if kind == "cmp":
                                    return self.mm(b.t[:, 0:nk], q, c["KC"][r, g, 0:nk], True, True, need, c["kc_rd"], inc=True)
                                if kind == "fox":
                                    self.mm(b.t[:, 0:nk], q, CK[r, t, 0:nk], True, False, need, c["ck_rd"][t])
                                    return self.mm(b.t[:, 0:nk], self.ident[0:8, h:h + 1].to_broadcast([8, 128]), c["NCR"][0:8, 0:nk],
                                                   False, True, c["cn_rd"], inc=True)
                                k = {"slc": 0, "win": 1, "swa": 2}[kind]
                                return self.mm(b.t[:, 0:nk], q, KD[r, k, g, 0:nk], True, True, need, c["kd_rd"][k], inc=True)

                            def values(ob, pts, marks, kind=kind, kinds=kinds, i=i, g=g, t=t, br=br, nk=nk):
                                first, final = kind == kinds[0], kind == kinds[-1]
                                nt = max(1, nk // 128)
                                for k in range(nt):
                                    for e2 in range(2):
                                        if kind == "cmp":
                                            v, rd = c["VM"][0:nk, g, :], c["vm_rd"]
                                        elif kind == "fox":
                                            v, rd = CV[:, t // 2, k, 128 * (t % 2) + 64 * e2:128 * (t % 2) + 64 * e2 + 64], c["cv_rd"][t // 2]
                                        else:
                                            kk = {"slc": 0, "win": 1, "swa": 2}[kind]
                                            v, rd = VN[:, kk, k, 64 * g:64 * g + 64], c["kd_rd"][kk]
                                        mk = self.mm(ob.t[64 * e2:64 * e2 + 64, 128 * i:128 * i + 128], v, pts[e2][:, k, :],
                                                     first and k == 0, final and k == nt - 1, marks[e2], rd, ob.free, inc=k == nt - 1)
                                return mk

                            def gate(ob, mk, t=t, br=br):
                                n = 4 * br + t
                                x, free = yield from c["gf_s"].take()
                                yield [mk]
                                d = self.a(gfs, ob.t[:, 0:256], ACT.Copy, mk, free, c["fz"])
                                self.give(ob, d)
                                yield [d]
                                d2 = yield from self.split(c["Bh"][:, n, :], c["Bl"][:, n, :], gfs, d, self.g_free)
                                c["gf_s"].give(x, d2)
                                self.br[br][t] = d2

                            shift, gc = None, None
                            if kind == "fox":
                                mask = c["caus"][:, 128 - 128 * i:256]
                                shift = c["CN"][:, i, h:h + 1]
                            elif kind == "cmp":
                                mask = strip[:, h, 159::16] if i == 0 else strip[:, h, 31::16]
                            else:
                                mask = strip[:, 8 * br + h, 128 - 128 * i:256]
                            if br == 0:
                                gc = GS[:, i, 3 * h + kinds.index(kind):3 * h + kinds.index(kind) + 1]
                            sink = c["SK"][:, h:h + 1] if br == 1 else None
                            yield dict(ready=ready, need=need, scores=scores, values=values, nk=nk, pair=e, mask=mask, box=box,
                                       first=i == 0 and kind == kinds[0], vready=vready,
                                       gate=gate if i == 1 and kind == kinds[-1] else None,
                                       mask_rd=lambda: [c["strip_rd"], c["sk_rd"], c["k2"], c["cn_rd"]], gate_rd=lambda: c["gs_rd"],
                                       gate_known=lambda: "gs_rd" in c, shift=shift, sink=sink, gate_col=gc)

    def merge_2(self, c):
        fz = self.now()
        self.place["out2", 3] = fz
        MTh, MTl = self.Rr(0, 8, 256), self.Rr(2048, 8, 256)
        ACC, TMP, TH = self.F(4096, 2, 512), self.F(5120, 2, 512), self.F(6144, 2, 512)
        acc_s, tmp_s, th_s = Slots(2), Slots(2), Slots(2)
        mt = [None] * 8
        state = {}

        def th_tail(d, n, b, mk):
            x, free = yield from th_s.take()
            yield [mk]
            th = TH[:, x].rearrange("p (a t) -> p a t", a=2)
            t = self.a(th, b.t[:, :].rearrange("p (a t) -> p a t", a=2), ACT.Tanh, mk, free, fz, scale=0.5)
            self.give(b, t)
            c["mg_rd"][d, n] = (th, t, x)

        def branch_tail(d, n, b, mk, prev):
            yield lambda: (d, n) in c["mg_rd"] and (prev is None or prev.done)
            th, tr, *x = c["mg_rd"][d, n]
            if n == 0:
                state[d] = yield from acc_s.take()
            at, free = state[d]
            acc = ACC[:, at].rearrange("p (a t) -> p a t", a=2)
            bv = b.t[:, :].rearrange("p (a t) -> p a t", a=2)
            yield [tr, mk]
            if n == 0:
                t = ta = self.stt(acc, th, 1.0, bv, ALU.add, ALU.mult, tr, mk, free, fz)
                self.give(b, t)
            else:
                y, free = yield from tmp_s.take()
                tmp = TMP[:, y].rearrange("p (a t) -> p a t", a=2)
                t = self.stt(tmp, th, 1.0, bv, ALU.add, ALU.mult, tr, mk, free, fz)
                self.give(b, t)
                ta = self.tt(acc, acc, tmp, ALU.add, t, state[d, "t"])
                tmp_s.give(y, ta)
            if x:
                th_s.give(x[0], t)
            state[d, "t"] = ta
            if n == 2:
                o = slice(2 * d, 2 * d + 2)
                yield [ta]
                t = self.a(MTh[:, o, :], acc, ACT.Copy, ta, fz, scale=0.5)
                yield [t]
                t = self.stt(MTl[:, o, :], acc, 0.5, MTh[:, o, :], ALU.mult, ALU.subtract, t, ta, fz)
                acc_s.give(at, t)
                mt[2 * d] = mt[2 * d + 1] = t
        prev = None
        for d in range(4):
            for n in range(3):
                if (d, n) not in c["mg_rd"]:
                    b, mk = yield from self.merge_gate(d, n)
                    self.spawn(th_tail(d, n, b, mk), 0.0)
                job = yield from self.w.job(("branch", d, n))
                b = yield from self.get(4)
                Bh, Bl = c["Bh"][:, 4 * n:4 * n + 4, :], c["Bl"][:, 4 * n:4 * n + 4, :]
                for f in range(2):
                    mk = yield from self.form_a(job, 128 * f, 128, b.t[:, 256 * f:256 * f + 256], 0, 256, Bh, Bl,
                                                lambda k, n=n: [self.br[n][k]], b.free)
                self.w.free(job, mk)
                prev = self.spawn(branch_tail(d, n, b, mk, prev), 0.0)
        self.h_free = [mk]

        hr = self.new_tiles()
        nt, xn, V2 = [None, None], self.F(4096, 2, D), self.VC
        xr = {}

        def out_tail(i, j, b, mk):
            yield [mk]
            xs = self.X[:, 2 + i, 256 * j:256 * j + 256]
            xr[i, j] = self.tt(xs, xs, b.t[:, 0:256], ALU.add, mk, self.xr[2 + i])
            self.give(b, xr[i, j])

        def tile(i):
            yield lambda: all((i, j) in xr for j in range(4))
            self.xr[2 + i] = [xr[i, j] for j in range(4)]
            yield from self.norm_tile(LAT, i, xn, nt, mt)
        ts = [self.spawn(tile(i), 0.0) for i in range(2)]
        at = self.vc["norm_ffn"]
        self.turn = self.spawn(self.tiles_h(lambda kt: V2[:, at + kt:at + kt + 1], lambda: [self.v2_rd], xn, nt), 0.0)
        jobs = {}
        self.w.AHEAD = 100.0
        for j, i in self.BY_TILE:
            if j not in jobs:
                jobs[j] = yield from self.w.job(("out2", j))
            b = yield from self.get(2)
            mk = yield from self.form_b(jobs[j], 0, 256, b.t[:, 0:256], 128 * i, MTh, MTl, lambda k: [mt[k]], b.free)
            self.spawn(out_tail(i, j, b, mk), 0.0)
            if i == 1:
                self.w.free(jobs[j], mk)
        yield lambda: all(t.done for t in ts) and self.turn.done
        self.w.AHEAD = Weights.AHEAD

    def ffn(self, c):
        vc, V2, hr = self.vc, self.VC, self.hr
        FTh, FTl = self.Rr(0, 3, 2, 256), self.Rr(1536, 3, 2, 256)
        fz = [hr[LAT], self.now()]
        Yv = self.F(4096, 2, 2, 256)
        y_s, ft_s, ft = Slots(2), Slots(3), {}
        acc = []
        for _ in range(4):
            acc.append((yield from self.get(1)))
        V = lambda name, k: V2[:, vc[name] + k:vc[name] + k + 1]
        st = {}

        def gate_tail(k, b, mk):
            x, free = yield from y_s.take()
            Y = Yv[:, x]
            yield [mk]
            ts = []
            for f in range(2):
                m = 2 * k + f
                p = b.t[:, 256 * f:256 * f + 256]
                ts.append(self.a(Y[:, f, :], p, ACT.Identity, mk, free, fz, scale=V("conv_w", 44 + m), bias=V("conv_b", m)))
            tl = []
            yield ts
            for f in range(2):
                m = 2 * k + f
                p = b.t[:, 256 * f:256 * f + 256]
                t1 = self.stt(Y[:, f, 1:256], p[:, 0:255], V("conv_w", 22 + m), Y[:, f, 1:256], ALU.mult, ALU.add, ts)
                tl.append(self.stt(Y[:, f, 2:256], p[:, 0:254], V("conv_w", m), Y[:, f, 2:256], ALU.mult, ALU.add, t1))
            self.give(b, tl)
            yield tl
            st[k] = (x, self.a(Y, Y, ACT.Gelu_apprx_tanh, tl))

        def up_tail(k, b, mk):
            yield lambda: k in st
            x, tg = st[k]
            Y = Yv[:, x]
            yield [tg, mk]
            t = self.tt(Y, Y, b.t[:, :].rearrange("p (f t) -> p f t", f=2), ALU.mult, tg, mk)
            self.give(b, t)
            z, free = yield from ft_s.take()
            yield [t]
            t = yield from self.split(FTh[:, z], FTl[:, z], Y, t, free, fz)
            ft[k] = (z, t)
            y_s.give(x, t)
        for k in range(12):
            if k < 11:
                for key, tail in (("gate", gate_tail), ("up", up_tail)):
                    job = yield from self.w.job((key, k))
                    b = yield from self.get(1)
                    for f in range(2):
                        mk = yield from self.form_a(job, 128 * f, 128, b.t[:, 256 * f:256 * f + 256], 256, 256, self.Hh, self.Hl,
                                                    self.hrd(1, 2), b.free)
                    self.w.free(job, mk)
                    self.spawn(tail(k, b, mk), 0.0)
            if k > 0:
                q = k - 1
                yield lambda: q in ft
                z, tf = ft[q]
                for hf in range(2):
                    job = yield from self.w.job(("down", q, hf))
                    yield lambda: known(job.ready)
                    for i in range(2):
                        yield [tf, job.ready]
                        a = acc[2 * i + hf]
                        for f in range(2):
                            fh, fl = FTh[:, z, f, 128 * i:128 * i + 128], FTl[:, z, f, 128 * i:128 * i + 128]
                            last = q == 10 and f == 1
                            self.mm(a.t[:, :], fh, job.hi(f), q == 0 and f == 0, False, tf, job.ready[f], a.free)
                            self.mm(a.t[:, :], fh, job.lo(f), False, False)
                            mk = self.mm(a.t[:, :], fl, job.hi(f), False, last, inc=True)
                        if q == 10:
                            xs = self.X[:, 2 + i, 512 * hf:512 * hf + 512]
                            t = self.tt(xs, xs, a.t[:, :], ALU.add, mk, self.xr[2 + i])
                            self.dma(self.sp, "out", self.out[self.o0 + i][:, 512 * hf:512 * hf + 512], xs, t)
                    self.w.free(job, mk)
                ft_s.give(z, mk)

    def main(self):
        begun = self.start()
        hr = self.new_h()
        nt = {s: [None, None] for s in (CT, LAT)}
        xn = self.F(9728, 2, D)
        for i in range(2):
            self.spawn(self.norm_tile(CT, i, xn, nt[CT], []), 0.0)
        self.spawn(self.make_h(hr, self.h_cols(0, CT), CT, xn, self.F(11776, 2, 2, 256), nt[CT]), 0.0)
        self.spawn(self.w.prepare(), 1.0)

        def own():
            for k in ada_own(0):
                yield from self.ada_step(*k)
            self.g_free = [(self.pe.name, self.pe.count)]
        self.own = self.spawn(own(), 3.0)
        for j in range(4):
            for part in range(2):
                yield from self.ada_step(0, part, j)
        f = self.fence = self.now()

        def turn():
            xn = self.F(4096, 2, D)
            for i in range(2):
                self.spawn(self.norm_tile(LAT, i, xn, nt[LAT], f), 0.0)
            yield from self.make_h(hr, self.h_cols(0, LAT), LAT, xn, self.F(12800, 2, 2, 256), nt[LAT], f)
            yield lambda: all(t.done for t in begun) and known(hr[CT])
        self.turn = self.spawn(turn(), 0.0)
        for l in range(min(self.upto, 3) + 1):
            streams = [CT, LAT] if l < 3 else [LAT]
            if l == 3 and self.upto > 3:
                self.vc = dict(norm_mix=0, norm_ffn=8, conv_w=16, conv_b=82)
                self.spawn(self.columns_2(), 0.0)
            yield from (self.layer_a, self.layer_b, self.layer_c, self.layer_a)[l](*((l, streams) if l % 3 == 0 else (l,)))
            yield lambda: self.ada_left == 0
            nxt = (lambda s, l=l: self.h_cols(l + 1, s)) if l < 3 and self.upto > l else None
            if l == 3 and self.upto > 3:
                nxt = lambda s: (lambda kt: self.VC[:, kt:kt + 1], lambda: [self.v2_rd])
            yield from self.finish_layer(l, streams, nxt)
            if nxt is None:
                yield lambda: self.turn.done
            self.fence = self.now()
            if l == 0:
                self.fence += [self.ext_rd]
        if self.upto > 3:
            yield from self.second()
        else:
            for t in range(4):
                self.dma(self.sp, "out", self.out[t], self.X[:, t, :], self.xr[t])

    def build(self):
        self.go(self.spawn(self.main(), 2.0))
        self.sp.wait(("dma_out", 64), self.ext_rd)

    def emit(self, ctx):
        nc = self.nc
        names = ["pe", "act", "dve", "pool", "sp"] + sorted(self.dma_count)
        sems = {n: ctx.enter_context(nc.semaphore("s_" + n)) for n in names}
        blk = ctx.enter_context(nc.Block())

        @blk.tensor
        def _(e):
            self.pe.play(e, sems)

        @blk.scalar
        def _(e):
            self.act.play(e, sems)

        @blk.vector
        def _(e):
            self.dve.play(e, sems)

        @blk.gpsimd
        def _(e):
            self.pool.play(e, sems)

        @blk.sync
        def _(e):
            self.sp.play(e, sems)


def packed(ins):
    a = {k: np.asarray(v) for k, v in ins.items()}
    r = lambda x: x.reshape(-1, 128)
    first = [r(a[f"l{l}_g_pre"]) for l in range(4)] + [r(a[n]) for n in ("l1_g_qa", "l1_g_kva", "l2_g_head", "l2_conv")]
    pad = [np.zeros((104 - sum(len(x) for x in first), 128), np.float32)]
    bias = [r(a[f"l{l}_b_ada"][0:2048]) for l in range(4)]
    gains = np.concatenate([a["qk_gain_2"][0]] * 2, axis=1)
    second = [r(a[n]) for n in ("norm_mix_2", "norm_ffn_2", "conv_w_2", "conv_b_2")] + [gains, r(a["cmp_pos_2"])]
    return {
        "weights": np.concatenate([j.pack(a) for j in plan()]),
        "cond": np.concatenate([r(a["c_ctx"]), r(a["c"])]),
        "vecs": np.concatenate(first + pad + bias),
        "vecs2": np.concatenate(second),
        "rows": np.concatenate([a["l0_sink"], a["l3_sink"], a["sinks_2"][0], a["forget_bias_2"][0]])[None],
        **{n: a[n] for n in ("x", "ctx", "l2_b_gate", "rel_bias_2", "cmp_w2_2")},
        **{f"l{l}_{n}": a[f"l{l}_{n}"] for l in range(4) for n in ("g_post", "b_ada")},
    }


def konst():
    f = np.float32
    K = np.zeros((128, 896), f)
    K[:, 0:128] = np.eye(128, dtype=f)
    for s in range(2):
        K[s::32, 128 + 128 * s:256 + 128 * s] = 1.0
    tok = np.arange(256)
    r, c = (tok // 64).astype(f), (tok % 64).astype(f)
    inv = (f(10000.0) ** (-np.arange(16, dtype=f) / f(16))).astype(f)
    ang = np.concatenate([r[:, None] * inv, c[:, None] * inv], axis=-1).astype(f)
    p = np.arange(128)
    a = ang[:, (p % 64) // 2].T
    K[:, 384:640] = np.cos(a)
    K[:, 640:896] = np.sin(a) * np.where(p % 2 == 0, -1.0, 1.0)[:, None]
    band = np.zeros((128, 2, 512), f)
    q = np.arange(128)
    for i in range(2):
        kk = np.arange(256)
        bad = np.abs(128 * i + q[:, None] - kk[None, :]) > 128
        band[:, i, 256:512] = np.where(bad, f(NEG), f(0))
    a = np.arange(128)
    ml = np.zeros((128, 2, 128), f)
    ml[:, 0] = np.where(a[:, None] <= a[None, :], f(0), f(NEG))
    ml[:, 1] = np.where(a[:, None] >= a[None, :], f(0), f(NEG))
    K2 = np.zeros((128, 577), f)
    K2[:, 0:128] = a[:, None] <= a[None, :]
    K2[:, 128:256] = 1.0
    for g in range(2):
        for n in range(15):
            K2[15 * g + n::32, 256 + 32 * g + n] = 1.0
            K2[30::32, 256 + 32 * g + n] = 1.0
    jj = np.arange(256)
    K2[:, 320:576] = np.where(128 + a[:, None] - jj[None, :] >= 0, f(0), f(NEG))
    K2[:, 576] = a >= 31
    m = np.arange(384)
    dist = 255 - m
    dd = np.maximum(dist, 0)
    ratio = np.log(np.maximum(dd, 1).astype(f) / f(16)) / f(np.log(8.0))
    large = np.minimum(16 + (ratio * f(16)).astype(np.int32), 31)
    bucket = np.where(dd < 16, dd, large)
    oh = np.zeros((34, 384), f)
    ok = dist >= 0
    oh[bucket[ok], m[ok]] = 1.0
    oh[32] = np.where(ok, f(0), f(NEG))
    oh[33] = np.where(dist >= 128, f(NEG), f(0))
    tr = np.zeros((2, 16), f)
    tr[0] = 1.0
    tr[1, 8:] = 1.0
    return {"konst2": K2, "onehot": oh, "tabrows": tr, "mlmask": ml.reshape(128, 256), "konst": K, "band": band.reshape(128, 1024)}


def ctx_stack_two_blocks_kernel(nc, ins, out):
    with ExitStack() as ctx:
        net = Net(nc, ctx, ins, out.rearrange("a (t p) d -> (a t) p d", p=128), 4)
        net.build()
        net.emit(ctx)


def kernel(**inputs):
    import numpy as _np
    import concourse.bacc as _bacc
    from concourse import mybir as _mybir
    from concourse.bass_utils import run_bass_kernel_spmd as _run

    nc = _bacc.Bacc("TRN2", target_bir_lowering=False, num_devices=1)
    arrays, args = {}, {}
    for name, a in {**packed(inputs), **konst()}.items():
        a = _np.ascontiguousarray(a)
        arrays[f"in_{name}_dram"] = a
        args[name] = nc.dram_tensor(f"in_{name}_dram", a.shape, _mybir.dt.from_np(a.dtype), kind="ExternalInput").ap()
    out = nc.dram_tensor("out_0_dram", (1, 256, 1024), _mybir.dt.float32, kind="ExternalOutput").ap()
    ctx_stack_two_blocks_kernel(nc, args, out)
    r = _run(nc, [arrays], core_ids=[0])
    return r.results[0]["out_0_dram"]
```
